# Optimizing a Trainium2 kernel written in Bass

```python
import math
import jax
import jax.numpy as jnp
from jax import lax
import numpy as np
import jax, jax.numpy as jnp

D_MODEL = 1024
BATCH = 1
SEQ = 256
DEPTH = 2

N_MIXERS = 2
N_SSD_LAYERS = (DEPTH + N_MIXERS - 1) // N_MIXERS
N_MLA_LAYERS = DEPTH // N_MIXERS
N_SUBLAYERS = 3

D_FF = 2816
FFN_RES_WEIGHT = 0.5
NORM_EPS = 1e-6

SSD_EXPAND = 2
D_INNER = SSD_EXPAND * D_MODEL
SSD_HEAD_DIM = 64
SSD_HEADS = D_INNER // SSD_HEAD_DIM
SSD_GROUPS = 8
SSD_HEADS_PER_GROUP = SSD_HEADS // SSD_GROUPS
SSD_STATE = 128
SSD_CONV = 5
SSD_CHUNK = 128
SSD_CONV_CH = D_INNER + 2 * SSD_GROUPS * SSD_STATE
SSD_IN = D_INNER + SSD_CONV_CH + 2 * SSD_HEADS
SSD_NORM_GROUP = D_INNER // SSD_GROUPS

MLA_HEADS = 16
MLA_Q_LORA = 384
MLA_KV_LORA = 256
MLA_NOPE = 64
MLA_ROPE = 32
MLA_V = 64
MLA_QK = MLA_NOPE + MLA_ROPE
MLA_IN = MLA_Q_LORA + MLA_KV_LORA + MLA_ROPE
ROPE_THETA = 10000.0
ATTN_Q_BLOCK = 128
MAX_POS_OFFSET = 1024


def rms_norm(x, g):
    xf = x.astype(jnp.float32)
    y = xf * lax.rsqrt(jnp.mean(xf * xf, axis=-1, keepdims=True) + NORM_EPS)
    return (y * g.astype(jnp.float32)).astype(x.dtype)

def modulate(x, g, shift, scale):
    return rms_norm(x, g) * (1.0 + scale[:, None, :]) + shift[:, None, :]

def swiglu(h, w_gate, w_up, w_down):
    return (jax.nn.silu(h @ w_gate) * (h @ w_up)) @ w_down

def depthwise_conv_centred(x, w, bias):
    ch = x.shape[-1]
    pad = SSD_CONV // 2
    out = lax.conv_general_dilated(
        x, w[:, None, :], window_strides=(1,), padding=[(pad, pad)],
        dimension_numbers=("NWC", "WIO", "NWC"), feature_group_count=ch)
    return out + bias

def ssd_chunked(x, dt, A, Bm, Cm):
    b, s, g, r, p = x.shape
    n = Bm.shape[-1]
    nc = s // SSD_CHUNK
    q = SSD_CHUNK
    x = x.reshape(b, nc, q, g, r, p)
    dt = dt.reshape(b, nc, q, g, r)
    Bm = Bm.reshape(b, nc, q, g, n)
    Cm = Cm.reshape(b, nc, q, g, n)
    a_cum = jnp.cumsum(dt * A, axis=2)
    xdt = x * dt[..., None]

    seg = a_cum[:, :, :, None] - a_cum[:, :, None, :]
    mask = jnp.tril(jnp.ones((q, q), dtype=bool))[:, :, None, None]
    decay = jnp.exp(jnp.where(mask, seg, -jnp.inf))
    cb = jnp.einsum("bcign,bcjgn->bcijg", Cm, Bm)
    y_diag = jnp.einsum("bcijgr,bcjgrp->bcigrp", cb[..., None] * decay, xdt)

    decay_to_end = jnp.exp(a_cum[:, :, -1:] - a_cum)
    states = jnp.einsum("bcjgn,bcjgrp->bcgrpn", Bm, xdt * decay_to_end[..., None])
    chunk_decay = jnp.exp(a_cum[:, :, -1])

    def step(h, inp):
        st, dec = inp
        return h * dec[..., None, None] + st, h

    h0 = jnp.zeros((b, g, r, p, n), dtype=states.dtype)
    _, h_prev = lax.scan(step, h0, (jnp.moveaxis(states, 1, 0), jnp.moveaxis(chunk_decay, 1, 0)))
    h_prev = jnp.moveaxis(h_prev, 0, 1)

    y_off = jnp.einsum("bcign,bcgrpn->bcigrp", Cm, h_prev) * jnp.exp(a_cum)[..., None]
    return (y_diag + y_off).reshape(b, s, g, r, p)

def ssd_mixer(h, w_in, conv_w, conv_b, dt_bias, a_log, d_skip, norm_g, w_out):
    b, s, _ = h.shape
    g, r = SSD_GROUPS, SSD_HEADS_PER_GROUP
    proj = h @ w_in
    z, xbc, dt_raw = jnp.split(proj, [D_INNER, D_INNER + SSD_CONV_CH], axis=-1)
    xbc = jax.nn.silu(depthwise_conv_centred(xbc, conv_w, conv_b))
    xs, Bm, Cm = jnp.split(xbc, [D_INNER, D_INNER + SSD_GROUPS * SSD_STATE], axis=-1)
    xs = xs.reshape(b, s, g, r, SSD_HEAD_DIM)
    Bm = Bm.reshape(b, s, g, SSD_STATE)
    Cm = Cm.reshape(b, s, g, SSD_STATE)
    dt = jax.nn.softplus(dt_raw.reshape(b, s, 2, g, r) + dt_bias.reshape(2, g, r))
    A = -jnp.exp(a_log).reshape(2, g, r)

    flip = lambda t: jnp.flip(t, axis=1)
    y_fwd = ssd_chunked(xs, dt[:, :, 0], A[0], Bm, Cm)
    y_bwd = flip(ssd_chunked(flip(xs), flip(dt[:, :, 1]), A[1], flip(Bm), flip(Cm)))
    y = y_fwd + y_bwd + xs * d_skip.reshape(g, r)[..., None]

    y = y.reshape(b, s, D_INNER) * jax.nn.silu(z)
    y = rms_norm(y.reshape(b, s, g, SSD_NORM_GROUP), norm_g.reshape(g, SSD_NORM_GROUP))
    return y.reshape(b, s, D_INNER) @ w_out

def rope_tables(positions):
    inv_freq = ROPE_THETA ** (-jnp.arange(0, MLA_ROPE, 2, dtype=jnp.float32) / MLA_ROPE)
    ang = positions.astype(jnp.float32)[..., None] * inv_freq
    return jnp.cos(ang)[:, :, None, :], jnp.sin(ang)[:, :, None, :]

def apply_rope_tail(t, cos, sin):
    t_nope, t_pe = t[..., :MLA_NOPE], t[..., MLA_NOPE:]
    x1, x2 = jnp.split(t_pe.astype(jnp.float32), 2, axis=-1)
    rot = jnp.concatenate([x1 * cos - x2 * sin, x2 * cos + x1 * sin], axis=-1).astype(t.dtype)
    return jnp.concatenate([t_nope, rot], axis=-1)

def blocked_attention(q, k, v):
    b, s, h, dq = q.shape
    nq = s // ATTN_Q_BLOCK
    scale = dq ** -0.5
    qb = jnp.moveaxis(q.reshape(b, nq, ATTN_Q_BLOCK, h, dq), 1, 0)

    def one_block(q_blk):
        logits = jnp.einsum("bqhd,bkhd->bhqk", q_blk, k).astype(jnp.float32) * scale
        p = jax.nn.softmax(logits, axis=-1).astype(v.dtype)
        return jnp.einsum("bhqk,bkhv->bqhv", p, v)

    o = lax.map(one_block, qb)
    return jnp.moveaxis(o, 0, 1).reshape(b, s, h, v.shape[-1])

def mla_mixer(h, positions, w_in, q_norm_g, kv_norm_g, w_uq, w_ukv, q_head_g, k_head_g, w_out):
    b, s, _ = h.shape
    q_lat, kv_lat, k_pe = jnp.split(h @ w_in, [MLA_Q_LORA, MLA_Q_LORA + MLA_KV_LORA], axis=-1)
    q = (rms_norm(q_lat, q_norm_g) @ w_uq).reshape(b, s, MLA_HEADS, MLA_QK)
    kv = (rms_norm(kv_lat, kv_norm_g) @ w_ukv).reshape(b, s, MLA_HEADS, MLA_NOPE + MLA_V)
    k_nope, v = jnp.split(kv, [MLA_NOPE], axis=-1)
    k_pe = jnp.broadcast_to(k_pe[:, :, None, :], (b, s, MLA_HEADS, MLA_ROPE))
    k = jnp.concatenate([k_nope, k_pe], axis=-1)
    q = rms_norm(q, q_head_g)
    k = rms_norm(k, k_head_g)
    cos, sin = rope_tables(positions)
    q = apply_rope_tail(q, cos, sin)
    k = apply_rope_tail(k, cos, sin)
    o = blocked_attention(q, k, v)
    return o.reshape(b, s, MLA_HEADS * MLA_V) @ w_out

def first_inputs(seed: int = 0) -> dict:
    key = jax.random.key(seed)
    ks = iter(jax.random.split(key, 40))

    def normal(shape, scale):
        return scale * jax.random.normal(next(ks), shape, jnp.float32)

    def gain(shape):
        return 1.0 + 0.05 * jax.random.normal(next(ks), shape, jnp.float32)

    na, nb = N_SSD_LAYERS, N_MLA_LAYERS
    x = normal((BATCH, SEQ, D_MODEL), 1.0)
    c = normal((BATCH, D_MODEL), 1.0)
    positions = (jax.random.randint(next(ks), (BATCH, 1), 0, MAX_POS_OFFSET, dtype=jnp.int32)
                 + jnp.arange(SEQ, dtype=jnp.int32)[None, :])
    norm_g = gain((DEPTH, N_SUBLAYERS, D_MODEL))
    w_mod = normal((DEPTH, D_MODEL, N_SUBLAYERS * 3 * D_MODEL), D_MODEL ** -0.5)
    b_mod = normal((DEPTH, N_SUBLAYERS * 3 * D_MODEL), 0.02)
    ffn_w_gate = normal((DEPTH, 2, D_MODEL, D_FF), D_MODEL ** -0.5)
    ffn_w_up = normal((DEPTH, 2, D_MODEL, D_FF), D_MODEL ** -0.5)
    ffn_w_down = normal((DEPTH, 2, D_FF, D_MODEL), D_FF ** -0.5)

    ssd_w_in = normal((na, D_MODEL, SSD_IN), D_MODEL ** -0.5)
    ssd_conv_w = normal((na, SSD_CONV, SSD_CONV_CH), SSD_CONV ** -0.5)
    ssd_conv_b = normal((na, SSD_CONV_CH), 0.02)
    dt0 = jnp.exp(jax.random.uniform(next(ks), (na, 2, SSD_HEADS), jnp.float32,
                                     math.log(1e-3), math.log(1e-1)))
    ssd_dt_bias = dt0 + jnp.log(-jnp.expm1(-dt0))
    ssd_a_log = jnp.log(jax.random.uniform(next(ks), (na, 2, SSD_HEADS), jnp.float32, 1.0, 16.0))
    ssd_d = gain((na, SSD_HEADS))
    ssd_norm_g = gain((na, D_INNER))
    ssd_w_out = normal((na, D_INNER, D_MODEL), D_INNER ** -0.5)

    mla_w_in = normal((nb, D_MODEL, MLA_IN), D_MODEL ** -0.5)
    mla_q_norm_g = gain((nb, MLA_Q_LORA))
    mla_kv_norm_g = gain((nb, MLA_KV_LORA))
    mla_w_uq = normal((nb, MLA_Q_LORA, MLA_HEADS * MLA_QK), MLA_Q_LORA ** -0.5)
    mla_w_ukv = normal((nb, MLA_KV_LORA, MLA_HEADS * (MLA_NOPE + MLA_V)), MLA_KV_LORA ** -0.5)
    mla_q_head_g = gain((nb, MLA_QK))
    mla_k_head_g = gain((nb, MLA_QK))
    mla_w_out = normal((nb, MLA_HEADS * MLA_V, D_MODEL), (MLA_HEADS * MLA_V) ** -0.5)

    return {
        "x": x, "c": c, "positions": positions,
        "norm_g": norm_g, "w_mod": w_mod, "b_mod": b_mod,
        "ffn_w_gate": ffn_w_gate, "ffn_w_up": ffn_w_up, "ffn_w_down": ffn_w_down,
        "ssd_w_in": ssd_w_in, "ssd_conv_w": ssd_conv_w, "ssd_conv_b": ssd_conv_b,
        "ssd_dt_bias": ssd_dt_bias, "ssd_a_log": ssd_a_log, "ssd_d": ssd_d,
        "ssd_norm_g": ssd_norm_g, "ssd_w_out": ssd_w_out,
        "mla_w_in": mla_w_in, "mla_q_norm_g": mla_q_norm_g, "mla_kv_norm_g": mla_kv_norm_g,
        "mla_w_uq": mla_w_uq, "mla_w_ukv": mla_w_ukv, "mla_q_head_g": mla_q_head_g,
        "mla_k_head_g": mla_k_head_g, "mla_w_out": mla_w_out,
    }

def first_block(x, c, positions, norm_g, w_mod, b_mod, ffn_w_gate, ffn_w_up, ffn_w_down,
              ssd_w_in, ssd_conv_w, ssd_conv_b, ssd_dt_bias, ssd_a_log, ssd_d,
              ssd_norm_g, ssd_w_out,
              mla_w_in, mla_q_norm_g, mla_kv_norm_g, mla_w_uq, mla_w_ukv,
              mla_q_head_g, mla_k_head_g, mla_w_out):
    cond = jax.nn.silu(c)
    for i in range(DEPTH):
        mod = (cond @ w_mod[i] + b_mod[i]).reshape(-1, N_SUBLAYERS, 3, D_MODEL)

        h = modulate(x, norm_g[i, 0], mod[:, 0, 0], mod[:, 0, 1])
        x = x + FFN_RES_WEIGHT * mod[:, 0, 2][:, None, :] * swiglu(
            h, ffn_w_gate[i, 0], ffn_w_up[i, 0], ffn_w_down[i, 0])

        h = modulate(x, norm_g[i, 1], mod[:, 1, 0], mod[:, 1, 1])
        j = i // N_MIXERS
        if i % N_MIXERS == 0:
            y = ssd_mixer(h, ssd_w_in[j], ssd_conv_w[j], ssd_conv_b[j], ssd_dt_bias[j],
                          ssd_a_log[j], ssd_d[j], ssd_norm_g[j], ssd_w_out[j])
        else:
            y = mla_mixer(h, positions, mla_w_in[j], mla_q_norm_g[j], mla_kv_norm_g[j],
                          mla_w_uq[j], mla_w_ukv[j], mla_q_head_g[j], mla_k_head_g[j],
                          mla_w_out[j])
        x = x + mod[:, 1, 2][:, None, :] * y

        h = modulate(x, norm_g[i, 2], mod[:, 2, 0], mod[:, 2, 1])
        x = x + FFN_RES_WEIGHT * mod[:, 2, 2][:, None, :] * swiglu(
            h, ffn_w_gate[i, 1], ffn_w_up[i, 1], ffn_w_down[i, 1])
    return x


MIX_WIDTH = D_MODEL
RWKV_WIDTH = MIX_WIDTH // 2
HEAD_SIZE = 64
RWKV_HEADS = RWKV_WIDTH // HEAD_SIZE
DECAY_LORA = 64
AAA_LORA = 64
MV_LORA = 32
GATE_LORA = 128
RWKV_COLS = 3 * RWKV_WIDTH + DECAY_LORA + AAA_LORA + GATE_LORA
POOL_WIDTH = MIX_WIDTH - RWKV_WIDTH
POOL_WINDOWS = (2, 4, 8, 16)
POOL_GROUP = POOL_WIDTH // len(POOL_WINDOWS)
IN_COLS = RWKV_COLS + POOL_WIDTH
GN_EPS = 64e-5
N_KEYS = 128
N_EXPERTS = N_KEYS * N_KEYS
PEER_HEADS = 8
PEER_QDIM = 256
PEER_HALF = PEER_QDIM // 2
PEER_TOPK = 16
TOK_BLOCK = 128


def rmsnorm(x, g):
    x32 = x.astype(jnp.float32)
    y = x32 * lax.rsqrt(jnp.mean(x32 * x32, axis=-1, keepdims=True) + NORM_EPS)
    return (y * g.astype(jnp.float32)).astype(x.dtype)

def modulate_2(h, shift, scale):
    return h * (1 + scale[:, None, :]) + shift[:, None, :]

def token_shift(z, mu):
    prev = jnp.pad(z, ((0, 0), (1, 0), (0, 0)))[:, :-1]
    return z + (prev - z) * mu

def rwkv7_step(state, inp):
    r_t, w_t, k_t, v_t, kk_t, a_t = inp
    sa = jnp.einsum('bhvk,bhk->bhv', state, -kk_t)
    state = (state * w_t[:, :, None, :]
             + sa[..., None] * (kk_t * a_t)[:, :, None, :]
             + v_t[..., None] * k_t[:, :, None, :])
    y = jnp.einsum('bhvk,bhk->bhv', state, r_t)
    return state, y

def rwkv7_mix(r, k, v, wd, ad, gd, w0, w_up, a0, a_up, g_up, k_k, k_a, r_k, lnx_g, lnx_b):
    B, S, _ = r.shape
    f32 = jnp.float32
    w = -jax.nn.softplus(-(w0 + jnp.tanh(wd) @ w_up)) - 0.5
    decay = jnp.exp(-jnp.exp(w.astype(f32)))
    a = jax.nn.sigmoid(a0 + ad @ a_up)
    g = jax.nn.sigmoid(gd) @ g_up

    def heads(t):
        return t.reshape(B, S, RWKV_HEADS, HEAD_SIZE).astype(f32)

    kk = heads(k * k_k)
    kk = kk / jnp.maximum(jnp.sqrt(jnp.sum(kk * kk, axis=-1, keepdims=True)), 1e-12)
    k = k * (1 + (a - 1) * k_a)
    rh, kh, vh, ah, wh = heads(r), heads(k), heads(v), heads(a), heads(decay)
    tm = lambda t: jnp.moveaxis(t, 1, 0)
    s0 = jnp.zeros((B, RWKV_HEADS, HEAD_SIZE, HEAD_SIZE), f32)
    _, ys = lax.scan(rwkv7_step, s0, (tm(rh), tm(wh), tm(kh), tm(vh), tm(kk), tm(ah)))
    y = jnp.moveaxis(ys, 0, 1)
    mean = jnp.mean(y, axis=-1, keepdims=True)
    var = jnp.mean(jnp.square(y - mean), axis=-1, keepdims=True)
    yn = ((y - mean) * lax.rsqrt(var + GN_EPS)).reshape(B, S, RWKV_WIDTH)
    yn = yn * lnx_g.astype(f32) + lnx_b.astype(f32)
    bonus = jnp.sum(rh * kh * r_k.astype(f32), axis=-1, keepdims=True) * vh
    out = (yn + bonus.reshape(B, S, RWKV_WIDTH)) * g.astype(f32)
    return out.astype(r.dtype)

def multiscale_pool(p, pool_w, pool_scale):
    B, S, _ = p.shape
    f32 = jnp.float32
    p32 = p.astype(f32)
    cs = jnp.cumsum(p32, axis=1)
    pos = jnp.arange(1, S + 1, dtype=f32)
    groups = []
    for j, win in enumerate(POOL_WINDOWS):
        sl = slice(j * POOL_GROUP, (j + 1) * POOL_GROUP)
        csj = cs[..., sl]
        lag = jnp.pad(csj, ((0, 0), (win, 0), (0, 0)))[:, :S]
        mean = (csj - lag) / jnp.minimum(pos, float(win))[None, :, None]
        groups.append(mean - p32[..., sl])
    d = jnp.stack(groups, axis=2)
    out = jnp.einsum('bsgc,gcd->bsgd', d, pool_w.astype(f32)).reshape(B, S, POOL_WIDTH)
    return (out * pool_scale.astype(f32)).astype(p.dtype)

def peer_ffn(h, peer_q, peer_keys, peer_u, peer_v):
    B, S, D = h.shape
    q = (h @ peer_q).reshape(B, S, PEER_HEADS, 2, PEER_HALF)
    scores = jnp.einsum('bshpd,hpkd->bshpk', q, peer_keys)
    s, i = lax.top_k(scores, PEER_TOPK)
    cand_s = (s[..., 0, :, None] + s[..., 1, None, :]).reshape(B, S, PEER_HEADS, PEER_TOPK * PEER_TOPK)
    cand_i = (i[..., 0, :, None] * N_KEYS + i[..., 1, None, :]).reshape(B, S, PEER_HEADS, PEER_TOPK * PEER_TOPK)
    top_s, sel = lax.top_k(cand_s, PEER_TOPK)
    idx = jnp.take_along_axis(cand_i, sel, axis=-1)
    gate = jax.nn.softmax(top_s.astype(jnp.float32), axis=-1)
    T = B * S
    E = PEER_HEADS * PEER_TOPK
    nb = T // TOK_BLOCK
    hb = h.reshape(nb, TOK_BLOCK, D)
    ib = idx.reshape(nb, TOK_BLOCK, E)
    gb = gate.astype(h.dtype).reshape(nb, TOK_BLOCK, E)

    def block(args):
        hx, ix, gx = args
        u_sel = jnp.take(peer_u, ix, axis=0)
        v_sel = jnp.take(peer_v, ix, axis=0)
        act = jax.nn.gelu(jnp.einsum('td,ted->te', hx, u_sel), approximate=False)
        return jnp.einsum('te,ted->td', gx * act, v_sel)

    out = lax.map(block, (hb, ib, gb))
    return out.reshape(B, S, D)

def second_inputs(seed: int = 0) -> dict:
    key = jax.random.key(seed)
    ks = jax.random.split(key, 32)
    nrm = lambda k, shape, s: jax.random.normal(k, shape, jnp.float32) * s
    L, Lr = DEPTH, DEPTH - 1
    return {
        "x": nrm(ks[0], (BATCH, SEQ, D_MODEL), 1.0),
        "c": nrm(ks[1], (BATCH, D_MODEL), 1.0),
        "ada_w": nrm(ks[2], (L, D_MODEL, 6 * D_MODEL), 0.5 * D_MODEL ** -0.5),
        "ada_b": nrm(ks[3], (L, 6 * D_MODEL), 0.01),
        "ln1_g": 1.0 + nrm(ks[4], (L, D_MODEL), 0.01),
        "w_in": nrm(ks[5], (L, D_MODEL, IN_COLS), D_MODEL ** -0.5),
        "mu_shift": jax.random.uniform(ks[6], (L, RWKV_COLS), jnp.float32),
        "w0": nrm(ks[7], (L, RWKV_WIDTH), 0.5),
        "w_up": nrm(ks[8], (L, DECAY_LORA, RWKV_WIDTH), 0.1 * DECAY_LORA ** -0.5),
        "a0": nrm(ks[9], (L, RWKV_WIDTH), 0.1),
        "a_up": nrm(ks[10], (L, AAA_LORA, RWKV_WIDTH), 0.1 * AAA_LORA ** -0.5),
        "g_up": nrm(ks[11], (L, GATE_LORA, RWKV_WIDTH), GATE_LORA ** -0.5),
        "vres_down": nrm(ks[12], (Lr, D_MODEL, MV_LORA), D_MODEL ** -0.5),
        "vres_mu": jax.random.uniform(ks[13], (Lr, MV_LORA), jnp.float32),
        "vres_v0": 1.0 + nrm(ks[14], (Lr, RWKV_WIDTH), 0.1),
        "vres_up": nrm(ks[15], (Lr, MV_LORA, RWKV_WIDTH), 0.1 * MV_LORA ** -0.5),
        "k_k": 0.85 + nrm(ks[16], (L, RWKV_WIDTH), 0.02),
        "k_a": 1.0 + nrm(ks[17], (L, RWKV_WIDTH), 0.02),
        "r_k": -0.04 + nrm(ks[18], (L, RWKV_HEADS, HEAD_SIZE), 0.02),
        "lnx_g": 1.0 + nrm(ks[19], (L, RWKV_WIDTH), 0.01),
        "lnx_b": nrm(ks[20], (L, RWKV_WIDTH), 0.01),
        "pool_w": nrm(ks[21], (L, len(POOL_WINDOWS), POOL_GROUP, POOL_GROUP), POOL_GROUP ** -0.5),
        "pool_scale": 1.0 + nrm(ks[22], (L, POOL_WIDTH), 0.01),
        "w_out": nrm(ks[23], (L, MIX_WIDTH, D_MODEL), MIX_WIDTH ** -0.5),
        "ln2_g": 1.0 + nrm(ks[24], (L, D_MODEL), 0.01),
        "peer_q": nrm(ks[25], (L, D_MODEL, PEER_HEADS * PEER_QDIM), D_MODEL ** -0.5),
        "peer_keys": nrm(ks[26], (L, PEER_HEADS, 2, N_KEYS, PEER_HALF), PEER_HALF ** -0.5),
        "peer_u": nrm(ks[27], (L, N_EXPERTS, D_MODEL), D_MODEL ** -0.5),
        "peer_v": nrm(ks[28], (L, N_EXPERTS, D_MODEL), PEER_HEADS ** -0.5),
        "lnf_g": 1.0 + nrm(ks[29], (D_MODEL,), 0.01),
    }

def second_block(x, c, ada_w, ada_b, ln1_g, w_in, mu_shift, w0, w_up, a0, a_up, g_up,
              vres_down, vres_mu, vres_v0, vres_up, k_k, k_a, r_k, lnx_g, lnx_b,
              pool_w, pool_scale, w_out, ln2_g, peer_q, peer_keys, peer_u, peer_v, lnf_g):
    split_pts = [RWKV_WIDTH, 2 * RWKV_WIDTH, 3 * RWKV_WIDTH,
                 3 * RWKV_WIDTH + DECAY_LORA, 3 * RWKV_WIDTH + DECAY_LORA + AAA_LORA]
    c_act = jax.nn.silu(c)
    v_first = None
    for l in range(DEPTH):
        mod = c_act @ ada_w[l] + ada_b[l]
        sh1, sc1, g1, sh2, sc2, g2 = jnp.split(mod, 6, axis=-1)

        h = modulate_2(rmsnorm(x, ln1_g[l]), sh1, sc1)
        w_full = w_in[l] if l == 0 else jnp.concatenate([w_in[l], vres_down[l - 1]], axis=1)
        proj = h @ w_full
        rw = token_shift(proj[..., :RWKV_COLS], mu_shift[l])
        r, k, v, wd, ad, gd = jnp.split(rw, split_pts, axis=-1)
        pool_in = proj[..., RWKV_COLS:RWKV_COLS + POOL_WIDTH]
        if l == 0:
            v_first = v
        else:
            vd = token_shift(proj[..., RWKV_COLS + POOL_WIDTH:], vres_mu[l - 1])
            v = v + (v_first - v) * jax.nn.sigmoid(vres_v0[l - 1] + vd @ vres_up[l - 1])
        y_rwkv = rwkv7_mix(r, k, v, wd, ad, gd, w0[l], w_up[l], a0[l], a_up[l], g_up[l],
                           k_k[l], k_a[l], r_k[l], lnx_g[l], lnx_b[l])
        y_pool = multiscale_pool(pool_in, pool_w[l], pool_scale[l])
        mix = jnp.concatenate([y_rwkv, y_pool], axis=-1) @ w_out[l]
        x = x + g1[:, None, :] * mix

        h2 = modulate_2(rmsnorm(x, ln2_g[l]), sh2, sc2)
        x = x + g2[:, None, :] * peer_ffn(h2, peer_q[l], peer_keys[l], peer_u[l], peer_v[l])
    return rmsnorm(x, lnf_g)


def setup_inputs(seed=0):
    out = dict(first_inputs(seed))
    for name, value in second_inputs(seed + 1).items():
        if name != "x":
            out[name + "_2"] = value
    return out


def reference(
    x, c, positions, norm_g, w_mod, b_mod, ffn_w_gate, ffn_w_up, ffn_w_down, ssd_w_in,
    ssd_conv_w, ssd_conv_b, ssd_dt_bias, ssd_a_log, ssd_d, ssd_norm_g, ssd_w_out, mla_w_in,
    mla_q_norm_g, mla_kv_norm_g, mla_w_uq, mla_w_ukv, mla_q_head_g, mla_k_head_g, mla_w_out,
    c_2, ada_w_2, ada_b_2, ln1_g_2, w_in_2, mu_shift_2, w0_2, w_up_2, a0_2, a_up_2, g_up_2,
    vres_down_2, vres_mu_2, vres_v0_2, vres_up_2, k_k_2, k_a_2, r_k_2, lnx_g_2, lnx_b_2,
    pool_w_2, pool_scale_2, w_out_2, ln2_g_2, peer_q_2, peer_keys_2, peer_u_2, peer_v_2,
    lnf_g_2,
):
    x = first_block(
        x, c, positions, norm_g, w_mod, b_mod, ffn_w_gate, ffn_w_up, ffn_w_down, ssd_w_in,
        ssd_conv_w, ssd_conv_b, ssd_dt_bias, ssd_a_log, ssd_d, ssd_norm_g, ssd_w_out, mla_w_in,
        mla_q_norm_g, mla_kv_norm_g, mla_w_uq, mla_w_ukv, mla_q_head_g, mla_k_head_g, mla_w_out,
    )
    return second_block(
        x, c_2, ada_w_2, ada_b_2, ln1_g_2, w_in_2, mu_shift_2, w0_2, w_up_2, a0_2, a_up_2,
        g_up_2, vres_down_2, vres_mu_2, vres_v0_2, vres_up_2, k_k_2, k_a_2, r_k_2, lnx_g_2,
        lnx_b_2, pool_w_2, pool_scale_2, w_out_2, ln2_g_2, peer_q_2, peer_keys_2, peer_u_2,
        peer_v_2, lnf_g_2,
    )


_drawn_inputs = setup_inputs


def setup_inputs(seed=0):
    import zlib

    import numpy as np

    out = dict(_drawn_inputs(seed))
    spreads = {}
    factors = {'ssd_conv_b': 4.225,
     'ssd_d': 7.223,
     'mla_q_norm_g': 8.0,
     'mla_kv_norm_g': 4.238,
     'mla_q_head_g': 8.0,
     'mla_k_head_g': 8.0,
     'ada_b_2': 5.023,
     'ln1_g_2': 8.0,
     'w_up_2': 64.0,
     'a0_2': 6.565,
     'a_up_2': 7.354,
     'vres_down_2': 8.0,
     'vres_mu_2': 8.0,
     'vres_v0_2': 34.729,
     'vres_up_2': 8.0,
     'k_k_2': 64.0,
     'k_a_2': 8.0,
     'r_k_2': 7.165,
     'lnx_g_2': 64.0,
     'lnx_b_2': 64.0,
     'pool_scale_2': 64.0,
     'ln2_g_2': 64.0,
     'lnf_g_2': 31.035,
     'w0_2': 8.0,
     'peer_q_2': 4.028,
     'peer_keys_2': 4.54,
     'peer_u_2': 4.454,
     'peer_v_2': 3.638}
    for name, (base, spread) in spreads.items():
        noise = np.random.default_rng([zlib.crc32(name.encode()), seed]).standard_normal(out[name].shape)
        drawn = base * np.exp(spread * noise) if base else spread * noise
        out[name] = jnp.asarray(drawn.astype(out[name].dtype))
    for name, factor in factors.items():
        out[name] = (out[name] * factor).astype(out[name].dtype)
    return out
```

```python
from contextlib import ExitStack

import numpy as np

import concourse.bass as bass
from concourse import mybir

F32 = mybir.dt.float32
BF16 = mybir.dt.bfloat16
I32 = mybir.dt.int32
U32 = mybir.dt.uint32
ALU = mybir.AluOpType
ACT = mybir.ActivationFunctionType
AX = mybir.AxisListType

P = 128
D = 1024
T = 256
DT = D // P
TT = T // P
FF = 2816
FT = FF // P
EPS = 1e-6

SSD_HEADS, SSD_GROUPS, DIN = 32, 8, 2048
ZT, XBCT = DIN // P, 4096 // P
CONV = 5

MH, NOPE, ROPE, QK, MV = 16, 64, 32, 96, 64
QL, KVL = 384, 256

RW, HS = 512, 64
RH = RW // HS
CH = 16
NCH = T // CH
GN_EPS = 64e-5

PH, NK, TOPK = 8, 128, 16
NSUB = 10

RING = 8
NEG = -1e30


def stream_plan():
    base, n = {}, 0

    def add(name, count):
        nonlocal n
        base[name] = n
        n += count

    for i in range(2):
        add(("mod", 3 * i), 24)
        add(("ffn", 2 * i), 3 * FT)
        add(("mod", 3 * i + 1), 24)
        if i == 0:
            add("ssd_in", ZT + XBCT + 1)
            add("ssd_out", 2 * DT)
        else:
            add("mla_in", 6)
            add("mla_out", DT)
        add(("mod", 3 * i + 2), 24)
        add(("ffn", 2 * i + 1), 3 * FT)
    for l in range(2):
        add(("mod", 6 + 2 * l), 24)
        add(("mix_in", l), 18 + l)
        add(("mix_out", l), DT)
        add(("mod", 7 + 2 * l), 24)
        add(("peer_q", l), 2 * PH)
        add(("uv", l), 2 * NK)
    return base, n


BASE, NBLOCKS = stream_plan()

COLS = {}


def _cols():
    n = 0
    for name, k in [
        ("c", 8), ("c_2", 8), ("norm_g", 48), ("b_mod", 144), ("ada_b", 96), ("ln1", 16), ("ln2", 16), ("lnf", 8),
        ("dt_bias", 1), ("a_log", 1), ("conv_w", XBCT * CONV), ("conv_b", XBCT), ("ssd_d", ZT), ("ssd_g", ZT),
        ("q_norm", 3), ("kv_norm", 2), ("q_head", 1), ("k_head", 1),
        ("mu", 28), ("w0", 8), ("a0", 8), ("k_k", 8), ("k_a", 8), ("r_k", 8), ("lnx_g", 8), ("lnx_b", 8),
        ("pool_scale", 8), ("vres_mu", 1), ("vres_v0", 4), ("freq", 1), ("even", 1), ("odd", 1),
    ]:
        COLS[name] = n
        n += k
    return n


NCOLS = _cols()

CONSTS = {}


def _consts():
    n = 0
    for name, k in [("ident", P), ("ones", P), ("iota", P), ("half", P), ("mask4", 4 * P), ("maskn", 2 * P),
                    ("restart", T), ("recip", 4 * T), ("rope", QK), ("causal", 2 * P)]:
        CONSTS[name] = (n, k)
        n += k
    return n


NCONST = _consts()
KEPT = 4 * P

SIGNALS = (
    "block_used", "loads", "aux_loads", "inits", "cond_ready", "mod_cols",
    "norm_sq", "norm_sum", "norm_var", "ssd_var", "mla_latvar", "mla_var", "rw_kkvar", "rw_gnvar", "norm_sqrt", "norm_scaled", "h_ready", "x_upd",
    "ffn_silu", "ffn_a", "proj_evac", "act_chain", "dve_chain", "pool_chain", "out_done", "out_ready",
    "conv_step", "conv_silu", "ssd_pads", "ssd_abs", "ssd_w", "ssd_ln", "ssd_dt", "ssd_tr", "ssd_xtok", "ssd_cb", "ssd_cb_sb", "ssd_seg",
    "ssd_exp", "ssd_m", "ssd_y", "ssd_yev", "ssd_yz", "ssd_ysq", "ssd_ysum", "ssd_ysqrt", "ssd_yn",
    "mla_w", "mla_latsq", "mla_latsum", "mla_latsqrt", "mla_lat", "mla_proj", "mla_pev", "mla_kpe", "mla_sq",
    "mla_sum", "mla_sqrt", "mla_qkn", "mla_rot", "mla_rope", "mla_angr", "mla_ang", "mla_logit", "mla_max", "mla_exp",
    "mla_prob", "mla_pt", "mla_pts", "mla_o", "mla_oev",
    "rw_w", "rw_shift", "rw_lo", "rw_lora", "rw_gates", "rw_vres", "rw_vresa", "rw_kksq", "rw_kksum", "rw_kksqrt",
    "rw_ld", "rw_exps", "rw_feat", "rw_zeroed", "rw_tr", "rw_trev", "rw_mat", "rw_matev", "rw_neu", "rw_neuev",
    "rw_x", "rw_xev", "rw_pq", "rw_pqev", "rw_gh", "rw_ghev", "rw_zy", "rw_zyev", "rw_step", "rw_state",
    "rw_y", "rw_yall", "rw_mean", "rw_cent", "rw_zpad", "rw_var", "rw_sd", "rw_bonus", "rw_bon", "rw_mix", "rw_pool", "rw_pl",
    "pe_keys", "pe_q", "pe_sc", "pe_scev", "pe_top", "pe_exp", "pe_sm", "pe_tr", "pe_ijg",
    "pe_oh", "pe_w", "pe_wev", "pe_gelu", "pe_gated", "pe_acc",
)


def build(nc, stream, cols_d, consts_d, x_d, pos_d, wuq_d, wukv_d, keys_d, pool_d, lora_d, gup_d, vup_d, out_d):
    with ExitStack() as ctx:
        def sb(name, shape, dt=F32):
            return ctx.enter_context(nc.sbuf_tensor(name, shape, dt))

        sem = {n: ctx.enter_context(nc.semaphore(n)) for n in SIGNALS}
        slot_full = [ctx.enter_context(nc.semaphore(f"slot_full_{i}")) for i in range(RING)]

        ring = sb("ring", [P, RING, 1024])
        AR = sb("arena", [P, 128, 256])
        x = sb("x", [P, DT, T])
        h = sb("h", [P, DT, T])
        vfirst = sb("vfirst", [P, 4, T])
        cols = sb("cols", [P, NCOLS])
        kept = sb("kept", [P, KEPT])
        ident, ones, iota, half = (kept[:, i * P:(i + 1) * P] for i in range(4))
        zeros = sb("zeros", [P, 512], BF16)
        eps = sb("eps", [P, 4])
        cond = sb("cond", [P, 16])
        modc = sb("modc", [P, 24])
        rs, rv, rt = (sb(n_, [P, T]) for n_ in ("rs", "rv", "rt"))
        work = sb("work", [P, 2048])
        ijg = sb("ijg", [P, 3, T])
        PS = ctx.enter_context(nc.psum_tensor("psum", [P, 8, 512], F32))
        acc = PS[:, 4:8, :].rearrange("p b (s t) -> p (b s) t", s=2)
        sil = work[:, 0:1024].rearrange("p (b t) -> p b t", b=4)
        gat = work[:, 1024:2048].rearrange("p (b t) -> p b t", b=4)
        SQ = AR[:, 120:128, :]
        ATF = AR[:, 0:FT, :]

        def col(name, k=0, n=1):
            return cols[:, COLS[name] + k:COLS[name] + k + n]

        def const(name):
            s, n = CONSTS[name]
            return consts_d[:, s:s + n]

        def flat(v):
            return v.rearrange("p a b -> p (a b)")

        def bc(v, n):
            return v.rearrange("p (a b) -> p a b", b=1).to_broadcast([v.shape[0], v.shape[1], n])

        def rep(v, n):
            return v[:, None, :].to_broadcast([v.shape[0], n, v.shape[1]])

        EV, n_ev = {}, 0
        for name, count in (("ssd_z", ZT), ("ssd_xbc", XBCT), ("ssd_dt", 1), ("mla_in", 6), (("mix_in", 0), 18),
                            (("peer_q", 0), 16), (("mix_in", 1), 19), (("peer_q", 1), 16)):
            EV[name] = n_ev
            n_ev += count
        PRIME = 4

        Z, XS, BM, CM = AR[:, 0:16, :], AR[:, 16:32, :], AR[:, 32:40, :], AR[:, 40:48, :]
        XTOK = AR[:, 48:64, :].rearrange("p (a b) t -> p a (b t)", a=TT)
        Y = AR[:, 64:80, :]
        DTF, AF, SF, AUX = (AR[0:64, 80 + i, :] for i in range(4))
        NST = AR[:, 84, 0:128].rearrange("p (a b) -> p a b", a=TT)
        DTT = AR[:, 84, 128:256].rearrange("p (a b) -> p a b", a=TT)
        CBS = AR[:, 85:101, :].rearrange("p (g u) t -> p g u t", u=TT)
        PADS = AR[:, 101:106, :].rearrange("p a b -> p (a b)")[:, 0:4 * 260].rearrange("p (a b) -> p a b", a=4)
        CVA = AR[:, 106:110, :]
        EXB = AR[:, 110:113, :].rearrange("p a b -> p (a b)").rearrange("p (a b) -> p a b", a=2)
        MB = AR[:, 113:117, :].rearrange("p (c u) t -> p c u t", u=TT)
        TMP = AR[:, 117, :]
        CMASK = AR[:, 118, :]
        CMB = AR[:, 119, 0:128].bitcast(BF16)
        IDB = ctx.enter_context(nc.sbuf_tensor("ident_bf16", [P, P], BF16))
        QLAT, KVLAT, KPE = AR[:, 24:27, :], AR[:, 27:29, :], AR[:, 29, :]
        WUQ = AR[:, 32:50, :].rearrange("p a b -> p (a b)").rearrange("p (k n) -> p k n", k=3)
        WUKV = AR[:, 50:66, :].rearrange("p a b -> p (a b)").rearrange("p (k n) -> p k n", k=2)
        QH, KH = AR[0:QK, 66:82, :], AR[0:QK, 82:98, :]
        VTOK = AR[:, 98:106, :].rearrange("p (a b) t -> p a (b t)", a=TT)
        OT = AR[:, 106:114, :]
        COS, SIN = AR[0:QK, 114, :], AR[0:QK, 115, :]
        ANG = AR[0:QK, 116:120, :]
        SQM = AR[:, 0:16, :]
        PROB = AR[:, 0:4, :].rearrange("p (b q) t -> p b q t", b=2)
        PT = AR[:, 4:8, :].rearrange("p (b q) t -> p b q t", b=2)
        RPM = AR[0:QK, 31, 0:QK]
        STAT = AR[:, 30, :]
        RSM = AR[:, 16:20, :]
        def words(a, b):
            return AR[:, a:b, :].rearrange("p a b -> p (a b)")

        V_, BON, GG, PL = AR[:, 0:4, :], AR[:, 4:8, :], AR[:, 8:12, :], AR[:, 12:16, :]
        VTK = words(16, 20).rearrange("p (t n) -> p t n", t=TT)
        RCN = sum(CONSTS[n_][1] for n_ in ("mask4", "maskn", "restart", "recip"))
        RC = words(20, 28)
        rc_at = {}
        at = 0
        for name_ in ("mask4", "maskn", "restart", "recip"):
            rc_at[name_] = (at, at + CONSTS[name_][1])
            at += CONSTS[name_][1]
        MASK4, MASKN, RESTART, RECIP = (RC[:, a:b] for a, b in rc_at.values())
        WUP, GUP, VUP, POOLW = words(28, 30), words(30, 32), words(32, 34), words(34, 36)
        ST = AR[:, 36:53, :].rearrange("p c (m k) -> p c m k", m=4)
        LO, GD, VD = AR[:, 36, :], AR[:, 37, :], AR[0:32, 38, :]
        ZT_, YR = AR[:, 53:57, :], AR[:, 57:61, :]
        ARH = words(61, 69).rearrange("p (n k c) -> p n k c", n=8, k=2)
        BTIL, KTIL = AR[:, 69:73, :], AR[:, 73:77, :]
        KK, AA, LL, LD, EL, EM, R_, K_ = (AR[:, 77 + 4 * i:81 + 4 * i, :] for i in range(8))
        MM = words(77, 109).rearrange("p (c k n) -> p c k n", c=16, k=4)
        GT = words(77, 109).rearrange("p (m c n) -> p m c n", m=4, c=NCH)
        NA = words(109, 117).rearrange("p (c n) -> p c n", c=16)
        NB, NC_ = (words(61 + 8 * i, 69 + 8 * i).rearrange("p (c n) -> p c n", c=16) for i in range(2))
        WW = words(117, 125).rearrange("p (c n) -> p c n", c=16)
        XB, PQ = NB, NC_
        BEO = words(109, 117).rearrange("p (t h n) -> p t h n", t=TT, h=RH)
        KEO = words(117, 125).rearrange("p (t h n) -> p t h n", t=TT, h=RH)
        BHAT, KHAT = h[:, 0:4, :], h[:, 4:8, :]
        S0, S1 = (work[:, 1024 * i:1024 * (i + 1)].rearrange("p (m t) -> p m t", m=4) for i in range(2))
        ATK = work[:, 0:1024].rearrange("p (t n) -> p t n", t=TT)
        LC = rs[:, 0:64]
        ZPAD = words(109, 114)[:, 0:4 * 257].rearrange("p (a b) -> p a b", a=4)
        ZDIF = AR[:, 114:118, :]
        GNV, GNT = AR[:, 77:81, :], AR[:, 81:85, :]
        QP = AR[:, 0:16, :]
        KEYS = words(16, 24).rearrange("p (n k) -> p n k", n=16)
        SC, SC2 = (words(24 + 16 * i, 40 + 16 * i).rearrange("p (t n k) -> p t n k", t=TT, n=16) for i in range(2))
        VAL, IDX, IDXF = (words(56 + 2 * i, 58 + 2 * i).rearrange("p (t n k) -> p t n k", t=TT, n=16) for i in range(3))
        CAND, CAND2 = (words(62 + 16 * i, 78 + 16 * i).rearrange("p (t n k) -> p t n k", t=TT, n=PH) for i in range(2))
        TOP, SEL, HI, LOW = (words(94 + i, 95 + i).rearrange("p (t n k) -> p t n k", t=TT, n=PH) for i in range(4))
        EQ = words(98, 106)
        IJT = words(106, 109).rearrange("p (k t n) -> p k t n", k=3, t=TT)
        SELI = words(109, 110)
        SMX = words(110, 111)
        WALL = words(0, 128).rearrange("p (t j) -> p t j", t=T)
        OHI, OHJ = (work[:, 1024 * i:1024 * (i + 1)].rearrange("p (b t n) -> p b t n", b=2, t=4) for i in range(2))

        block = ctx.enter_context(nc.Block())

        @block.sync
        def _(sp):
            sp.dma_start(cols[:, :], cols_d).then_inc(sem["loads"], 16)
            sp.dma_start(x[:, :, :], x_d).then_inc(sem["loads"], 16)
            sp.dma_start(kept[:, :], consts_d[:, 0:KEPT]).then_inc(sem["loads"], 16)
            for s in range(RING):
                sp.dma_start(ring[:, s, :], stream[s]).then_inc(slot_full[s], 16)
            full = (NBLOCKS - RING) // RING
            with sp.Fori(0, full) as i:
                for s in range(RING):
                    sp.wait_ge(sem["block_used"], i * RING + (s + 1))
                    sp.dma_start(ring[:, s, :], stream[i * RING + (s + RING)]).then_inc(slot_full[s], 16)
            for n in range((full + 1) * RING, NBLOCKS):
                sp.wait_ge(sem["block_used"], n - RING + 1)
                sp.dma_start(ring[:, n % RING, :], stream[n]).then_inc(slot_full[n % RING], 16)
            sp.wait_ge(sem["out_ready"], DT)
            sp.dma_start(out_d, h[:, :, :]).then_inc(sem["out_done"], 16)
            sp.wait_ge(sem["out_done"], 16)

        @block.tensor
        def _(pe):
            def arrived(n, i=0):
                pe.wait_ge(slot_full[n % RING], (i + (n // RING + 1)) * 16)
                return ring[:, n % RING, :].rearrange("p (k c) -> p k c", k=8)

            def mod_columns(s):
                if s == 0:
                    pe.wait_ge(sem["cond_ready"], 1)
                else:
                    pe.wait_ge(sem["mod_cols"], s)
                base = BASE["mod", s]
                c0 = 0 if s < 6 else 8
                with pe.Fori(0, 3) as i:
                    for k in range(8):
                        w = arrived(base + k, i)
                        for d in range(DT):
                            mm = pe.matmul(PS[:, 3, bass.ds(i * 8 + k, 1)], w[:, d, :], cond[:, c0 + d:c0 + d + 1],
                                           start=(d == 0), stop=(d == DT - 1))
                        mm.then_inc(sem["block_used"], 1)

            def norm_sum(s):
                for d in range(DT):
                    pe.wait_ge(sem["norm_sq"], 8 * s + d + 1)
                    mm = pe.matmul(PS[:, 2, 0:T], ones, SQ[:, d, :], start=(d == 0), stop=(d == DT - 1))
                mm.then_inc(sem["norm_sum"], 1)

            def h_in(s):
                pe.wait_ge(sem["h_ready"], 8 * s + 8)

            def open_acc():
                for b in range(4):
                    pe.matmul(PS[:, 4 + b, :], zeros[:, 0:P], zeros[:, :], start=True, stop=False, skip_group_check=True)

            def add_rows(w, rhs):
                for d in range(DT):
                    mm = pe.matmul(acc[:, d, :], w[:, d, :], rhs, start=False, stop=False, skip_group_check=True)
                return mm

            def ffn(s, f):
                h_in(s)
                base = BASE["ffn", f]

                def pair(n, k, i):
                    for half_ in range(2):
                        w = arrived(base + n + half_, i)
                        if half_ == 0:
                            pe.wait_ge(sem["ffn_a"], i * 4 + (FT * f + k - 1 + PRIME - 2))
                        for d in range(DT):
                            mm = pe.matmul(PS[:, k % 2, half_ * T:(half_ + 1) * T], w[:, d, :], h[:, d, :],
                                           start=(d == 0), stop=(d == DT - 1))
                        mm.then_inc(sem["block_used"], 1)

                with pe.Fori(0, FT // 4) as i:
                    for k in range(4):
                        pair(2 * k, k, i)
                for k in range(FT // 4 * 4, FT):
                    pair(2 * k, k, 0)
                open_acc()
                rows = base + 2 * FT
                with pe.Fori(0, FT // 8) as i:
                    for k in range(8):
                        w = arrived(rows + k, i)
                        pe.wait_ge(sem["ffn_a"], i * 8 + (FT * f + k + 1 + PRIME - 2))
                        add_rows(w, ATF[:, i * 8 + k, :]).then_inc(sem["block_used"], 1)
                for k in range(FT // 8 * 8, FT):
                    w = arrived(rows + k)
                    pe.wait_ge(sem["ffn_a"], FT * f + k + 1 + PRIME - 2)
                    add_rows(w, ATF[:, k, :]).then_inc(sem["block_used"], 1)

            def project(first, count, ev, width=P, rows=0):
                if ev + PRIME > 0:
                    pe.wait_ge(sem["proj_evac"], ev + PRIME)

                def one(k, i):
                    w = arrived(first + k, i)
                    pe.wait_ge(sem["proj_evac"], i * 8 + (ev + k - 1 + PRIME))
                    for d in range(DT):
                        mm = pe.matmul(PS[rows:rows + width, k % 2, 0:T], w[:, d, 0:width],
                                       h[:, d, :], start=(d == 0), stop=(d == DT - 1))
                    mm.then_inc(sem["block_used"], 1)

                if count // 8:
                    with pe.Fori(0, count // 8) as i:
                        for k in range(8):
                            one(k, i)
                for k in range(count // 8 * 8, count):
                    one(k, 0)

            def out_project(first, rhs, ktiles=8):
                for d in range(DT):
                    for b in range(ktiles // 8):
                        w = arrived(first + d * (ktiles // 8) + b)
                        for k in range(8):
                            mm = pe.matmul(acc[:, d, :], w[:, k, :], rhs(8 * b + k), start=(b == 0 and k == 0),
                                           stop=(b == ktiles // 8 - 1 and k == 7))
                        mm.then_inc(sem["block_used"], 1)

            def ssd():
                h_in(1)
                b0 = BASE["ssd_in"]
                project(b0, ZT, EV["ssd_z"])
                project(b0 + ZT, XBCT, EV["ssd_xbc"])
                project(b0 + ZT + XBCT, 1, EV["ssd_dt"], width=64)
                pe.wait_ge(sem["conv_silu"], XBCT + PRIME)
                for tt in range(TT):
                    for q in range(4):
                        n = tt * 4 + q
                        if n >= 2:
                            pe.wait_ge(sem["ssd_xtok"], n - 1)
                        for j in range(4):
                            mm = pe.transpose(PS[:, 4 + n % 2, j * P:(j + 1) * P], XS[:, q * 4 + j, tt * P:(tt + 1) * P], ident)
                        mm.then_inc(sem["ssd_tr"], 1)
                pe.wait_ge(sem["ssd_dt"], 1)
                pe.wait_ge(sem["proj_evac"], EV["ssd_dt"] + 1 + PRIME)
                for tt in range(TT):
                    pe.transpose(PS[:, 0, tt * 64:(tt + 1) * 64], SF[:, tt * P:(tt + 1) * P], ident[0:64, 0:64])
                for tt in range(TT):
                    mm = pe.transpose(PS[:, 0, 128 + tt * 64:128 + (tt + 1) * 64], DTF[:, tt * P:(tt + 1) * P], ident[0:64, 0:64])
                mm.then_inc(sem["ssd_tr"], 1)
                for g in range(SSD_GROUPS):
                    if g >= 2:
                        pe.wait_ge(sem["ssd_cb_sb"], g - 1)
                    for u in range(TT):
                        mm = pe.matmul(PS[:, 6 + g % 2, u * T:(u + 1) * T], BM[:, g, u * P:(u + 1) * P], CM[:, g, :],
                                       start=True, stop=True)
                    mm.then_inc(sem["ssd_cb"], 1)
                pe.wait_ge(sem["ssd_xtok"], 9)
                pe.wait_ge(sem["ssd_cb_sb"], SSD_GROUPS)

                def segments(n):
                    hd, u = n // 2, n % 2
                    if n >= 2:
                        pe.wait_ge(sem["ssd_exp"], n - 1)
                    main, other = (hd, 32 + hd) if u == 0 else (32 + hd, hd)
                    bank = PS[:, n % 2, :]
                    tri = (CMB[:, 0:P], CMB[:, P:2 * P]) if u == 0 else (CMB[:, P:2 * P], CMB[:, 0:P])
                    pe.matmul(bank[:, 0:T], ident[0:64, main:main + 1].to_broadcast([64, P]), SF[:, :],
                              start=True, stop=False, skip_group_check=True)
                    pe.matmul(bank[:, u * P:(u + 1) * P], IDB[:, :], tri[0], start=False, stop=False, skip_group_check=True)
                    pe.matmul(bank[:, T:T + P], ident[0:64, other:other + 1].to_broadcast([64, P]), SF[:, u * P:(u + 1) * P],
                              start=False, stop=False, skip_group_check=True)
                    pe.matmul(bank[:, T:T + P], IDB[:, :], tri[1], start=False, stop=True, skip_group_check=True)\
                      .then_inc(sem["ssd_seg"], 1)

                def outputs(hd):
                    pe.wait_ge(sem["ssd_m"], 2 * hd + 2)
                    r = 64 * (hd % 2)
                    pair = hd // 2
                    if pair >= 2 and hd % 2 == 0:
                        pe.wait_ge(sem["ssd_yev"], pair - 1)
                    for u in range(TT):
                        mm = pe.matmul(PS[r:r + 64, 4 + pair % 2, 0:T], XTOK[:, u, hd * 64:(hd + 1) * 64], MB[:, hd % 2, u, :],
                                       start=(u == 0), stop=(u == TT - 1))
                    mm.then_inc(sem["ssd_y"], 1)

                for n in range(2 * SSD_HEADS + 2):
                    if n < 2 * SSD_HEADS:
                        segments(n)
                    if n >= 3 and n % 2 == 1:
                        outputs((n - 3) // 2)
                for g in range(SSD_GROUPS):
                    pe.wait_ge(sem["ssd_ysq"], 1)
                    for j in range(2):
                        mm = pe.matmul(acc[:, g, :], ones, AR[:, 16 + 2 * g + j, :], start=(j == 0), stop=(j == 1))
                mm.then_inc(sem["ssd_ysum"], 1)
                pe.wait_ge(sem["ssd_yn"], ZT)
                out_project(BASE["ssd_out"], lambda k: Y[:, k, :], 16)

            def mla():
                h_in(4)
                b0 = BASE["mla_in"]
                project(b0, 5, EV["mla_in"])
                w = arrived(b0 + 5)
                pe.wait_ge(sem["proj_evac"], EV["mla_in"] + 5 + PRIME)
                for d in range(DT):
                    mm = pe.matmul(PS[64:96, 1, 0:T], w[:, d, 0:ROPE], h[:, d, :], start=(d == 0), stop=(d == DT - 1))
                mm.then_inc(sem["block_used"], 1)
                pe.wait_ge(sem["mla_latsq"], 1)
                for k in range(3):
                    pe.matmul(PS[:, 1, 0:T], ones, SQM[:, k, :], start=(k == 0), stop=(k == 2))
                for k in range(2):
                    mm = pe.matmul(PS[:, 1, T:2 * T], ones, SQM[:, 3 + k, :], start=(k == 0), stop=(k == 1))
                mm.then_inc(sem["mla_latsum"], 1)
                pe.wait_ge(sem["mla_lat"], 1)
                pe.wait_ge(sem["mla_w"], 64)
                for n in range(16):
                    if n >= 4:
                        pe.wait_ge(sem["mla_pev"], n - 3)
                    for j in range(2):
                        hd = 2 * (n % 8) + j
                        o = PS[0:QK if n < 8 else NOPE, 4 + n % 4, j * T:(j + 1) * T]
                        if n < 8:
                            for k in range(3):
                                mm = pe.matmul(o, WUQ[:, k, hd * QK:(hd + 1) * QK], QLAT[:, k, :], start=(k == 0), stop=(k == 2))
                        else:
                            for k in range(2):
                                mm = pe.matmul(o, WUKV[:, k, hd * NOPE:(hd + 1) * NOPE], KVLAT[:, k, :],
                                               start=(k == 0), stop=(k == 1))
                    mm.then_inc(sem["mla_proj"], 1)
                for n in range(4):
                    tt, c = n // 2, n % 2
                    pe.wait_ge(sem["mla_pev"], 13 + n)
                    for k in range(2):
                        mm = pe.matmul(PS[:, 4 + n, :], KVLAT[:, k, tt * P:(tt + 1) * P],
                                       WUKV[:, k, 1024 + c * 512:1024 + (c + 1) * 512], start=(k == 0), stop=(k == 1))
                    mm.then_inc(sem["mla_proj"], 1)
                for n in range(16):
                    pe.wait_ge(sem["mla_sq"], n // 8 + 1)
                    if n >= 2:
                        pe.wait_ge(sem["mla_var"], n - 1)
                    pe.matmul(PS[0:QK, n % 2, :], ones[0:QK, 0:QK], flat(SQM[0:QK, 2 * (n % 8):2 * (n % 8) + 2, :]),
                              start=True, stop=True).then_inc(sem["mla_sum"], 1)
                pe.wait_ge(sem["mla_ang"], 1)
                pe.wait_ge(sem["mla_pev"], 20)
                for n in range(16):
                    q = QH if n < 8 else KH
                    pe.wait_ge(sem["mla_qkn"], n + 1)
                    if n >= 2:
                        pe.wait_ge(sem["mla_rope"], n - 1)
                    pe.matmul(PS[0:QK, 6 + n % 2, :], RPM, flat(q[:, 2 * (n % 8):2 * (n % 8) + 2, :]),
                              start=True, stop=True).then_inc(sem["mla_rot"], 1)
                pe.wait_ge(sem["mla_rope"], 16)

                def logits(hd):
                    if hd >= 2:
                        pe.wait_ge(sem["mla_exp"], hd - 1)
                    for q in range(TT):
                        mm = pe.matmul(PS[:, hd % 2, q * T:(q + 1) * T], QH[:, hd, q * P:(q + 1) * P], KH[:, hd, :],
                                       start=True, stop=True)
                    mm.then_inc(sem["mla_logit"], 1)

                def turn(hd):
                    pe.wait_ge(sem["mla_prob"], hd + 1)
                    if hd >= 2:
                        pe.wait_ge(sem["mla_pts"], hd - 1)
                    for k in range(TT):
                        for q in range(TT):
                            mm = pe.transpose(PS[:, 2 + hd % 2, k * T + q * P:k * T + (q + 1) * P],
                                              PROB[:, hd % 2, q, k * P:(k + 1) * P], ident)
                    mm.then_inc(sem["mla_pt"], 1)

                def values(hd):
                    pe.wait_ge(sem["mla_pts"], hd + 1)
                    pair, r = hd // 2, 64 * (hd % 2)
                    if pair >= 2 and hd % 2 == 0:
                        pe.wait_ge(sem["mla_oev"], pair - 1)
                    for k in range(TT):
                        mm = pe.matmul(PS[r:r + 64, 4 + pair % 2, 0:T], VTOK[:, k, hd * MV:(hd + 1) * MV], PT[:, hd % 2, k, :],
                                       start=(k == 0), stop=(k == TT - 1))
                    mm.then_inc(sem["mla_o"], 1)

                for n in range(MH + 2):
                    if n < MH:
                        logits(n)
                    if 1 <= n <= MH:
                        turn(n - 1)
                    if n >= 2:
                        values(n - 2)
                pe.wait_ge(sem["mla_oev"], 8)
                out_project(BASE["mla_out"], lambda k: OT[:, k, :])

            def rwkv(l):
                h_in(6 + 2 * l)
                project(BASE["mix_in", l], 18, EV["mix_in", l])
                if l == 1:
                    w = arrived(BASE["mix_in", 1] + 18)
                    pe.wait_ge(sem["proj_evac"], EV["mix_in", 1] + 18 + PRIME)
                    for d in range(DT):
                        mm = pe.matmul(PS[0:32, 0, 0:T], w[:, d, 0:32], h[:, d, :], start=(d == 0), stop=(d == DT - 1))
                    mm.then_inc(sem["block_used"], 1)
                pe.wait_ge(sem["rw_w"], 64 + 80 * l)
                pe.wait_ge(sem["rw_lo"], l + 1)
                pe.wait_ge(sem["proj_evac"], EV["mix_in", l] + 18 + l + PRIME)
                for m in range(4):
                    pe.matmul(PS[:, m // 2, (m % 2) * T:(m % 2 + 1) * T], WUP[0:64, m * P:(m + 1) * P], LO[0:64, :],
                              start=True, stop=True)
                for m in range(4):
                    pe.matmul(acc[:, m, :], WUP[64:128, m * P:(m + 1) * P], LO[64:128, :], start=True, stop=True)
                for m in range(4):
                    mm = pe.matmul(acc[:, 4 + m, :], GUP[:, m * P:(m + 1) * P], GD, start=True, stop=True)
                mm.then_inc(sem["rw_lora"], 1)
                if l == 1:
                    pe.wait_ge(sem["rw_gates"], 3 * l + 1)
                    for m in range(4):
                        mm = pe.matmul(PS[:, m // 2, (m % 2) * T:(m % 2 + 1) * T], VUP[0:32, m * P:(m + 1) * P], VD,
                                       start=True, stop=True)
                    mm.then_inc(sem["rw_vres"], 1)
                pe.wait_ge(sem["rw_kksq"], l + 1)
                pe.wait_ge(sem["rw_gates"], 3 * l + 3)
                for c in range(2):
                    mm = pe.matmul(PS[:, 4 + c, :], half, flat(S0[:, 2 * c:2 * c + 2, :]), start=True, stop=True)
                mm.then_inc(sem["rw_kksum"], 1)
                pe.wait_ge(sem["rw_feat"], l + 1)

                def turned(n, src):
                    if n >= 2:
                        pe.wait_ge(sem["rw_trev"], 8 * l + n - 1)
                    for m in range(4):
                        mm = pe.transpose(PS[:, 6 + n % 2, m * P:(m + 1) * P], src(m), ident)
                    mm.then_inc(sem["rw_tr"], 1)

                for tt in range(TT):
                    turned(tt, lambda m: ARH[:, 2 * m + tt, 0, :])
                for tt in range(TT):
                    turned(2 + tt, lambda m: V_[:, m, tt * P:(tt + 1) * P])
                for c in range(16):
                    hd, tt = c // 2, c % 2
                    m, r = hd // 2, 64 * (hd % 2)
                    if c >= 4:
                        pe.wait_ge(sem["rw_matev"], 20 * l + 5 * ((c - 4) // 4) + (c - 4) % 4 + 1)
                    arh = ARH[r:r + 64, 2 * m + tt, :, :].rearrange("p a b -> p (a b)")
                    tok = slice(tt * P, (tt + 1) * P)
                    bank = PS[:, c % 4, :]
                    pe.matmul(bank[:, 0:2 * P], BTIL[r:r + 64, m, tok], arh, start=True, stop=True)
                    pe.matmul(bank[:, 2 * P:4 * P], KTIL[r:r + 64, m, tok], arh, start=True, stop=True)\
                      .then_inc(sem["rw_mat"], 1)
                    if c % 4 == 0 and c >= 8:
                        pe.wait_ge(sem["rw_matev"], 20 * l + 5 * (c // 4 - 2) + 5)
                    if c == 0:
                        pe.wait_ge(sem["rw_kksqrt"], l + 1)
                    if c == 4:
                        pe.wait_ge(sem["rw_trev"], 8 * l + 4)
                    mm = pe.matmul(PS[:, 4 + 2 * (m % 2) + hd % 2, tt * P:(tt + 1) * P], ARH[r:r + 64, 2 * m + tt, 0, :],
                                   BTIL[r:r + 64, m, tok], start=True, stop=True)
                    if c % 4 == 3:
                        mm.then_inc(sem["rw_mat"], 1)
                pe.wait_ge(sem["rw_trev"], 8 * l + 4)
                pe.wait_ge(sem["rw_matev"], 20 * (l + 1))
                m1 = MM[:, :, 0, :]
                steps = ((m1, NA), (NA, m1), (NB, WW), (NC_, NB), (NB, NC_), (NA, WW), (NC_, NA), (NB, WW))
                after = (None, None, 0, 1, 2, 3, 4, 6)
                for st, (lhs, rhs) in enumerate(steps):
                    for b in range(4):
                        if after[st] is not None:
                            pe.wait_ge(sem["rw_neuev"], 36 * l + 4 + 4 * after[st] + b + 1)
                        for j in range(4):
                            c = 4 * b + j
                            mm = pe.matmul(PS[:, (4 * st + b) % 8, j * P:(j + 1) * P], lhs[:, c, :], rhs[:, c, :], start=True, stop=True)
                        mm.then_inc(sem["rw_neu"], 1)
                pe.wait_ge(sem["rw_neuev"], 36 * (l + 1))
                for b in range(2):
                    for j in range(8):
                        c = 8 * b + j
                        hd, tt = c // 2, c % 2
                        mm = pe.matmul(PS[:, b, j * 64:(j + 1) * 64], MM[:, c, 2, :], VTK[:, tt, hd * 64:(hd + 1) * 64],
                                       start=True, stop=True)
                mm.then_inc(sem["rw_x"], 1)
                pe.wait_ge(sem["rw_xev"], l + 1)
                for c in range(16):
                    mm = pe.matmul(PS[:, 4 + c // 4, (c % 4) * P:(c % 4 + 1) * P], WW[:, c, :], XB[:, c, :], start=True, stop=True)
                mm.then_inc(sem["rw_pq"], 1)
                pe.wait_ge(sem["rw_pqev"], l + 1)
                for hd in range(RH):
                    m, r = hd // 2, 64 * (hd % 2)
                    for tt in range(TT):
                        c = 2 * hd + tt
                        at = (m % 2) * T + tt * P
                        oz, oy = PS[r:r + 64, m // 2, at:at + P], PS[r:r + 64, 2 + m // 2, at:at + P]
                        pe.matmul(oz, PQ[:, c, 0:64], MM[:, c, 1, :], start=True, stop=True)
                        pe.matmul(oy, PQ[:, c, 64:128], MM[:, c, 1, :], start=True, stop=False)
                        mm = pe.matmul(oy, VTK[:, tt, hd * 64:(hd + 1) * 64], MM[:, c, 3, :], start=False, stop=True)
                mm.then_inc(sem["rw_zy"], 1)
                for tt in range(TT):
                    turned(4 + tt, lambda m: BHAT[:, m, tt * P:(tt + 1) * P])
                for tt in range(TT):
                    turned(6 + tt, lambda m: KHAT[:, m, tt * P:(tt + 1) * P])
                pe.wait_ge(sem["rw_trev"], 8 * (l + 1))
                for m in range(4):
                    if m:
                        pe.wait_ge(sem["rw_ghev"], 4 * l + m)
                    for a in range(2):
                        hd, r = 2 * m + a, 64 * a
                        for tt in range(TT):
                            for q in range(4):
                                rows = slice(32 * q, 32 * q + 32)
                                pq = PQ[rows, 2 * hd + tt, :]
                                o = PS[r:r + 64, 4 + q, :]
                                pe.matmul(o[:, tt * P:(tt + 1) * P], pq[:, 0:64], BEO[rows, tt, hd, :], start=True, stop=True,
                                          tile_position=(32 * q, r))
                                for par in range(2):
                                    at = 256 + tt * P + par * 64
                                    pe.matmul(o[:, at:at + 64], BEO[rows, tt, hd, par * 64:(par + 1) * 64], pq[:, 64:128],
                                              start=True, stop=False, tile_position=(32 * q, r))
                                    mm = pe.matmul(o[:, at:at + 64], KEO[rows, tt, hd, par * 64:(par + 1) * 64],
                                                   VTK[rows, tt, hd * 64:(hd + 1) * 64], start=False, stop=True,
                                                   tile_position=(32 * q, r))
                    mm.then_inc(sem["rw_gh"], 1)
                pe.wait_ge(sem["rw_ghev"], 4 * (l + 1))
                for c in range(NCH - 1):
                    pe.wait_ge(sem["rw_state"], NCH * l + c + 1)
                    for m in range(4):
                        mm = pe.matmul(PS[:, 4 + c % 2, m * 64:(m + 1) * 64], GT[:, m, c, :], ST[:, c, m, :],
                                       start=True, stop=True)
                    mm.then_inc(sem["rw_step"], 1)
                pe.wait_ge(sem["rw_state"], NCH * (l + 1))
                pe.wait_ge(sem["rw_zyev"], l + 1)
                for hd in range(RH):
                    m, r = hd // 2, 64 * (hd % 2)
                    for c in range(NCH):
                        at = (m % 2) * T + c * CH
                        mm = pe.matmul(PS[r:r + 64, (6 if r else 0) + m // 2, at:at + CH], ST[r:r + 64, c, m, :],
                                       ZT_[r:r + 64, m, c * CH:(c + 1) * CH], start=True, stop=True)
                mm.then_inc(sem["rw_y"], 1)
                pe.wait_ge(sem["rw_yall"], l + 1)
                for c in range(2):
                    mm = pe.matmul(PS[:, 2 + c, :], half, flat(YR[:, 2 * c:2 * c + 2, :]), start=True, stop=True)
                mm.then_inc(sem["rw_mean"], 1)
                for c in range(2):
                    mm = pe.matmul(PS[:, 4 + c, :], half, flat(BON[:, 2 * c:2 * c + 2, :]), start=True, stop=True)
                mm.then_inc(sem["rw_bonus"], 1)
                pe.wait_ge(sem["rw_pool"], l + 1)
                for m in range(4):
                    mm = pe.matmul(PS[:, 6 + m // 2, (m % 2) * T:(m % 2 + 1) * T], POOLW[:, m * P:(m + 1) * P], PL[:, m, :],
                                   start=True, stop=True)
                mm.then_inc(sem["rw_pl"], 1)
                pe.wait_ge(sem["rw_cent"], l + 1)
                for c in range(2):
                    mm = pe.matmul(PS[:, c, :], half, flat(S0[:, 2 * c:2 * c + 2, :]), start=True, stop=True)
                mm.then_inc(sem["rw_var"], 1)
                pe.wait_ge(sem["rw_mix"], l + 1)
                out_project(BASE["mix_out", l], lambda k: YR[:, k, :] if k < 4 else PL[:, k - 4, :])

            def peer(l):
                h_in(7 + 2 * l)
                project(BASE["peer_q", l], 16, EV["peer_q", l])
                pe.wait_ge(sem["proj_evac"], EV["peer_q", l] + 16 + PRIME)
                pe.wait_ge(sem["pe_keys"], 16 * (l + 1))
                for tt in range(TT):
                    for b in range(4):
                        n = tt * 4 + b
                        if n >= 4:
                            pe.wait_ge(sem["pe_scev"], 8 * l + n - 3)
                        for j in range(4):
                            hp = 4 * b + j
                            mm = pe.matmul(PS[:, 4 + n % 4, j * P:(j + 1) * P], QP[:, hp, tt * P:(tt + 1) * P], KEYS[:, hp, :],
                                           start=True, stop=True)
                        mm.then_inc(sem["pe_sc"], 1)
                pe.wait_ge(sem["pe_sm"], l + 1)
                for k in range(3):
                    for tt in range(TT):
                        o = PS[:, k // 2, (k % 2) * T + tt * P:(k % 2) * T + (tt + 1) * P]
                        mm = pe.transpose(o, IJT[:, k, tt, :], ident)
                mm.then_inc(sem["pe_tr"], 1)
                pe.wait_ge(sem["pe_ijg"], l + 1)
                with pe.Fori(0, T // 8) as i:
                    for k in range(2):
                        pe.wait_ge(sem["pe_oh"], i * 2 + (64 * l + k + 1))
                        pe.wait_ge(sem["pe_wev"], i * 2 + (64 * l + k - 1 + PRIME))
                        for j in range(4):
                            mm = pe.matmul(PS[:, k, j * P:(j + 1) * P], OHI[:, k, j, :], OHJ[:, k, j, :],
                                           start=True, stop=True)
                        mm.then_inc(sem["pe_w"], 1)
                pe.wait_ge(sem["pe_wev"], 64 * (l + 1) + PRIME)
                open_acc()
                base = BASE["uv", l]

                def down(n, j, i):
                    w = arrived(base + n, i)
                    pe.wait_ge(sem["pe_gelu"], i * 4 + (NK * l + j - 1 + PRIME))
                    for d in range(DT):
                        mm = pe.matmul(PS[:, j % 2, 0:T], w[:, d, :], h[:, d, :], start=(d == 0), stop=(d == DT - 1))
                    mm.then_inc(sem["block_used"], 1)

                def up(n, j, i):
                    w = arrived(base + n, i)
                    pe.wait_ge(sem["pe_gated"], i * 4 + (NK * l + j + 1 + PRIME))
                    add_rows(w, gat[:, j % 4, :]).then_inc(sem["block_used"], 1)

                down(0, 0, 0)
                whole = (NK - 1) // 4
                with pe.Fori(0, whole) as i:
                    for k in range(4):
                        down(1 + 2 * k, k + 1, i)
                        up(2 + 2 * k, k, i)
                for j in range(4 * whole, NK - 1):
                    down(1 + 2 * j, j + 1, 0)
                    up(2 + 2 * j, j, 0)
                up(2 * NK - 1, NK - 1, 0)

            pe.wait_ge(sem["inits"], 4)
            pe.wait_ge(sem["loads"], 48)
            for i in range(2):
                for s, stage in ((3 * i, lambda: ffn(3 * i, 2 * i)), (3 * i + 1, ssd if i == 0 else mla),
                                 (3 * i + 2, lambda: ffn(3 * i + 2, 2 * i + 1))):
                    mod_columns(s)
                    norm_sum(s)
                    stage()
            for l in range(2):
                for s, stage in ((6 + 2 * l, rwkv), (7 + 2 * l, peer)):
                    mod_columns(s)
                    norm_sum(s)
                    stage(l)
            norm_sum(NSUB)


        @block.scalar
        def _(act):
            chain = [0]

            def link(ins):
                chain[0] += 1
                ins.then_inc(sem["act_chain"], 1)
                act.wait_ge(sem["act_chain"], chain[0])

            def ready(n, i=0):
                act.wait_ge(sem["block_used"], i * RING + (n + 1))

            def norm_squares(s):
                for d in range(DT):
                    if s:
                        act.wait_ge(sem["x_upd"], 8 * (s - 1) + d + 1)
                    act.activation(SQ[:, d, :], x[:, d, :], ACT.Square).then_inc(sem["norm_sq"], 1)
                act.wait_ge(sem["norm_var"], s + 1)
                act.activation(rs[:, :], rv[:, :], ACT.Sqrt).then_inc(sem["norm_sqrt"], 1)

            def shift(s):
                for d in range(DT):
                    act.wait_ge(sem["norm_scaled"], 8 * s + d + 1)
                    act.activation(h[:, d, :], h[:, d, :], ACT.Identity, bias=modc[:, d:d + 1], scale=1.0)\
                       .then_inc(sem["h_ready"], 1)

            def ffn(f):
                base = BASE["ffn", f]

                def gate(k, i):
                    act.wait_ge(sem["block_used"], i * 8 + (base + 2 * k + 2))
                    act.activation(sil[:, k % 4, :], PS[:, k % 2, 0:T], ACT.Silu).then_inc(sem["ffn_silu"], 1)

                with act.Fori(0, FT // 4) as i:
                    for k in range(4):
                        gate(k, i)
                for k in range(FT // 4 * 4, FT):
                    gate(k, 0)

            def ssd():
                b0 = BASE["ssd_in"]
                with act.Fori(0, ZT // 8) as i:
                    for k in range(8):
                        ready(b0 + k, i)
                        act.activation(Z[:, i * 8 + k, :], PS[:, k % 2, 0:T], ACT.Silu)\
                           .then_inc(sem["proj_evac"], 1)
                with act.Fori(0, XBCT // 8) as i:
                    for k in range(8):
                        ready(b0 + ZT + k, i)
                        act.activation(PADS[:, k % 4, 2:2 + T], PS[:, k % 2, 0:T], ACT.Copy)\
                           .then_inc(sem["proj_evac"], 1)
                        act.wait_ge(sem["conv_step"], i * 40 + 5 * (k + 1))
                        act.activation(AR[:, i * 8 + (16 + k), :], CVA[:, k % 4, :], ACT.Silu,
                                       bias=cols[:, bass.ds(i * 8 + (COLS["conv_b"] + k), 1)], scale=1.0)\
                           .then_inc(sem["conv_silu"], 1)
                ready(b0 + ZT + XBCT)
                act.activation(AUX, PS[0:64, 0, 0:T], ACT.Abs, bias=col("dt_bias")[0:64, :], scale=1.0)
                act.activation(DTF, PS[0:64, 0, 0:T], ACT.Relu, bias=col("dt_bias")[0:64, :], scale=1.0)\
                   .then_inc(sem["proj_evac"], 1)
                act.wait_ge(sem["proj_evac"], EV["ssd_dt"] + 1 + PRIME)
                link(act.activation(eps[0:64, 2:3], col("a_log")[0:64, :], ACT.Exp))
                act.activation(AUX, AUX, ACT.Exp, scale=-1.0).then_inc(sem["ssd_abs"], 1)
                act.wait_ge(sem["ssd_w"], 1)
                act.activation(AF, SF, ACT.Ln).then_inc(sem["ssd_ln"], 1)
                for n in range(8):
                    act.wait_ge(sem["ssd_tr"], n + 1)
                    act.activation(XTOK[:, n // 4, (n % 4) * 512:(n % 4 + 1) * 512], PS[:, 4 + n % 2, :], ACT.Copy)\
                       .then_inc(sem["ssd_xtok"], 1)
                act.wait_ge(sem["ssd_tr"], 9)
                act.activation(flat(NST), PS[:, 0, 0:P], ACT.Copy, scale=-1.0)
                act.activation(flat(DTT), PS[:, 0, P:2 * P], ACT.Copy).then_inc(sem["ssd_xtok"], 1)
                for g in range(SSD_GROUPS):
                    act.wait_ge(sem["ssd_cb"], g + 1)
                    act.activation(flat(CBS[:, g, :, :]), PS[:, 6 + g % 2, :], ACT.Copy).then_inc(sem["ssd_cb_sb"], 1)
                act.wait_ge(sem["ssd_xtok"], 9)
                for n in range(2 * SSD_HEADS):
                    hd, u = n // 2, n % 2
                    main, other = (hd, 32 + hd) if u == 0 else (32 + hd, hd)
                    act.wait_ge(sem["ssd_seg"], n + 1)
                    if n >= 2:
                        act.wait_ge(sem["ssd_m"], n - 1)
                    act.activation(EXB[:, n % 2, 0:T], PS[:, n % 2, 0:T], ACT.Exp, bias=NST[:, u, main:main + 1], scale=1.0)
                    act.activation(EXB[:, n % 2, T:T + P], PS[:, n % 2, T:T + P], ACT.Exp, bias=NST[:, u, other:other + 1],
                                   scale=1.0).then_inc(sem["ssd_exp"], 1)
                act.wait_ge(sem["ssd_yz"], 1)
                act.activation(flat(XS), flat(Y), ACT.Square).then_inc(sem["ssd_ysq"], 1)
                act.wait_ge(sem["ssd_var"], 1)
                act.activation(flat(BM), flat(CM), ACT.Sqrt).then_inc(sem["ssd_ysqrt"], 1)

            def mla():
                b0 = BASE["mla_in"]
                for k in range(5):
                    ready(b0 + k)
                    act.activation(AR[:, 24 + k, :], PS[:, k % 2, 0:T], ACT.Copy)\
                       .then_inc(sem["proj_evac"], 1)
                ready(b0 + 5)
                act.activation(KPE[64:96, :], PS[64:96, 1, 0:T], ACT.Copy).then_inc(sem["proj_evac"], 1)
                act.wait_ge(sem["proj_evac"], EV["mla_in"] + 6 + PRIME)
                act.activation(flat(SQM[:, 0:5, :]), flat(AR[:, 24:29, :]), ACT.Square).then_inc(sem["mla_latsq"], 1)
                act.wait_ge(sem["mla_latvar"], 1)
                act.activation(flat(RSM[:, 0:2, :]), flat(AR[:, 20:22, :]), ACT.Sqrt)\
                   .then_inc(sem["mla_latsqrt"], 1)

                def evac(n):
                    act.wait_ge(sem["mla_proj"], n + 1)
                    if n < 16:
                        rows = QK if n < 8 else NOPE
                        o = AR[0:rows, 66 + 2 * n:68 + 2 * n, :]
                        act.activation(flat(o), PS[0:rows, 4 + n % 4, :], ACT.Copy).then_inc(sem["mla_pev"], 1)
                    else:
                        c = n - 16
                        act.activation(VTOK[:, c // 2, (c % 2) * 512:(c % 2 + 1) * 512], PS[:, 4 + c, :], ACT.Copy)\
                           .then_inc(sem["mla_pev"], 1)

                for n in range(8):
                    evac(n)
                act.wait_ge(sem["mla_pev"], 8)
                act.activation(flat(SQM[0:QK, :, :]), flat(QH), ACT.Square).then_inc(sem["mla_sq"], 1)
                for n in range(8, 20):
                    evac(n)
                for n in range(16):
                    if n == 8:
                        act.wait_ge(sem["mla_sum"], 8)
                        act.wait_ge(sem["mla_kpe"], 1)
                        act.wait_ge(sem["mla_pev"], 16)
                        act.activation(flat(SQM[0:QK, :, :]), flat(KH), ACT.Square).then_inc(sem["mla_sq"], 1)
                    act.wait_ge(sem["mla_var"], n + 1)
                    act.activation(flat(RSM[0:QK, 2 * (n % 2):2 * (n % 2) + 2, :]),
                                   flat(AR[0:QK, 20 + 2 * (n % 2):22 + 2 * (n % 2), :]), ACT.Sqrt).then_inc(sem["mla_sqrt"], 1)
                act.wait_ge(sem["mla_angr"], 1)
                act.activation(SIN, ANG[:, 1, :], ACT.Sin)
                act.activation(COS, ANG[:, 2, :], ACT.Sin).then_inc(sem["mla_ang"], 1)
                for n in range(MH + 1):
                    if n < MH:
                        act.wait_ge(sem["mla_max"], n + 1)
                        if n >= 2:
                            act.wait_ge(sem["mla_pt"], n - 1)
                        for q in range(TT):
                            e = act.activation(PROB[:, n % 2, q, :], PS[:, n % 2, q * T:(q + 1) * T], ACT.Exp,
                                               bias=STAT[:, 8 * n + 2 + q:8 * n + 3 + q], scale=QK ** -0.5,
                                               accum_out=STAT[:, 8 * n + 4 + q:8 * n + 5 + q])
                        e.then_inc(sem["mla_exp"], 1)
                    if n >= 1:
                        act.wait_ge(sem["mla_pt"], n)
                        if n >= 3:
                            act.wait_ge(sem["mla_o"], n - 2)
                        act.activation(flat(PT[:, (n - 1) % 2, :, :]), PS[:, 2 + (n - 1) % 2, :], ACT.Copy)\
                           .then_inc(sem["mla_pts"], 1)

            def rwkv(l):
                first, shifted = BASE["mix_in", l], 14 * l
                act.wait_ge(sem["rw_zpad"], l + 1)
                for n in range(18 + l):
                    ready(first + n)
                    bank = PS[:, n % 2, 0:T]
                    if n < 14:
                        if n >= 4:
                            act.wait_ge(sem["rw_shift"], shifted + n - 3)
                        act.activation(ZPAD[:, n % 4, 1:1 + T], bank, ACT.Copy).then_inc(sem["proj_evac"], 1)
                    elif n < 18:
                        act.activation(PL[:, n - 14, :], bank, ACT.Copy).then_inc(sem["proj_evac"], 1)
                    else:
                        act.wait_ge(sem["rw_shift"], shifted + 14)
                        act.activation(ZPAD[0:32, 2, 1:1 + T], PS[0:32, 0, 0:T], ACT.Copy).then_inc(sem["proj_evac"], 1)
                act.wait_ge(sem["rw_shift"], shifted + 14 + l)
                act.activation(LO[0:64, :], LO[0:64, :], ACT.Tanh)
                act.activation(GD, GD, ACT.Sigmoid).then_inc(sem["rw_lo"], 1)
                act.wait_ge(sem["rw_lora"], l + 1)
                for m in range(4):
                    e = act.activation(LD[:, m, :], PS[:, m // 2, (m % 2) * T:(m % 2 + 1) * T], ACT.Sigmoid,
                                       bias=col("w0", 4 * l + m), scale=1.0)
                e.then_inc(sem["rw_gates"], 1)
                for m in range(4):
                    e = act.activation(AA[:, m, :], acc[:, m, :], ACT.Sigmoid, bias=col("a0", 4 * l + m), scale=1.0)
                e.then_inc(sem["rw_gates"], 1)
                act.activation(flat(GG), flat(acc[:, 4:8, :]), ACT.Copy).then_inc(sem["rw_gates"], 1)
                if l == 1:
                    act.wait_ge(sem["rw_vres"], 1)
                    for m in range(4):
                        e = act.activation(S0[:, m, :], PS[:, m // 2, (m % 2) * T:(m % 2 + 1) * T], ACT.Sigmoid,
                                           bias=col("vres_v0", m), scale=1.0)
                    e.then_inc(sem["rw_vresa"], 1)
                act.wait_ge(sem["rw_kkvar"], l + 1)
                act.activation(flat(S0), flat(KTIL), ACT.Sqrt).then_inc(sem["rw_kksqrt"], 1)
                act.wait_ge(sem["rw_ld"], l + 1)
                act.activation(flat(EL), flat(LL), ACT.Exp)
                act.activation(flat(EM), flat(LL), ACT.Exp, scale=-1.0)
                act.activation(flat(LD), flat(LD), ACT.Exp).then_inc(sem["rw_exps"], 1)
                act.wait_ge(sem["rw_gnvar"], l + 1)
                act.activation(flat(S0), flat(GNV), ACT.Sqrt).then_inc(sem["rw_sd"], 1)

            def peer(l):
                for n in range(16):
                    ready(BASE["peer_q", l] + n)
                    act.activation(QP[:, n, :], PS[:, n % 2, 0:T], ACT.Copy)\
                       .then_inc(sem["proj_evac"], 1)
                for n in range(8):
                    act.wait_ge(sem["pe_sc"], 8 * l + n + 1)
                    o = SC[:, n // 4, 4 * (n % 4):4 * (n % 4) + 4, :]
                    act.activation(flat(o), PS[:, 4 + n % 4, :], ACT.Copy).then_inc(sem["pe_scev"], 1)
                act.wait_ge(sem["pe_top"], l + 1)
                act.activation(SMX, SMX, ACT.Exp).then_inc(sem["pe_exp"], 1)
                act.wait_ge(sem["pe_tr"], l + 1)
                act.activation(flat(ijg[:, :, :]), PS[:, 0:2, :].rearrange("p a b -> p (a b)")[:, 0:3 * T], ACT.Copy)\
                   .then_inc(sem["pe_ijg"], 1)
                with act.Fori(0, T // 8) as i:
                    for k in range(2):
                        act.wait_ge(sem["pe_w"], i * 2 + (64 * l + k + 1 + 2))
                        act.activation(WALL[:, bass.ds(i * 8 + 4 * k, 4), :].rearrange("p a b -> p (a b)"), PS[:, k, :], ACT.Copy)\
                           .then_inc(sem["pe_wev"], 1)
                base = BASE["uv", l]

                def gelu(j, i):
                    act.wait_ge(sem["block_used"], i * 8 + (base + max(1, 2 * j)))
                    act.activation(sil[:, j % 4, :], PS[:, j % 2, 0:T], ACT.Gelu).then_inc(sem["pe_gelu"], 1)

                for j in range(4):
                    gelu(j, 0)
                with act.Fori(0, NK // 4 - 1) as i:
                    for k in range(4):
                        gelu(4 + k, i)

            act.sem_inc(sem["proj_evac"], PRIME)
            act.sem_inc(sem["conv_silu"], PRIME)
            act.sem_inc(sem["pe_wev"], PRIME)
            act.sem_inc(sem["pe_gelu"], PRIME)
            act.sem_inc(sem["pe_gated"], PRIME)
            act.sem_inc(sem["ffn_a"], PRIME - 2)
            act.sem_inc(sem["pe_w"], 2)
            act.wait_ge(sem["inits"], 4)
            act.wait_ge(sem["loads"], 48)
            act.activation(cond[:, :], cols[:, 0:16], ACT.Silu).then_inc(sem["cond_ready"], 1)
            for s in range(NSUB):
                norm_squares(s)
                shift(s)
                if s in (0, 2, 3, 5):
                    ffn((0, 2, 3, 5).index(s))
                elif s == 1:
                    ssd()
                elif s == 4:
                    mla()
                elif s % 2 == 0:
                    rwkv((s - 6) // 2)
                else:
                    peer((s - 7) // 2)
            norm_squares(NSUB)

        @block.vector
        def _(dve):
            chain = [0]

            def link(ins):
                chain[0] += 1
                ins.then_inc(sem["dve_chain"], 1)
                dve.wait_ge(sem["dve_chain"], chain[0])

            def ready(n):
                dve.wait_ge(sem["block_used"], n + 1)

            def inverse_root(r, v, t):
                link(dve.reciprocal(r, r))
                link(dve.scalar_tensor_tensor(t, r, -0.5, v, ALU.mult, ALU.mult))
                link(dve.tensor_tensor(t, t, r, ALU.mult))
                link(dve.scalar_tensor_tensor(r, t, 1.5, r, ALU.add, ALU.mult))

            def mod_columns(s):
                if s:
                    dve.wait_ge(sem["x_upd"], 8 * s)
                ready(BASE["mod", s] + 23)
                bias = col("b_mod", 24 * s, 24) if s < 6 else col("ada_b", 24 * (s - 6), 24)
                g = col("norm_g", 8 * s, 8) if s < 6 else col("ln1" if s % 2 == 0 else "ln2", 8 * ((s - 6) // 2), 8)
                dve.tensor_tensor(modc[:, :], PS[:, 3, 0:24], bias, ALU.add).then_inc(sem["mod_cols"], 1)
                dve.wait_ge(sem["mod_cols"], s + 1)
                link(dve.scalar_tensor_tensor(modc[:, 8:16], modc[:, 8:16], 1.0, g, ALU.add, ALU.mult))
                if s in (0, 2, 3, 5):
                    link(dve.tensor_scalar(modc[:, 16:24], modc[:, 16:24], 0.5, None, ALU.mult))

            def normed(s):
                dve.wait_ge(sem["norm_sum"], s + 1)
                dve.tensor_scalar(rv[:, :], PS[:, 2, 0:T], 1.0 / D, EPS, ALU.mult, ALU.add).then_inc(sem["norm_var"], 1)
                dve.wait_ge(sem["norm_sqrt"], s + 1)
                inverse_root(rs[:, :], rv[:, :], rt[:, :])
                for d in range(DT):
                    g = modc[:, 8 + d:9 + d] if s < NSUB else col("lnf", d)
                    dve.scalar_tensor_tensor(h[:, d, :], x[:, d, :], g, rs[:, :], ALU.mult, ALU.mult)\
                       .then_inc(sem["norm_scaled" if s < NSUB else "out_ready"], 1)

            def residual(last):
                for d in range(DT):
                    ready(last(d | 1))
                    dve.scalar_tensor_tensor(x[:, d, :], acc[:, d, :], modc[:, 16 + d:17 + d], x[:, d, :], ALU.mult, ALU.add)\
                       .then_inc(sem["x_upd"], 1)

            def ffn(f):
                base = BASE["ffn", f]

                def product(k, i):
                    dve.wait_ge(sem["ffn_silu"], i * 4 + (FT * f + k + 1))
                    dve.wait_ge(sem["block_used"], i * 8 + (base + 2 * k + 2))
                    dve.tensor_tensor(ATF[:, i * 4 + k, :], sil[:, k % 4, :], PS[:, k % 2, T:2 * T], ALU.mult)\
                       .then_inc(sem["ffn_a"], 1)

                with dve.Fori(0, FT // 4) as i:
                    for k in range(4):
                        product(k, i)
                for k in range(FT // 4 * 4, FT):
                    product(k, 0)
                residual(lambda d: base + 3 * FT - 1)

            def ssd():
                cw = COLS["conv_w"]
                with dve.Fori(0, XBCT // 8) as i:
                    for k in range(8):
                        o = CVA[:, k % 4, :]
                        dve.wait_ge(sem["proj_evac"], i * 8 + (EV["ssd_xbc"] + k + 1 + PRIME))
                        dve.wait_ge(sem["conv_silu"], i * 8 + (k - 3 + PRIME))
                        for j in range(CONV):
                            w = cols[:, bass.ds(i * 40 + (cw + 5 * k + j), 1)]
                            src = PADS[:, k % 4, j:j + T]
                            if j == 0:
                                ins = dve.tensor_scalar(o, src, w, None, ALU.mult)
                            else:
                                dve.wait_ge(sem["conv_step"], i * 40 + (5 * k + j))
                                ins = dve.scalar_tensor_tensor(o, src, w, o, ALU.mult, ALU.add)
                            ins.then_inc(sem["conv_step"], 1)
                dve.wait_ge(sem["ssd_abs"], 1)
                dve.tensor_scalar(SF, AUX, 1.0, None, ALU.add).then_inc(sem["ssd_w"], 1)
                dve.wait_ge(sem["ssd_ln"], 1)
                t0, t1 = AR[0:64, 117, :], AR[0:64, 110, :]
                link(dve.tensor_tensor(AF, AF, AUX, ALU.mult))
                link(dve.tensor_scalar(SF, SF, -1.0, None, ALU.add))
                link(dve.tensor_scalar(t0, SF, 1e-30, None, ALU.max))
                link(dve.reciprocal(t0, t0))
                link(dve.tensor_tensor(AF, AF, t0, ALU.mult))
                link(dve.scalar_tensor_tensor(t1, SF, 0.0, AUX, ALU.is_equal, ALU.mult))
                link(dve.tensor_tensor(AF, AF, t1, ALU.add))
                link(dve.tensor_tensor(DTF, DTF, AF, ALU.add))
                link(dve.tensor_scalar(AF, DTF, eps[0:64, 2:3], -1.0, ALU.mult, ALU.mult))
                link(dve.memset(AUX, 1.0))
                link(dve.tensor_tensor_scan(SF, AUX, AF, 0.0, ALU.mult, ALU.add))
                dve.tensor_tensor(SF[32:64, :], AF[32:64, :], SF[32:64, :], ALU.subtract).then_inc(sem["ssd_dt"], 1)
                dve.wait_ge(sem["ssd_cb_sb"], SSD_GROUPS)
                dve.wait_ge(sem["ssd_xtok"], 9)

                def out_pair(p):
                    dve.wait_ge(sem["ssd_y"], 2 * p + 2)
                    dve.scalar_tensor_tensor(Y[:, p, :], XS[:, p, :], col("ssd_d", p), PS[:, 4 + p % 2, 0:T], ALU.mult, ALU.add)\
                       .then_inc(sem["ssd_yev"], 1)

                for n in range(2 * SSD_HEADS):
                    hd, u = n // 2, n % 2
                    g = hd // 4
                    main, other = (hd, 32 + hd) if u == 0 else (32 + hd, hd)
                    diag, off = slice(u * P, (u + 1) * P), slice((1 - u) * P, (2 - u) * P)
                    tmp = TMP[:, (n % 2) * P:(n % 2 + 1) * P]
                    dve.wait_ge(sem["ssd_exp"], n + 1)
                    if hd >= 2:
                        dve.wait_ge(sem["ssd_y"], hd - 1)
                    link(dve.tensor_scalar(tmp, EXB[:, n % 2, T:T + P], DTT[:, u, other:other + 1], None, ALU.mult))
                    dve.scalar_tensor_tensor(MB[:, hd % 2, u, off], EXB[:, n % 2, off], DTT[:, u, main:main + 1],
                                             CBS[:, g, u, off], ALU.mult, ALU.mult)
                    link(dve.scalar_tensor_tensor(tmp, EXB[:, n % 2, diag], DTT[:, u, main:main + 1], tmp, ALU.mult, ALU.add))
                    dve.tensor_tensor(MB[:, hd % 2, u, diag], tmp, CBS[:, g, u, diag], ALU.mult).then_inc(sem["ssd_m"], 1)
                    if n >= 6 and (n - 6) % 4 == 0:
                        out_pair((n - 6) // 4)
                out_pair(15)
                dve.wait_ge(sem["ssd_yev"], 16)
                dve.tensor_tensor(flat(Y), flat(Y), flat(Z), ALU.mult).then_inc(sem["ssd_yz"], 1)
                dve.wait_ge(sem["ssd_ysum"], 1)
                dve.tensor_scalar(flat(CM), flat(acc), 1.0 / 256, EPS, ALU.mult, ALU.add).then_inc(sem["ssd_var"], 1)
                dve.wait_ge(sem["ssd_ysqrt"], 1)
                inverse_root(flat(BM), flat(CM), flat(AR[:, 16:24, :]))
                for k in range(ZT):
                    dve.scalar_tensor_tensor(Y[:, k, :], Y[:, k, :], col("ssd_g", k), BM[:, k // 2, :], ALU.mult, ALU.mult)\
                       .then_inc(sem["ssd_yn"], 1)
                residual(lambda d: BASE["ssd_out"] + 2 * d + 1)

            def mla():
                dve.wait_ge(sem["mla_w"], 64)
                c1, c2 = 6.28125, 1.93500518798828125e-3
                c3 = 2 * np.pi - c1 - c2
                pi = float(np.float32(np.pi))
                magic = 12582912.0
                link(dve.tensor_copy(ANG[:, 1, :], ANG[:, 0, :].bitcast(I32)))
                link(dve.tensor_scalar(ANG[:, 1, :], ANG[:, 1, :], col("freq")[0:QK, :], None, ALU.mult))
                link(dve.tensor_scalar(ANG[:, 2, :], ANG[:, 1, :], 1.0 / (2 * np.pi), magic, ALU.mult, ALU.add))
                link(dve.tensor_scalar(ANG[:, 2, :], ANG[:, 2, :], -magic, None, ALU.add))
                for c in (c1, c2, c3):
                    link(dve.scalar_tensor_tensor(ANG[:, 1, :], ANG[:, 2, :], -c, ANG[:, 1, :], ALU.mult, ALU.add))
                link(dve.tensor_scalar(ANG[:, 1, :], ANG[:, 1, :], pi, -pi, ALU.min, ALU.max))
                link(dve.tensor_scalar(ANG[:, 2, :], ANG[:, 1, :], np.pi / 2, None, ALU.add))
                link(dve.tensor_scalar(ANG[:, 3, :], ANG[:, 2, :], pi, -2 * np.pi, ALU.is_gt, ALU.mult))
                link(dve.tensor_tensor(ANG[:, 2, :], ANG[:, 2, :], ANG[:, 3, :], ALU.add))
                dve.tensor_scalar(ANG[:, 2, :], ANG[:, 2, :], pi, -pi, ALU.min, ALU.max).then_inc(sem["mla_angr"], 1)
                dve.wait_ge(sem["mla_latsum"], 1)
                dve.tensor_scalar(AR[:, 20, :], PS[:, 1, 0:T], 1.0 / QL, EPS, ALU.mult, ALU.add)
                dve.tensor_scalar(AR[:, 21, :], PS[:, 1, T:2 * T], 1.0 / KVL, EPS, ALU.mult, ALU.add).then_inc(sem["mla_latvar"], 1)
                dve.wait_ge(sem["mla_latsqrt"], 1)
                inverse_root(flat(RSM[:, 0:2, :]), flat(AR[:, 20:22, :]), flat(AR[:, 22:24, :]))
                for k in range(5):
                    e = dve.scalar_tensor_tensor(AR[:, 24 + k, :], AR[:, 24 + k, :], col("q_norm", k) if k < 3 else col("kv_norm", k - 3),
                                                 RSM[:, 0 if k < 3 else 1, :], ALU.mult, ALU.mult)
                e.then_inc(sem["mla_lat"], 1)
                def mean_square(n):
                    dve.wait_ge(sem["mla_sum"], n + 1)
                    dve.tensor_scalar(flat(AR[0:QK, 20 + 2 * (n % 2):22 + 2 * (n % 2), :]), PS[0:QK, n % 2, :], 1.0 / QK, EPS,
                                      ALU.mult, ALU.add).then_inc(sem["mla_var"], 1)

                mean_square(0)
                for n in range(16):
                    q = QH if n < 8 else KH
                    two = flat(q[:, 2 * (n % 8):2 * (n % 8) + 2, :])
                    r, v, t = (flat(AR[0:QK, k + 2 * (n % 2):k + 2 + 2 * (n % 2), :]) for k in (16, 20, 24))
                    if n < 15:
                        mean_square(n + 1)
                    dve.wait_ge(sem["mla_sqrt"], n + 1)
                    inverse_root(r, v, t)
                    dve.scalar_tensor_tensor(two, two, col("q_head" if n < 8 else "k_head")[0:QK, :], r, ALU.mult, ALU.mult)\
                       .then_inc(sem["mla_qkn"], 1)
                dve.wait_ge(sem["mla_ang"], 1)
                dve.wait_ge(sem["mla_qkn"], 16)
                for n in range(16):
                    q = QH if n < 8 else KH
                    two = q[:, 2 * (n % 8):2 * (n % 8) + 2, :]
                    t = SQM[0:QK, 8 + 2 * (n % 2):10 + 2 * (n % 2), :]
                    dve.wait_ge(sem["mla_rot"], n + 1)
                    dve.tensor_tensor(t, PS[0:QK, 6 + n % 2, :].rearrange("p (a b) -> p a b", a=2), rep(SIN, 2), ALU.mult)
                    link(dve.tensor_tensor(two, two, rep(COS, 2), ALU.mult))
                    dve.tensor_tensor(two, two, t, ALU.add).then_inc(sem["mla_rope"], 1)
                for n in range(MH + 3):
                    if n < MH:
                        c = 8 * n
                        dve.wait_ge(sem["mla_logit"], n + 1)
                        link(dve.tensor_reduce(STAT[:, c:c + 2], PS[:, n % 2, :].rearrange("p (a b) -> p a b", a=2), AX.X, ALU.max))
                        dve.tensor_scalar(STAT[:, c + 2:c + 4], STAT[:, c:c + 2], -QK ** -0.5, None, ALU.mult)\
                           .then_inc(sem["mla_max"], 1)
                    if 1 <= n <= MH:
                        c = 8 * (n - 1)
                        dve.wait_ge(sem["mla_exp"], n)
                        link(dve.reciprocal(STAT[:, c + 6:c + 8], STAT[:, c + 4:c + 6]))
                        for q in range(TT):
                            p = PROB[:, (n - 1) % 2, q, :]
                            e = dve.tensor_scalar(p, p, STAT[:, c + 6 + q:c + 7 + q], None, ALU.mult)
                        e.then_inc(sem["mla_prob"], 1)
                    if n >= 3 and n % 2 == 1 and (n - 3) // 2 < 8 and n - 3 < MH:
                        p = (n - 3) // 2
                        dve.wait_ge(sem["mla_o"], 2 * p + 2)
                        dve.tensor_copy(OT[:, p, :], PS[:, 4 + p % 2, 0:T]).then_inc(sem["mla_oev"], 1)
                residual(lambda d: BASE["mla_out"] + d)

            def rwkv(l):
                shifted = 14 * l
                V4 = lambda name: col(name, 4 * l, 4)
                for n in list(range(14)) + [18] * l:
                    rows = 32 if n == 18 else P
                    z = ZPAD[0:rows, n % 4, :]
                    dif = ZDIF[0:rows, n % 4, :]
                    o = VD if n == 18 else R_[:, n, :] if n < 4 else K_[:, n - 4, :] if n < 8 else V_[:, n - 8, :] if n < 12 \
                        else (LO, GD)[n - 12]
                    mu = col("vres_mu")[0:32, :] if n == 18 else col("mu", 14 * l + n)
                    dve.wait_ge(sem["proj_evac"], EV["mix_in", l] + n + 1 + PRIME)
                    link(dve.tensor_tensor(dif, z[:, 0:T], z[:, 1:1 + T], ALU.subtract))
                    dve.scalar_tensor_tensor(o, dif, mu, z[:, 1:1 + T], ALU.mult, ALU.add).then_inc(sem["rw_shift"], 1)
                dve.wait_ge(sem["rw_shift"], shifted + 14 + l)
                dve.wait_ge(sem["rw_w"], 64 + 80 * l)
                if l == 0:
                    link(dve.tensor_copy(flat(vfirst[:, :, :]), flat(V_)))
                else:
                    dve.wait_ge(sem["rw_vresa"], 1)
                    link(dve.tensor_tensor(flat(S1), flat(vfirst[:, :, :]), flat(V_), ALU.subtract))
                    link(dve.tensor_tensor(flat(S1), flat(S1), flat(S0), ALU.mult))
                    link(dve.tensor_tensor(flat(V_), flat(V_), flat(S1), ALU.add))
                link(dve.tensor_tensor(KK, K_, bc(V4("k_k"), T), ALU.mult))
                dve.tensor_tensor(flat(S0), flat(KK), flat(KK), ALU.mult).then_inc(sem["rw_kksq"], 1)
                dve.wait_ge(sem["rw_gates"], 3 * l + 1)
                link(dve.tensor_scalar(flat(LD), flat(LD), -float(np.exp(-0.5)), None, ALU.mult))
                for m in range(4):
                    e = dve.tensor_tensor_scan(LL[:, m, :], RESTART, LD[:, m, :], 0.0, ALU.mult, ALU.add)
                link(e)
                dve.tensor_tensor(flat(LD), flat(LL), flat(LD), ALU.subtract).then_inc(sem["rw_ld"], 1)
                dve.wait_ge(sem["rw_gates"], 3 * l + 2)
                link(dve.tensor_scalar(flat(S1), flat(AA), -1.0, None, ALU.add))
                link(dve.tensor_tensor(S1, S1, bc(V4("k_a"), T), ALU.mult))
                link(dve.scalar_tensor_tensor(flat(K_), flat(S1), 1.0, flat(K_), ALU.add, ALU.mult))
                link(dve.tensor_tensor(flat(BON), flat(R_), flat(K_), ALU.mult))
                link(dve.tensor_tensor(BON, BON, bc(V4("r_k"), T), ALU.mult))
                dve.wait_ge(sem["rw_kksum"], l + 1)
                dve.tensor_scalar(flat(KTIL), PS[:, 4:6, :].rearrange("p a b -> p (a b)"), 1e-24, None, ALU.max)\
                   .then_inc(sem["rw_kkvar"], 1)
                dve.wait_ge(sem["rw_kksqrt"], l + 1)
                inverse_root(flat(S0), flat(KTIL), flat(BTIL))
                link(dve.tensor_tensor(flat(KK), flat(KK), flat(S0), ALU.mult))
                link(dve.tensor_tensor(flat(AA), flat(KK), flat(AA), ALU.mult))
                dve.wait_ge(sem["rw_exps"], l + 1)

                def m8(v):
                    return v.rearrange("p m (t c) -> p (m t) c", t=TT)

                dve.scalar_tensor_tensor(ARH[:, :, 0, :], m8(KK), -1.0, m8(LD), ALU.mult, ALU.mult)
                dve.tensor_tensor(ARH[:, :, 1, :], m8(R_), m8(EL), ALU.mult)
                dve.tensor_tensor(flat(ZT_), flat(R_), flat(EL), ALU.mult)
                dve.tensor_tensor(flat(BTIL), flat(AA), flat(EM), ALU.mult)
                dve.tensor_tensor(flat(KTIL), flat(K_), flat(EM), ALU.mult)
                link(dve.tensor_copy(LC, flat(EL).rearrange("p (c j) -> p c j", j=CH)[:, :, CH - 1]))

                def chunks(v):
                    return flat(v).rearrange("p (c j) -> p c j", j=CH)

                dve.tensor_tensor(chunks(BHAT), chunks(BTIL), bc(LC, CH), ALU.mult)
                dve.tensor_tensor(chunks(KHAT), chunks(KTIL), bc(LC, CH), ALU.mult).then_inc(sem["rw_feat"], 1)
                for n in range(4):
                    dve.wait_ge(sem["rw_tr"], 8 * l + n + 1)
                    dve.tensor_copy((ATK if n < 2 else VTK)[:, n % 2, :], PS[:, 6 + n % 2, :]).then_inc(sem["rw_trev"], 1)
                for c in range(16):
                    dve.wait_ge(sem["rw_mat"], 20 * l + 5 * (c // 4) + c % 4 + 1)
                    dve.tensor_tensor(MM[:, c, :, :].rearrange("p a b -> p (a b)"), PS[:, c % 4, :], MASK4, ALU.mult)\
                       .then_inc(sem["rw_matev"], 1)
                    if c % 4 == 3:
                        b = c // 4
                        dve.wait_ge(sem["rw_mat"], 20 * l + 5 * b + 5)
                        dve.tensor_tensor(NA[:, 4 * b:4 * b + 4, :].rearrange("p (a t) n -> p a (t n)", t=2), PS[:, 4 + 2 * (b % 2):6 + 2 * (b % 2), 0:T],
                                          rep(MASKN, 2), ALU.mult).then_inc(sem["rw_matev"], 1)
                dve.wait_ge(sem["rw_matev"], 20 * (l + 1))
                for b in range(4):
                    dve.tensor_tensor(WW[:, 4 * b:4 * b + 4, :], MM[:, 4 * b:4 * b + 4, 0, :], rep(ident, 4), ALU.add)\
                       .then_inc(sem["rw_neuev"], 1)
                dve.wait_ge(sem["rw_neuev"], 36 * l + 4)
                for st, o in enumerate((NB, NC_, WW, NA, NC_, WW, NB, WW)):
                    for b in range(4):
                        dve.wait_ge(sem["rw_neu"], 32 * l + 4 * st + b + 1)
                        src = PS[:, (4 * st + b) % 8, :].rearrange("p (a b) -> p a b", a=4)
                        to = o[:, 4 * b:4 * b + 4, :]
                        if o is WW:
                            dve.wait_ge(sem["rw_neuev"], 36 * l + 4 + 4 * (st - 1) + b + 1)
                            e = dve.tensor_tensor(to, src, to, ALU.add)
                        else:
                            e = dve.tensor_copy(to, src)
                        e.then_inc(sem["rw_neuev"], 1)
                dve.wait_ge(sem["rw_x"], l + 1)
                for tt in range(TT):
                    v = XB.rearrange("p (h t) n -> p h t n", t=TT)[:, :, tt, :]
                    dve.tensor_copy(v[:, :, 0:64], ATK[:, tt, :].rearrange("p (h k) -> p h k", h=RH))
                for b in range(2):
                    e = dve.tensor_copy(XB[:, 8 * b:8 * b + 8, 64:128], PS[:, b, :].rearrange("p (a b) -> p a b", a=8))
                e.then_inc(sem["rw_xev"], 1)
                dve.wait_ge(sem["rw_pq"], l + 1)
                for b in range(4):
                    e = dve.tensor_copy(PQ[:, 4 * b:4 * b + 4, :].rearrange("p a b -> p (a b)"), PS[:, 4 + b, :])
                e.then_inc(sem["rw_pqev"], 1)
                dve.wait_ge(sem["rw_zy"], l + 1)
                dve.tensor_tensor(flat(ZT_), flat(ZT_), PS[:, 0:2, :].rearrange("p a b -> p (a b)"), ALU.add)
                dve.tensor_copy(flat(YR), PS[:, 2:4, :].rearrange("p a b -> p (a b)")).then_inc(sem["rw_zyev"], 1)
                dve.wait_ge(sem["rw_zeroed"], l + 1)
                for a in range(2):
                    r = slice(64 * a, 64 * a + 64)
                    e = dve.tensor_tensor(GT[r, :, :, 64 * a:64 * a + 64].rearrange("p m c n -> p (m c) n"), bc(LC[r, :], 64),
                                          rep(ident[r, 64 * a:64 * a + 64], 64), ALU.mult)
                link(e)
                for n in range(4, 8):
                    dve.wait_ge(sem["rw_tr"], 8 * l + n + 1)
                    src = PS[:, 6 + n % 2, :].rearrange("p (h k) -> p h k", h=RH)
                    to = (BEO if n < 6 else KEO)[:, n % 2, :, :]
                    dve.tensor_scalar(to[:, :, 0:64], src, col("even"), None, ALU.mult)
                    dve.tensor_scalar(to[:, :, 64:128], src, col("odd"), None, ALU.mult).then_inc(sem["rw_trev"], 1)
                for m in range(4):
                    dve.wait_ge(sem["rw_gh"], 4 * l + m + 1)
                    for tt in range(TT):
                        for a in range(2):
                            r = slice(64 * a, 64 * a + 64)
                            to = GT[r, m, 8 * tt:8 * tt + 8, 64 * a:64 * a + 64].rearrange("p (q e) n -> p q e n", e=2)
                            dve.tensor_tensor(to, PS[r, 4:8, tt * P:(tt + 1) * P].rearrange("p q (e n) -> p q e n", e=2), to, ALU.add)
                        e = dve.tensor_copy(ST[:, 1 + 8 * tt:9 + 8 * tt, m, :].rearrange("p (q e) n -> p q e n", e=2),
                                            PS[:, 4:8, 256 + tt * P:256 + (tt + 1) * P].rearrange("p q (e n) -> p q e n", e=2))
                    e.then_inc(sem["rw_ghev"], 1)
                dve.wait_ge(sem["rw_ghev"], 4 * (l + 1))
                dve.memset(ST[:, 0, :, :].rearrange("p a b -> p (a b)"), 0.0).then_inc(sem["rw_state"], 1)
                for c in range(NCH - 1):
                    dve.wait_ge(sem["rw_step"], (NCH - 1) * l + c + 1)
                    s = ST[:, c + 1, :, :].rearrange("p a b -> p (a b)")
                    dve.tensor_tensor(s, PS[:, 4 + c % 2, 0:256], s, ALU.add).then_inc(sem["rw_state"], 1)
                dve.wait_ge(sem["rw_y"], l + 1)
                for a in range(2):
                    r = slice(64 * a, 64 * a + 64)
                    e = dve.tensor_tensor(flat(YR[r, :, :]), flat(YR[r, :, :]),
                                          PS[r, 6 * a:6 * a + 2, :].rearrange("p a b -> p (a b)"), ALU.add)
                e.then_inc(sem["rw_yall"], 1)
                dve.wait_ge(sem["rw_mean"], l + 1)
                link(dve.scalar_tensor_tensor(flat(YR), PS[:, 2:4, :].rearrange("p a b -> p (a b)"), -1.0 / HS, flat(YR),
                                              ALU.mult, ALU.add))
                dve.tensor_tensor(flat(S0), flat(YR), flat(YR), ALU.mult).then_inc(sem["rw_cent"], 1)
                dve.wait_ge(sem["rw_bonus"], l + 1)
                dve.tensor_tensor(flat(S1), PS[:, 4:6, :].rearrange("p a b -> p (a b)"), flat(V_), ALU.mult)
                dve.wait_ge(sem["rw_var"], l + 1)
                dve.tensor_scalar(flat(GNV), PS[:, 0:2, :].rearrange("p a b -> p (a b)"), 1.0 / HS, GN_EPS, ALU.mult, ALU.add)\
                   .then_inc(sem["rw_gnvar"], 1)
                dve.wait_ge(sem["rw_sd"], l + 1)
                inverse_root(flat(S0), flat(GNV), flat(GNT))
                link(dve.tensor_tensor(flat(YR), flat(YR), flat(S0), ALU.mult))
                link(dve.tensor_tensor(YR, YR, bc(V4("lnx_g"), T), ALU.mult))
                link(dve.tensor_tensor(YR, YR, bc(V4("lnx_b"), T), ALU.add))
                link(dve.tensor_tensor(flat(YR), flat(YR), flat(S1), ALU.add))
                dve.wait_ge(sem["rw_pl"], l + 1)
                dve.tensor_tensor(PL, PS[:, 6:8, :].rearrange("p a (b t) -> p (a b) t", b=2), bc(V4("pool_scale"), T), ALU.mult)
                dve.tensor_tensor(flat(YR), flat(YR), flat(GG), ALU.mult).then_inc(sem["rw_mix"], 1)
                residual(lambda d: BASE["mix_out", l] + d)

            def top16(groups):
                for v, s, o, ix in groups:
                    e = dve.max(o[:, 0:8], v)
                link(e)
                for v, s, o, ix in groups:
                    dve.max_index(ix[:, 0:8], o[:, 0:8], v)
                    e = dve.match_replace(s, o[:, 0:8], v, -3.0e38)
                link(e)
                for v, s, o, ix in groups:
                    e = dve.max(o[:, 8:16], s)
                link(e)
                for v, s, o, ix in groups:
                    e = dve.max_index(ix[:, 8:16], o[:, 8:16], s)
                link(e)

            def peer(l):
                dve.wait_ge(sem["pe_scev"], 8 * (l + 1))
                IU, SU = IDX.bitcast(U32), SEL.bitcast(U32)
                top16([(SC[:, t, n, :], SC2[:, t, n, :], VAL[:, t, n, :], IU[:, t, n, :]) for t in range(TT) for n in range(16)])
                link(dve.tensor_copy(IDXF.rearrange("p t n k -> p (t n k)"), IU.rearrange("p t n k -> p (t n k)")))
                vp = VAL.rearrange("p t (n h) k -> p t n h k", h=2)
                for t in range(TT):
                    e = dve.tensor_tensor(CAND[:, t, :, :].rearrange("p n (a b) -> p n a b", a=16),
                                          vp[:, t, :, 0, :].rearrange("p n (k o) -> p n k o", o=1).to_broadcast([P, PH, 16, 16]),
                                          vp[:, t, :, 1:2, :].to_broadcast([P, PH, 16, 16]), ALU.add)
                link(e)
                top16([(CAND[:, t, n, :], CAND2[:, t, n, :], TOP[:, t, n, :], SU[:, t, n, :]) for t in range(TT) for n in range(PH)])

                def f1(v):
                    return v.rearrange("p t n k -> p (t n k)")

                sel = SELI.bitcast(U32)
                link(dve.tensor_scalar(sel, f1(SU), 4, None, ALU.logical_shift_right))
                link(dve.tensor_copy(f1(HI), sel))
                link(dve.tensor_scalar(sel, f1(SU), 15, None, ALU.bitwise_and))
                link(dve.tensor_copy(f1(LOW), sel))
                fp = IDXF.rearrange("p t (n h) k -> p t n h k", h=2)
                for k, which in enumerate((HI, LOW)):
                    for t in range(TT):
                        e3 = EQ.rearrange("p (n a) -> p n a", a=16)
                        link(dve.tensor_tensor(e3, bc(which[:, t, :, :].rearrange("p n k -> p (n k)"), 16), rep(iota[:, 0:16], P),
                                               ALU.is_equal))
                        e4 = EQ.rearrange("p (n k a) -> p n k a", n=PH, a=16)
                        link(dve.tensor_tensor(e4, e4, fp[:, t, :, k:k + 1, :].to_broadcast([P, PH, 16, 16]), ALU.mult))
                        link(dve.tensor_reduce(IJT[:, k, t, :], e3, AX.X, ALU.add))
                tf = TOP.rearrange("p t n k -> p (t n) k")
                sm = SMX.rearrange("p (n k) -> p n k", k=16)
                dve.tensor_tensor(sm, tf, tf[:, :, 0:1].to_broadcast([P, 16, 16]), ALU.subtract).then_inc(sem["pe_top"], 1)
                dve.wait_ge(sem["pe_exp"], l + 1)
                tot = SELI[:, 0:16]
                link(dve.tensor_reduce(tot, sm, AX.X, ALU.add))
                link(dve.reciprocal(tot, tot))
                dve.tensor_tensor(IJT[:, 2, :, :].rearrange("p t (n k) -> p (t n) k", k=16), sm, bc(tot, 16), ALU.mult)\
                   .then_inc(sem["pe_sm"], 1)
                dve.wait_ge(sem["pe_ijg"], l + 1)
                with dve.Fori(0, T // 8) as i:
                    for k in range(2):
                        dve.wait_ge(sem["pe_w"], i * 2 + (64 * l + k - 1 + 2))
                        for j in range(4):
                            t = bass.ds(i * 8 + (4 * k + j), 1)
                            dve.tensor_scalar(OHI[:, k, j, :], iota, ijg[:, 0, t], ijg[:, 2, t], ALU.is_equal, ALU.mult)
                            e = dve.tensor_scalar(OHJ[:, k, j, :], iota, ijg[:, 1, t], None, ALU.is_equal)
                        e.then_inc(sem["pe_oh"], 1)
                with dve.Fori(0, NK // 4) as i:
                    for k in range(4):
                        dve.wait_ge(sem["pe_gelu"], i * 4 + (NK * l + k + 1 + PRIME))
                        dve.tensor_tensor(gat[:, k, :], sil[:, k, :], WALL[:, :, i * 4 + k], ALU.mult).then_inc(sem["pe_gated"], 1)
                residual(lambda d: BASE["uv", l] + 2 * NK - 1)

            dve.wait_ge(sem["inits"], 4)
            dve.wait_ge(sem["loads"], 48)
            for s in range(NSUB):
                mod_columns(s)
                normed(s)
                if s in (0, 2, 3, 5):
                    ffn((0, 2, 3, 5).index(s))
                elif s == 1:
                    ssd()
                elif s == 4:
                    mla()
                elif s % 2 == 0:
                    rwkv((s - 6) // 2)
                else:
                    peer((s - 7) // 2)
            normed(NSUB)

        @block.gpsimd
        def _(pool):
            chain = [0]

            def link(ins):
                chain[0] += 1
                ins.then_inc(sem["pool_chain"], 1)
                pool.wait_ge(sem["pool_chain"], chain[0])

            pool.memset(zeros[:, :], 0.0).then_inc(sem["inits"], 1)
            pool.memset(AR[:, 101:106, :].rearrange("p a b -> p (a b)"), 0.0).then_inc(sem["inits"], 1)
            pool.dma_start(CMASK, const("causal")).then_inc(sem["aux_loads"], 16)
            pool.wait_ge(sem["aux_loads"], 16)
            pool.tensor_copy(CMB, CMASK).then_inc(sem["inits"], 1)
            pool.wait_ge(sem["loads"], 48)
            pool.tensor_copy(IDB[:, :], ident).then_inc(sem["inits"], 1)
            pool.wait_ge(sem["x_upd"], 16)
            pool.dma_start(WUQ, wuq_d).then_inc(sem["mla_w"], 16)
            pool.dma_start(WUKV, wukv_d).then_inc(sem["mla_w"], 16)
            pool.dma_start(RPM, const("rope")[0:QK, :]).then_inc(sem["mla_w"], 16)
            pool.dma_start(ANG[:, 0, :].bitcast(I32), pos_d[0:1, :].to_broadcast([QK, T])).then_inc(sem["mla_w"], 16)
            pool.wait_ge(sem["proj_evac"], EV["mla_in"] + 6 + PRIME)
            pool.tensor_copy(KH[64:96, :, :], rep(KPE[64:96, :], MH)).then_inc(sem["mla_kpe"], 1)
            for l in range(2):
                pool.wait_ge(sem["x_upd"], 8 * (6 + 2 * l))
                pool.dma_start(RC, consts_d[:, CONSTS["mask4"][0]:CONSTS["mask4"][0] + RCN]).then_inc(sem["rw_w"], 16)
                pool.dma_start(WUP, lora_d[l]).then_inc(sem["rw_w"], 16)
                pool.dma_start(GUP, gup_d[l]).then_inc(sem["rw_w"], 16)
                pool.dma_start(POOLW, pool_d[l]).then_inc(sem["rw_w"], 16)
                if l == 1:
                    pool.dma_start(VUP[0:32, :], vup_d).then_inc(sem["rw_w"], 16)
                pool.memset(ZPAD[:, :, 0:1], 0.0).then_inc(sem["rw_zpad"], 1)
                pool.wait_ge(sem["rw_w"], 64 + 80 * l)
                pool.wait_ge(sem["proj_evac"], EV["mix_in", l] + 18 + PRIME)
                for j in range(4):
                    cur = PL[:, j, :]
                    for k in range(j + 1):
                        w, nxt = 1 << k, ijg[:, k % 2, :]
                        pool.tensor_copy(nxt[:, 0:w], cur[:, 0:w])
                        link(pool.tensor_tensor(nxt[:, w:T], cur[:, w:T], cur[:, 0:T - w], ALU.add))
                        cur = nxt
                    link(pool.tensor_tensor(cur, cur, RECIP[:, j * T:(j + 1) * T], ALU.mult))
                    link(pool.tensor_tensor(PL[:, j, :], cur, PL[:, j, :], ALU.subtract))
                pool.sem_inc(sem["rw_pool"], 1)
                pool.wait_ge(sem["rw_zy"], l + 1)
                link(pool.memset(GT[0:64, :, :, 64:128].rearrange("p m c n -> p (m c) n"), 0.0))
                pool.memset(GT[64:128, :, :, 0:64].rearrange("p m c n -> p (m c) n"), 0.0).then_inc(sem["rw_zeroed"], 1)
                pool.wait_ge(sem["x_upd"], 8 * (7 + 2 * l))
                pool.dma_start(KEYS, keys_d[l]).then_inc(sem["pe_keys"], 16)


def _columns(v, n):
    return np.ascontiguousarray(v.reshape(n, P).T)


def _square(v):
    out = np.zeros((P, 1), np.float32)
    out[:v.size, 0] = v.reshape(-1)
    return out


def _blocks(w):
    k, n = w.shape
    m = -(-n // P)
    if m * P != n:
        w = np.concatenate([w, np.zeros((k, m * P - n), w.dtype)], axis=1)
    return w.reshape(k // 1024, 8, P, m, P).transpose(3, 0, 2, 1, 4).reshape(-1, P, 1024)


def _constants():
    c = np.zeros((P, NCONST), np.float32)
    i = np.arange(P)

    def put(name, v):
        s, n = CONSTS[name]
        c[:v.shape[0], s:s + n] = v

    put("ident", np.eye(P, dtype=np.float32))
    put("ones", np.ones((P, P), np.float32))
    put("iota", np.broadcast_to(i.astype(np.float32), (P, P)))
    put("half", (i[:, None] // HS == i[None, :] // HS).astype(np.float32))
    same = i[:, None] // CH == i[None, :] // CH
    strict = (same & (i[:, None] < i[None, :])).astype(np.float32)
    incl = (same & (i[:, None] <= i[None, :])).astype(np.float32)
    put("mask4", np.concatenate([strict, incl, strict, incl], axis=1))
    put("maskn", np.concatenate([strict.T, strict.T], axis=1))
    put("restart", np.broadcast_to((np.arange(T) % CH != 0).astype(np.float32), (P, T)))
    rope = np.zeros((QK, QK), np.float32)
    for j in range(ROPE // 2):
        rope[NOPE + ROPE // 2 + j, NOPE + j] = -1.0
        rope[NOPE + j, NOPE + ROPE // 2 + j] = 1.0
    put("rope", rope)
    put("causal", np.concatenate([np.where(i[:, None] <= i[None, :], 0, NEG), np.where(i[:, None] >= i[None, :], 0, NEG)],
                                 axis=1).astype(np.float32))
    pos = np.arange(1, T + 1, dtype=np.float32)
    put("recip", np.broadcast_to(np.concatenate([1.0 / np.minimum(pos, w) for w in (2, 4, 8, 16)]).astype(np.float32), (P, 4 * T)))
    return c


def kernel(**inputs):
    import concourse.bacc as bacc
    from concourse.bass_utils import run_bass_kernel_spmd as run

    a = {k: np.asarray(v) for k, v in inputs.items()}
    stream = np.empty((NBLOCKS, P, 1024), np.float32)

    def put(name, blocks):
        stream[BASE[name]:BASE[name] + len(blocks)] = blocks

    for i in range(2):
        for s in range(3):
            put(("mod", 3 * i + s), _blocks(a["w_mod"][i][:, s * 3072:(s + 1) * 3072]))
        for s in range(2):
            b = BASE["ffn", 2 * i + s]
            stream[b:b + 2 * FT:2] = _blocks(a["ffn_w_gate"][i, s])
            stream[b + 1:b + 2 * FT:2] = _blocks(a["ffn_w_up"][i, s])
            stream[b + 2 * FT:b + 3 * FT] = a["ffn_w_down"][i, s].reshape(FT, P, 1024)
    put("ssd_in", _blocks(a["ssd_w_in"][0]))
    put("ssd_out", _blocks(a["ssd_w_out"][0]))
    put("mla_in", _blocks(a["mla_w_in"][0]))
    put("mla_out", _blocks(a["mla_w_out"][0]))
    for l in range(2):
        for s in range(2):
            put(("mod", 6 + 2 * l + s), _blocks(a["ada_w_2"][l][:, s * 3072:(s + 1) * 3072]))
        w = a["w_in_2"][l]
        put(("mix_in", l), _blocks(w if l == 0 else np.concatenate([w, a["vres_down_2"][0]], axis=1)))
        put(("mix_out", l), _blocks(a["w_out_2"][l]))
        put(("peer_q", l), _blocks(a["peer_q_2"][l]))
        b = BASE["uv", l]
        u = a["peer_u_2"][l].reshape(NK, NK, 8, P).transpose(1, 3, 2, 0).reshape(NK, P, 1024)
        v = a["peer_v_2"][l].reshape(NK, NK, D).transpose(1, 0, 2)
        stream[b] = u[0]
        stream[b + 1:b + 2 * NK - 1:2] = u[1:]
        stream[b + 2:b + 2 * NK - 1:2] = v[:-1]
        stream[b + 2 * NK - 1] = v[-1]

    freq = np.zeros(QK, np.float32)
    inv = (10000.0 ** (-np.arange(0, ROPE, 2, dtype=np.float32) / ROPE)).astype(np.float32)
    freq[NOPE:] = np.concatenate([inv, inv])
    parity = ((np.arange(P) // CH) % 2).astype(np.float32)
    parts = {
        "c": _columns(a["c"], 8), "c_2": _columns(a["c_2"], 8), "norm_g": _columns(a["norm_g"], 48),
        "b_mod": _columns(a["b_mod"], 144), "ada_b": _columns(a["ada_b_2"], 96), "ln1": _columns(a["ln1_g_2"], 16),
        "ln2": _columns(a["ln2_g_2"], 16), "lnf": _columns(a["lnf_g_2"], 8), "dt_bias": _square(a["ssd_dt_bias"]),
        "a_log": _square(a["ssd_a_log"]),
        "conv_w": a["ssd_conv_w"][0].reshape(CONV, XBCT, P).transpose(2, 1, 0).reshape(P, XBCT * CONV),
        "conv_b": _columns(a["ssd_conv_b"], XBCT), "ssd_d": _columns(np.repeat(a["ssd_d"][0], 64), ZT),
        "ssd_g": _columns(a["ssd_norm_g"], ZT), "q_norm": _columns(a["mla_q_norm_g"], 3),
        "kv_norm": _columns(a["mla_kv_norm_g"], 2), "q_head": _square(a["mla_q_head_g"]), "k_head": _square(a["mla_k_head_g"]),
        "mu": _columns(a["mu_shift_2"], 28), "w0": _columns(a["w0_2"], 8), "a0": _columns(a["a0_2"], 8),
        "k_k": _columns(a["k_k_2"], 8), "k_a": _columns(a["k_a_2"], 8), "r_k": _columns(a["r_k_2"], 8),
        "lnx_g": _columns(a["lnx_g_2"], 8), "lnx_b": _columns(a["lnx_b_2"], 8), "pool_scale": _columns(a["pool_scale_2"], 8),
        "vres_mu": _square(a["vres_mu_2"]), "vres_v0": _columns(a["vres_v0_2"], 4), "freq": _square(freq),
        "even": 1.0 - parity[:, None], "odd": parity[:, None],
    }
    cols = np.concatenate([parts[n] for n in COLS], axis=1).astype(np.float32)
    ukv = a["mla_w_ukv"][0].reshape(2, P, MH, 2, 64).transpose(1, 0, 3, 2, 4).reshape(P, 2, 2048)
    arrays = {
        "stream": stream, "columns": cols, "constants": _constants(),
        "x_in": a["x"][0].reshape(T, DT, P).transpose(2, 1, 0),
        "positions": a["positions"],
        "w_uq": a["mla_w_uq"][0].reshape(3, P, MH * QK).transpose(1, 0, 2),
        "w_ukv": ukv,
        "keys": a["peer_keys_2"].reshape(2, 16, NK, P).transpose(0, 3, 1, 2),
        "pool_w": a["pool_w_2"].transpose(0, 2, 1, 3).reshape(2, P, 512),
        "lora_up": np.concatenate([a["w_up_2"], a["a_up_2"]], axis=1),
        "gate_up": a["g_up_2"], "vres_up": a["vres_up_2"][0],
    }
    arrays = {k: np.ascontiguousarray(v) for k, v in arrays.items()}
    nc = bacc.Bacc("TRN2", target_bir_lowering=False, num_devices=1)
    aps = [nc.dram_tensor(k, v.shape, mybir.dt.from_np(v.dtype), kind="ExternalInput").ap() for k, v in arrays.items()]
    out = nc.dram_tensor("out", (P, DT, T), F32, kind="ExternalOutput").ap()
    build(nc, *aps, out)
    r = run(nc, [arrays], core_ids=[0])
    return np.ascontiguousarray(r.results[0]["out"].transpose(2, 1, 0).reshape(1, T, D))
```

```python
from contextlib import ExitStack

import numpy as np

import concourse.bass as bass
from concourse import mybir

F32 = mybir.dt.float32
F32R = mybir.dt.float32r
BF16 = mybir.dt.bfloat16
I32 = mybir.dt.int32
U32 = mybir.dt.uint32
ALU = mybir.AluOpType
ACT = mybir.ActivationFunctionType
AX = mybir.AxisListType

P = 128
D = 1024
T = 256
DT = D // P
TT = T // P
FF = 2816
FT = FF // P
EPS = 1e-6

SSD_HEADS, SSD_GROUPS, DIN = 32, 8, 2048
ZT, XBCT = DIN // P, 4096 // P
CONV = 5

MH, NOPE, ROPE, QK, MV = 16, 64, 32, 96, 64
QL, KVL = 384, 256

RW, HS = 512, 64
RH = RW // HS
CH = 16
NCH = T // CH
GN_EPS = 64e-5

PH, NK, TOPK = 8, 128, 16
NSUB = 10

RING = 4
STEP = 8
WS = 4
MOD_GROUPS = {0: (1, 2), 2: (3, 4, 5), 3: (6, 7), 5: (8, 9)}
MOD_RING = 4
NEG = -1e30


def stream_plan():
    base, n = {}, 0

    def add(name, count):
        nonlocal n
        base[name] = n
        n += count

    add("mod0", 24)
    for i in range(2):
        add(("ffn", 2 * i), 3 * FT)
        if i == 0:
            add("ssd_in", ZT + XBCT + 1)
            add("ssd_out", 2 * DT)
        else:
            add("mla_in", 6)
            add("mla_out", DT)
        add(("ffn", 2 * i + 1), 3 * FT)
    for l in range(2):
        add(("mix_in", l), 18 + l)
        add(("mix_out", l), DT)
        add(("peer_q", l), 2 * PH)
        add(("uv", l), 2 * NK)
    return base, n


BASE, NBLOCKS = stream_plan()

SPLIT = {**{("ffn", f): (3 * FT * f, FT * f) for f in range(4)},
         **{("uv", l): (12 * FT + 2 * NK * l, 4 * FT + NK * l) for l in range(2)}}

COLS = {}


def _cols():
    n = 0
    for name, k in [
        ("c", 8), ("c_2", 8), ("norm_g", 48), ("b_mod", 144), ("ada_b", 96), ("ln1", 16), ("ln2", 16), ("lnf", 8),
        ("dt_bias", 1), ("a_log", 1), ("conv_w", XBCT * CONV), ("conv_b", XBCT), ("ssd_d", ZT), ("ssd_g", ZT),
        ("q_norm", 3), ("kv_norm", 2), ("q_head", 1), ("k_head", 1),
        ("mu", 28), ("w0", 8), ("a0", 8), ("k_k", 8), ("k_a", 8), ("r_k", 8), ("lnx_g", 8), ("lnx_b", 8),
        ("pool_scale", 8), ("vres_mu", 1), ("vres_v0", 4), ("freq", 1), ("even", 1), ("odd", 1),
    ]:
        COLS[name] = n
        n += k
    return n


NCOLS = _cols()

CONSTS = {}


def _consts():
    n = 0
    for name, k in [("ident", P), ("ones", P), ("iota", P), ("half", P), ("mask4", 4 * P), ("maskn", 2 * P),
                    ("restart", T), ("recip", 4 * T), ("rope", QK), ("causal", 2 * P)]:
        CONSTS[name] = (n, k)
        n += k
    return n


NCONST = _consts()
KEPT = 4 * P

SIGNALS = (
    "block_used", "loads", "aux_loads", "inits", "cond_ready", "mod_acc", "mod_sum", "mod_cols",
    "norm_sq", "norm_sum", "norm_var", "ssd_var", "mla_latvar", "mla_var", "rw_kkvar", "rw_gnvar", "norm_sqrt", "norm_scaled", "h_ready", "x_upd",
    "ffn_silu", "ffn_a", "proj_evac", "act_chain", "dve_chain", "pool_chain", "out_done", "out_ready",
    "conv_step", "conv_silu", "ssd_pads", "ssd_abs", "ssd_w", "ssd_ln", "ssd_dt", "ssd_tr", "ssd_xtok", "ssd_cb", "ssd_cb_sb", "ssd_seg",
    "ssd_exp", "ssd_m", "ssd_y", "ssd_yev", "ssd_yz", "ssd_ysq", "ssd_ysum", "ssd_ysqrt", "ssd_yn",
    "mla_w", "mla_latsq", "mla_latsum", "mla_latsqrt", "mla_lat", "mla_proj", "mla_pev", "mla_kpe", "mla_sq",
    "mla_sum", "mla_sqrt", "mla_qkn", "mla_rot", "mla_rope", "mla_angr", "mla_ang", "mla_logit", "mla_max", "mla_exp",
    "mla_prob", "mla_pt", "mla_pts", "mla_o", "mla_oev",
    "rw_w", "rw_shift", "rw_lo", "rw_lora", "rw_gates", "rw_vres", "rw_vresa", "rw_kksq", "rw_kksum", "rw_kksqrt",
    "rw_ld", "rw_exps", "rw_feat", "rw_zeroed", "rw_tr", "rw_trev", "rw_mat", "rw_matev", "rw_neu", "rw_neuev",
    "rw_x", "rw_xev", "rw_pq", "rw_pqev", "rw_gh", "rw_ghev", "rw_zy", "rw_zyev", "rw_step", "rw_state",
    "rw_y", "rw_yall", "rw_mean", "rw_cent", "rw_zpad", "rw_var", "rw_sd", "rw_bonus", "rw_bon", "rw_mix", "rw_pool", "rw_pl",
    "pe_keys", "pe_q", "pe_sc", "pe_scev", "pe_top", "pe_exp", "pe_sm", "pe_tr", "pe_ijg",
    "pe_oh", "pe_w", "pe_wev", "pe_gelu", "pe_gated",
    "uv_h_hi", "h_lo", "block_hi", "block_lo", "gate_hi", "gate_lo",
)


def build(nc, stream, mods, cols_d, consts_d, x_d, pos_d, wuq_d, wukv_d, keys_d, pool_d, lora_d, gup_d, vup_d, out_d):
    with ExitStack() as ctx:
        def sb(name, shape, dt=F32):
            return ctx.enter_context(nc.sbuf_tensor(name, shape, dt))

        sem = {n: ctx.enter_context(nc.semaphore(n)) for n in SIGNALS}
        slot_full = [ctx.enter_context(nc.semaphore(f"slot_full_{i}")) for i in range(RING)]

        mod_full = [ctx.enter_context(nc.semaphore(f"mod_full_{i}")) for i in range(MOD_RING)]

        def sb_twice(name, shape, parts):
            with nc.sbuf_tensor(name, shape, F32) as whole:
                pass
            return whole, [sb(f"{name}_{i}", p, dt) for i, (p, dt) in enumerate(parts)]

        ring, (ring_lo,) = sb_twice("ring", [P, RING, 1024], [([P, RING, 1024], F32R)])
        whi = sb("weights_hi", [P, WS, 1024], F32R)
        AR = sb("arena", [P, 128, 256])
        x = sb("x", [P, DT, T])
        h, (h_lo,) = sb_twice("h", [P, DT, T], [([P, DT, T], F32R)])
        h_hi = sb("h_hi", [P, DT, T], F32R)
        vfirst = sb("vfirst", [P, 4, T])
        cols = sb("cols", [P, NCOLS])
        kept = sb("kept", [P, KEPT])
        ident, ones, iota, half = (kept[:, i * P:(i + 1) * P] for i in range(4))
        zeros = sb("zeros", [P, P], BF16)
        eps = sb("eps", [P, 4])
        cond = sb("cond", [P, 16])
        modc = sb("modc", [P, NSUB, 24])
        rs, rv = (sb(n_, [P, T]) for n_ in ("rs", "rv"))
        work, (_, gat_lo) = sb_twice("work", [P, 2048], [([P, 1024], F32), ([P, 4, T], F32R)])
        ijg, (gat_hi,) = sb_twice("ijg", [P, 3, T], [([P, 3, T], F32R)])
        PS = ctx.enter_context(nc.psum_tensor("psum", [P, 8, 512], F32))
        acc = PS[:, 4:8, :].rearrange("p b (s t) -> p (b s) t", s=2)
        sil = work[:, 0:1024].rearrange("p (b t) -> p b t", b=4)
        gat = work[:, 1024:2048].rearrange("p (b t) -> p b t", b=4)
        SQ = AR[:, 120:128, :]
        ATF = AR[:, 0:FT, :]

        def col(name, k=0, n=1):
            return cols[:, COLS[name] + k:COLS[name] + k + n]

        def const(name):
            s, n = CONSTS[name]
            return consts_d[:, s:s + n]

        def flat(v):
            return v.rearrange("p a b -> p (a b)")

        def bc(v, n):
            return v.rearrange("p (a b) -> p a b", b=1).to_broadcast([v.shape[0], v.shape[1], n])

        def rep(v, n):
            return v[:, None, :].to_broadcast([v.shape[0], n, v.shape[1]])

        EV, n_ev = {}, 0
        for name, count in (("ssd_z", ZT), ("ssd_xbc", XBCT), ("ssd_dt", 1), ("mla_in", 6), (("mix_in", 0), 18),
                            (("peer_q", 0), 16), (("mix_in", 1), 19), (("peer_q", 1), 16)):
            EV[name] = n_ev
            n_ev += count
        PRIME = 4

        MODSUM = AR[:, 66:102, :].rearrange("p a b -> p (a b)").rearrange("p (n k) -> p n k", n=9)
        MODRING = [AR[:, a:a + 4, :].rearrange("p a b -> p (a b)") for a in (22, 26, 106, 110)]
        Z, XS, BM, CM = AR[:, 0:16, :], AR[:, 16:32, :], AR[:, 32:40, :], AR[:, 40:48, :]
        XTOK = AR[:, 48:64, :].rearrange("p (a b) t -> p a (b t)", a=TT)
        Y = AR[:, 64:80, :]
        DTF, AF, SF, AUX = (AR[0:64, 80 + i, :] for i in range(4))
        NST = AR[:, 84, 0:128].rearrange("p (a b) -> p a b", a=TT)
        DTT = AR[:, 84, 128:256].rearrange("p (a b) -> p a b", a=TT)
        CBS = AR[:, 85:101, :].rearrange("p (g u) t -> p g u t", u=TT)
        PADS = AR[:, 101:106, :].rearrange("p a b -> p (a b)")[:, 0:4 * 260].rearrange("p (a b) -> p a b", a=4)
        CVA = AR[:, 106:110, :]
        EXB = AR[:, 110:113, :].rearrange("p a b -> p (a b)").rearrange("p (a b) -> p a b", a=2)
        MB = AR[:, 113:117, :].rearrange("p (c u) t -> p c u t", u=TT)
        TMP = AR[:, 117, :]
        CMASK = AR[:, 118, :]
        CMB = AR[:, 119, 0:128].bitcast(BF16)
        IDB = ctx.enter_context(nc.sbuf_tensor("ident_bf16", [P, P], BF16))
        QLAT, KVLAT, KPE = AR[:, 24:27, :], AR[:, 27:29, :], AR[:, 29, :]
        WUQ = AR[:, 32:50, :].rearrange("p a b -> p (a b)").rearrange("p (k n) -> p k n", k=3)
        WUKV = AR[:, 50:66, :].rearrange("p a b -> p (a b)").rearrange("p (k n) -> p k n", k=2)
        QH, KH = AR[0:QK, 66:82, :], AR[0:QK, 82:98, :]
        VTOK = AR[:, 98:106, :].rearrange("p (a b) t -> p a (b t)", a=TT)
        OT = AR[:, 106:114, :]
        COS, SIN = AR[0:QK, 114, :], AR[0:QK, 115, :]
        ANG = AR[0:QK, 116:120, :]
        SQM = AR[:, 0:16, :]
        PROB = AR[:, 0:4, :].rearrange("p (b q) t -> p b q t", b=2)
        PT = AR[:, 4:8, :].rearrange("p (b q) t -> p b q t", b=2)
        RPM = AR[0:QK, 31, 0:QK]
        STAT = AR[:, 30, :]
        RSM = AR[:, 16:20, :]
        def words(a, b):
            return AR[:, a:b, :].rearrange("p a b -> p (a b)")

        V_, BON, GG, PL = AR[:, 0:4, :], AR[:, 4:8, :], AR[:, 8:12, :], AR[:, 12:16, :]
        VTK = words(16, 20).rearrange("p (t n) -> p t n", t=TT)
        RCN = sum(CONSTS[n_][1] for n_ in ("mask4", "maskn", "restart", "recip"))
        RC = words(20, 28)
        rc_at = {}
        at = 0
        for name_ in ("mask4", "maskn", "restart", "recip"):
            rc_at[name_] = (at, at + CONSTS[name_][1])
            at += CONSTS[name_][1]
        MASK4, MASKN, RESTART, RECIP = (RC[:, a:b] for a, b in rc_at.values())
        WUP, GUP, VUP, POOLW = words(28, 30), words(30, 32), words(32, 34), words(34, 36)
        ST = AR[:, 36:53, :].rearrange("p c (m k) -> p c m k", m=4)
        LO, GD, VD = AR[:, 36, :], AR[:, 37, :], AR[0:32, 38, :]
        ZT_, YR = AR[:, 53:57, :], AR[:, 57:61, :]
        ARH = words(61, 69).rearrange("p (n k c) -> p n k c", n=8, k=2)
        BTIL, KTIL = AR[:, 69:73, :], AR[:, 73:77, :]
        KK, AA, LL, LD, EL, EM, R_, K_ = (AR[:, 77 + 4 * i:81 + 4 * i, :] for i in range(8))
        MM = words(77, 109).rearrange("p (c k n) -> p c k n", c=16, k=4)
        GT = words(77, 109).rearrange("p (m c n) -> p m c n", m=4, c=NCH)
        NA = words(109, 117).rearrange("p (c n) -> p c n", c=16)
        NB, NC_ = (words(61 + 8 * i, 69 + 8 * i).rearrange("p (c n) -> p c n", c=16) for i in range(2))
        WW = words(117, 125).rearrange("p (c n) -> p c n", c=16)
        XB, PQ = NB, NC_
        BEO = words(109, 117).rearrange("p (t h n) -> p t h n", t=TT, h=RH)
        KEO = words(117, 125).rearrange("p (t h n) -> p t h n", t=TT, h=RH)
        BHAT, KHAT = h[:, 0:4, :], h[:, 4:8, :]
        S0, S1 = (work[:, 1024 * i:1024 * (i + 1)].rearrange("p (m t) -> p m t", m=4) for i in range(2))
        ATK = work[:, 0:1024].rearrange("p (t n) -> p t n", t=TT)
        LC = rs[:, 0:64]
        ZPAD = words(109, 114)[:, 0:4 * 257].rearrange("p (a b) -> p a b", a=4)
        ZDIF = AR[:, 114:118, :]
        GNV, GNT = AR[:, 77:81, :], AR[:, 81:85, :]
        QP = AR[:, 0:16, :]
        KEYS = words(16, 24).rearrange("p (n k) -> p n k", n=16)
        SC, SC2 = (words(24 + 16 * i, 40 + 16 * i).rearrange("p (t n k) -> p t n k", t=TT, n=16) for i in range(2))
        VAL, IDX, IDXF = (words(56 + 2 * i, 58 + 2 * i).rearrange("p (t n k) -> p t n k", t=TT, n=16) for i in range(3))
        CAND, CAND2 = (words(62 + 16 * i, 78 + 16 * i).rearrange("p (t n k) -> p t n k", t=TT, n=PH) for i in range(2))
        TOP, SEL, HI, LOW = (words(94 + i, 95 + i).rearrange("p (t n k) -> p t n k", t=TT, n=PH) for i in range(4))
        EQ = words(98, 106)
        IJT = words(106, 109).rearrange("p (k t n) -> p k t n", k=3, t=TT)
        SELI = words(109, 110)
        SMX = words(110, 111)
        WALL = words(0, 128).rearrange("p (t j) -> p t j", t=T)
        OHI, OHJ = (work[:, 1024 * i:1024 * (i + 1)].rearrange("p (b t n) -> p b t n", b=2, t=4) for i in range(2))

        block = ctx.enter_context(nc.Block())

        @block.sync
        def _(sp):
            sp.dma_start(cols[:, :], cols_d).then_inc(sem["loads"], 16)
            sp.dma_start(x[:, :, :], x_d).then_inc(sem["loads"], 16)
            sp.dma_start(kept[:, :], consts_d[:, 0:KEPT]).then_inc(sem["loads"], 16)
            for s in range(RING):
                sp.dma_start(ring[:, s, :], stream[s]).then_inc(slot_full[s], 16)
            full = (NBLOCKS - RING) // STEP
            with sp.Fori(0, full) as i:
                for s in range(STEP):
                    sp.wait_ge(sem["block_used"], i * STEP + (s + 1))
                    sp.dma_start(ring[:, s % RING, :], stream[i * STEP + (s + RING)]).then_inc(slot_full[s % RING], 16)
            for n in range(full * STEP + RING, NBLOCKS):
                sp.wait_ge(sem["block_used"], n - RING + 1)
                sp.dma_start(ring[:, n % RING, :], stream[n]).then_inc(slot_full[n % RING], 16)
            sp.wait_ge(sem["out_ready"], DT)
            sp.dma_start(out_d, h[:, :, :]).then_inc(sem["out_done"], 16)
            sp.wait_ge(sem["out_done"], 16)

        @block.tensor
        def _(pe):
            def arrived(n, i=0):
                pe.wait_ge(slot_full[n % RING], i * (STEP // RING * 16) + (n // RING + 1) * 16)
                return ring[:, n % RING, :].rearrange("p (k c) -> p k c", k=8)

            def mod_columns(s, j):
                if s == 0:
                    pe.wait_ge(sem["block_used"], 24)
                else:
                    pe.wait_ge(sem["mod_acc"], 24 * s)
                if s:
                    pe.wait_ge(sem["mod_cols"], s)
                for m in range(24):
                    mm = pe.matmul(PS[:, 3, j * 24 + m:j * 24 + m + 1], MODSUM[:, 3 * j + m // 8, m % 8 * P:(m % 8 + 1) * P],
                                   ones[:, 0:1], start=True, stop=True)
                mm.then_inc(sem["mod_sum"], 1)

            def norm_sum(s):
                for d in range(DT):
                    pe.wait_ge(sem["norm_sq"], 8 * s + d + 1)
                    mm = pe.matmul(PS[:, 2, 0:T], ones, SQ[:, d, :], start=(d == 0), stop=(d == DT - 1))
                mm.then_inc(sem["norm_sum"], 1)

            def h_in(s):
                pe.wait_ge(sem["h_ready"], 8 * s + 8)

            def open_acc():
                for b in range(4):
                    pe.matmul(PS[:, 4 + b, :], zeros[:, :], rep(zeros[:, :], 4), start=True, stop=False, skip_group_check=True)

            def parts(section, n, i):
                pe.wait_ge(sem["block_lo"], i * 8 + (SPLIT[section][0] + n + 1))
                return (whi[:, n % WS, :].rearrange("p (k c) -> p k c", k=8),
                        ring_lo[:, (BASE[section] + n) % RING, :].rearrange("p (k c) -> p k c", k=8))

            def columns_in_parts(out, w, wl):
                for d in range(DT):
                    for p, (lhs, rhs) in enumerate(((w, h_hi), (w, h_lo), (wl, h_hi))):
                        mm = pe.matmul(out, lhs[:, d, :], rhs[:, d, :], start=(d == 0 and p == 0), stop=(d == DT - 1 and p == 2))
                mm.then_inc(sem["block_used"], 1)

            def rows_in_parts(w, wl, hi, lo):
                for d in range(DT):
                    for lhs, rhs in ((w, hi), (w, lo), (wl, hi)):
                        mm = pe.matmul(acc[:, d, :], lhs[:, d, :], rhs, start=False, stop=False, skip_group_check=True)
                mm.then_inc(sem["block_used"], 1)

            def ffn(s, f):
                pe.wait_ge(sem["h_lo"], 8 * f + 8)
                section = "ffn", f

                def pair(n, k, i):
                    for half_ in range(2):
                        w, wl = parts(section, n + half_, i)
                        if half_ == 0:
                            pe.wait_ge(sem["ffn_a"], i * 4 + (FT * f + k - 1 + PRIME - 2))
                        columns_in_parts(PS[:, k % 2, half_ * T:(half_ + 1) * T], w, wl)

                with pe.Fori(0, FT // 4) as i:
                    for k in range(4):
                        pair(2 * k, k, i)
                for k in range(FT // 4 * 4, FT):
                    pair(2 * k, k, 0)
                open_acc()

                def row(j, i):
                    w, wl = parts(section, 2 * FT + j, i)
                    pe.wait_ge(sem["gate_lo"], i * 8 + (SPLIT[section][1] + j + 1))
                    rows_in_parts(w, wl, gat_hi[:, j % 2, :], gat_lo[:, j % 4, :])

                with pe.Fori(0, FT // 8) as i:
                    for j in range(8):
                        row(j, i)
                for j in range(FT // 8 * 8, FT):
                    row(j, 0)

            def project(first, count, ev, width=P, rows=0):
                if ev + PRIME > 0:
                    pe.wait_ge(sem["proj_evac"], ev + PRIME)

                def one(k, i):
                    w = arrived(first + k, i)
                    pe.wait_ge(sem["proj_evac"], i * 8 + (ev + k - 1 + PRIME))
                    for d in range(DT):
                        mm = pe.matmul(PS[rows:rows + width, k % 2, 0:T], w[:, d, 0:width],
                                       h[:, d, :], start=(d == 0), stop=(d == DT - 1))
                    mm.then_inc(sem["block_used"], 1)

                if count // 8:
                    with pe.Fori(0, count // 8) as i:
                        for k in range(8):
                            one(k, i)
                for k in range(count // 8 * 8, count):
                    one(k, 0)

            def out_project(first, rhs, ktiles=8):
                for d in range(DT):
                    for b in range(ktiles // 8):
                        w = arrived(first + d * (ktiles // 8) + b)
                        for k in range(8):
                            mm = pe.matmul(acc[:, d, :], w[:, k, :], rhs(8 * b + k), start=(b == 0 and k == 0),
                                           stop=(b == ktiles // 8 - 1 and k == 7))
                        mm.then_inc(sem["block_used"], 1)

            def ssd():
                h_in(1)
                b0 = BASE["ssd_in"]
                project(b0, ZT, EV["ssd_z"])
                project(b0 + ZT, XBCT, EV["ssd_xbc"])
                project(b0 + ZT + XBCT, 1, EV["ssd_dt"], width=64)
                pe.wait_ge(sem["conv_silu"], XBCT + PRIME)
                for tt in range(TT):
                    for q in range(4):
                        n = tt * 4 + q
                        if n >= 2:
                            pe.wait_ge(sem["ssd_xtok"], n - 1)
                        for j in range(4):
                            mm = pe.transpose(PS[:, 4 + n % 2, j * P:(j + 1) * P], XS[:, q * 4 + j, tt * P:(tt + 1) * P], ident)
                        mm.then_inc(sem["ssd_tr"], 1)
                pe.wait_ge(sem["ssd_dt"], 1)
                pe.wait_ge(sem["proj_evac"], EV["ssd_dt"] + 1 + PRIME)
                for tt in range(TT):
                    pe.transpose(PS[:, 0, tt * 64:(tt + 1) * 64], SF[:, tt * P:(tt + 1) * P], ident[0:64, 0:64])
                for tt in range(TT):
                    mm = pe.transpose(PS[:, 0, 128 + tt * 64:128 + (tt + 1) * 64], DTF[:, tt * P:(tt + 1) * P], ident[0:64, 0:64])
                mm.then_inc(sem["ssd_tr"], 1)
                for g in range(SSD_GROUPS):
                    if g >= 2:
                        pe.wait_ge(sem["ssd_cb_sb"], g - 1)
                    for u in range(TT):
                        mm = pe.matmul(PS[:, 6 + g % 2, u * T:(u + 1) * T], BM[:, g, u * P:(u + 1) * P], CM[:, g, :],
                                       start=True, stop=True)
                    mm.then_inc(sem["ssd_cb"], 1)
                pe.wait_ge(sem["ssd_xtok"], 9)
                pe.wait_ge(sem["ssd_cb_sb"], SSD_GROUPS)

                def segments(n):
                    hd, u = n // 2, n % 2
                    if n >= 2:
                        pe.wait_ge(sem["ssd_exp"], n - 1)
                    main, other = (hd, 32 + hd) if u == 0 else (32 + hd, hd)
                    bank = PS[:, n % 2, :]
                    tri = (CMB[:, 0:P], CMB[:, P:2 * P]) if u == 0 else (CMB[:, P:2 * P], CMB[:, 0:P])
                    pe.matmul(bank[:, 0:T], ident[0:64, main:main + 1].to_broadcast([64, P]), SF[:, :],
                              start=True, stop=False, skip_group_check=True)
                    pe.matmul(bank[:, u * P:(u + 1) * P], IDB[:, :], tri[0], start=False, stop=False, skip_group_check=True)
                    pe.matmul(bank[:, T:T + P], ident[0:64, other:other + 1].to_broadcast([64, P]), SF[:, u * P:(u + 1) * P],
                              start=False, stop=False, skip_group_check=True)
                    pe.matmul(bank[:, T:T + P], IDB[:, :], tri[1], start=False, stop=True, skip_group_check=True)\
                      .then_inc(sem["ssd_seg"], 1)

                def outputs(hd):
                    pe.wait_ge(sem["ssd_m"], 2 * hd + 2)
                    r = 64 * (hd % 2)
                    pair = hd // 2
                    if pair >= 2 and hd % 2 == 0:
                        pe.wait_ge(sem["ssd_yev"], pair - 1)
                    for u in range(TT):
                        mm = pe.matmul(PS[r:r + 64, 4 + pair % 2, 0:T], XTOK[:, u, hd * 64:(hd + 1) * 64], MB[:, hd % 2, u, :],
                                       start=(u == 0), stop=(u == TT - 1))
                    mm.then_inc(sem["ssd_y"], 1)

                for n in range(2 * SSD_HEADS + 2):
                    if n < 2 * SSD_HEADS:
                        segments(n)
                    if n >= 3 and n % 2 == 1:
                        outputs((n - 3) // 2)
                for g in range(SSD_GROUPS):
                    pe.wait_ge(sem["ssd_ysq"], 1)
                    for j in range(2):
                        mm = pe.matmul(acc[:, g, :], ones, AR[:, 16 + 2 * g + j, :], start=(j == 0), stop=(j == 1))
                mm.then_inc(sem["ssd_ysum"], 1)
                pe.wait_ge(sem["ssd_yn"], ZT)
                out_project(BASE["ssd_out"], lambda k: Y[:, k, :], 16)

            def mla():
                h_in(4)
                b0 = BASE["mla_in"]
                project(b0, 5, EV["mla_in"])
                w = arrived(b0 + 5)
                pe.wait_ge(sem["proj_evac"], EV["mla_in"] + 5 + PRIME)
                for d in range(DT):
                    mm = pe.matmul(PS[64:96, 1, 0:T], w[:, d, 0:ROPE], h[:, d, :], start=(d == 0), stop=(d == DT - 1))
                mm.then_inc(sem["block_used"], 1)
                pe.wait_ge(sem["mla_latsq"], 1)
                for k in range(3):
                    pe.matmul(PS[:, 1, 0:T], ones, SQM[:, k, :], start=(k == 0), stop=(k == 2))
                for k in range(2):
                    mm = pe.matmul(PS[:, 1, T:2 * T], ones, SQM[:, 3 + k, :], start=(k == 0), stop=(k == 1))
                mm.then_inc(sem["mla_latsum"], 1)
                pe.wait_ge(sem["mla_lat"], 1)
                pe.wait_ge(sem["mla_w"], 64)
                for n in range(16):
                    if n >= 4:
                        pe.wait_ge(sem["mla_pev"], n - 3)
                    for j in range(2):
                        hd = 2 * (n % 8) + j
                        o = PS[0:QK if n < 8 else NOPE, 4 + n % 4, j * T:(j + 1) * T]
                        if n < 8:
                            for k in range(3):
                                mm = pe.matmul(o, WUQ[:, k, hd * QK:(hd + 1) * QK], QLAT[:, k, :], start=(k == 0), stop=(k == 2))
                        else:
                            for k in range(2):
                                mm = pe.matmul(o, WUKV[:, k, hd * NOPE:(hd + 1) * NOPE], KVLAT[:, k, :],
                                               start=(k == 0), stop=(k == 1))
                    mm.then_inc(sem["mla_proj"], 1)
                for n in range(4):
                    tt, c = n // 2, n % 2
                    pe.wait_ge(sem["mla_pev"], 13 + n)
                    for k in range(2):
                        mm = pe.matmul(PS[:, 4 + n, :], KVLAT[:, k, tt * P:(tt + 1) * P],
                                       WUKV[:, k, 1024 + c * 512:1024 + (c + 1) * 512], start=(k == 0), stop=(k == 1))
                    mm.then_inc(sem["mla_proj"], 1)
                for n in range(16):
                    pe.wait_ge(sem["mla_sq"], n // 8 + 1)
                    if n >= 2:
                        pe.wait_ge(sem["mla_var"], n - 1)
                    pe.matmul(PS[0:QK, n % 2, :], ones[0:QK, 0:QK], flat(SQM[0:QK, 2 * (n % 8):2 * (n % 8) + 2, :]),
                              start=True, stop=True).then_inc(sem["mla_sum"], 1)
                pe.wait_ge(sem["mla_ang"], 1)
                pe.wait_ge(sem["mla_pev"], 20)
                for n in range(16):
                    q = QH if n < 8 else KH
                    pe.wait_ge(sem["mla_qkn"], n + 1)
                    if n >= 2:
                        pe.wait_ge(sem["mla_rope"], n - 1)
                    pe.matmul(PS[0:QK, 6 + n % 2, :], RPM, flat(q[:, 2 * (n % 8):2 * (n % 8) + 2, :]),
                              start=True, stop=True).then_inc(sem["mla_rot"], 1)
                pe.wait_ge(sem["mla_rope"], 16)

                def logits(hd):
                    if hd >= 2:
                        pe.wait_ge(sem["mla_exp"], hd - 1)
                    for q in range(TT):
                        mm = pe.matmul(PS[:, hd % 2, q * T:(q + 1) * T], QH[:, hd, q * P:(q + 1) * P], KH[:, hd, :],
                                       start=True, stop=True)
                    mm.then_inc(sem["mla_logit"], 1)

                def turn(hd):
                    pe.wait_ge(sem["mla_prob"], hd + 1)
                    if hd >= 2:
                        pe.wait_ge(sem["mla_pts"], hd - 1)
                    for k in range(TT):
                        for q in range(TT):
                            mm = pe.transpose(PS[:, 2 + hd % 2, k * T + q * P:k * T + (q + 1) * P],
                                              PROB[:, hd % 2, q, k * P:(k + 1) * P], ident)
                    mm.then_inc(sem["mla_pt"], 1)

                def values(hd):
                    pe.wait_ge(sem["mla_pts"], hd + 1)
                    pair, r = hd // 2, 64 * (hd % 2)
                    if pair >= 2 and hd % 2 == 0:
                        pe.wait_ge(sem["mla_oev"], pair - 1)
                    for k in range(TT):
                        mm = pe.matmul(PS[r:r + 64, 4 + pair % 2, 0:T], VTOK[:, k, hd * MV:(hd + 1) * MV], PT[:, hd % 2, k, :],
                                       start=(k == 0), stop=(k == TT - 1))
                    mm.then_inc(sem["mla_o"], 1)

                for n in range(MH + 2):
                    if n < MH:
                        logits(n)
                    if 1 <= n <= MH:
                        turn(n - 1)
                    if n >= 2:
                        values(n - 2)
                pe.wait_ge(sem["mla_oev"], 8)
                out_project(BASE["mla_out"], lambda k: OT[:, k, :])

            def rwkv(l):
                h_in(6 + 2 * l)
                project(BASE["mix_in", l], 18, EV["mix_in", l])
                if l == 1:
                    w = arrived(BASE["mix_in", 1] + 18)
                    pe.wait_ge(sem["proj_evac"], EV["mix_in", 1] + 18 + PRIME)
                    for d in range(DT):
                        mm = pe.matmul(PS[0:32, 0, 0:T], w[:, d, 0:32], h[:, d, :], start=(d == 0), stop=(d == DT - 1))
                    mm.then_inc(sem["block_used"], 1)
                pe.wait_ge(sem["rw_w"], 64 + 80 * l)
                pe.wait_ge(sem["rw_lo"], l + 1)
                pe.wait_ge(sem["proj_evac"], EV["mix_in", l] + 18 + l + PRIME)
                for m in range(4):
                    pe.matmul(PS[:, m // 2, (m % 2) * T:(m % 2 + 1) * T], WUP[0:64, m * P:(m + 1) * P], LO[0:64, :],
                              start=True, stop=True)
                for m in range(4):
                    pe.matmul(acc[:, m, :], WUP[64:128, m * P:(m + 1) * P], LO[64:128, :], start=True, stop=True)
                for m in range(4):
                    mm = pe.matmul(acc[:, 4 + m, :], GUP[:, m * P:(m + 1) * P], GD, start=True, stop=True)
                mm.then_inc(sem["rw_lora"], 1)
                if l == 1:
                    pe.wait_ge(sem["rw_gates"], 3 * l + 1)
                    for m in range(4):
                        mm = pe.matmul(PS[:, m // 2, (m % 2) * T:(m % 2 + 1) * T], VUP[0:32, m * P:(m + 1) * P], VD,
                                       start=True, stop=True)
                    mm.then_inc(sem["rw_vres"], 1)
                pe.wait_ge(sem["rw_kksq"], l + 1)
                pe.wait_ge(sem["rw_gates"], 3 * l + 3)
                for c in range(2):
                    mm = pe.matmul(PS[:, 4 + c, :], half, flat(S0[:, 2 * c:2 * c + 2, :]), start=True, stop=True)
                mm.then_inc(sem["rw_kksum"], 1)
                pe.wait_ge(sem["rw_feat"], l + 1)

                def turned(n, src):
                    if n >= 2:
                        pe.wait_ge(sem["rw_trev"], 8 * l + n - 1)
                    for m in range(4):
                        mm = pe.transpose(PS[:, 6 + n % 2, m * P:(m + 1) * P], src(m), ident)
                    mm.then_inc(sem["rw_tr"], 1)

                for tt in range(TT):
                    turned(tt, lambda m: ARH[:, 2 * m + tt, 0, :])
                for tt in range(TT):
                    turned(2 + tt, lambda m: V_[:, m, tt * P:(tt + 1) * P])
                for c in range(16):
                    hd, tt = c // 2, c % 2
                    m, r = hd // 2, 64 * (hd % 2)
                    if c >= 4:
                        pe.wait_ge(sem["rw_matev"], 20 * l + 5 * ((c - 4) // 4) + (c - 4) % 4 + 1)
                    arh = ARH[r:r + 64, 2 * m + tt, :, :].rearrange("p a b -> p (a b)")
                    tok = slice(tt * P, (tt + 1) * P)
                    bank = PS[:, c % 4, :]
                    pe.matmul(bank[:, 0:2 * P], BTIL[r:r + 64, m, tok], arh, start=True, stop=True)
                    pe.matmul(bank[:, 2 * P:4 * P], KTIL[r:r + 64, m, tok], arh, start=True, stop=True)\
                      .then_inc(sem["rw_mat"], 1)
                    if c % 4 == 0 and c >= 8:
                        pe.wait_ge(sem["rw_matev"], 20 * l + 5 * (c // 4 - 2) + 5)
                    if c == 0:
                        pe.wait_ge(sem["rw_kksqrt"], l + 1)
                    if c == 4:
                        pe.wait_ge(sem["rw_trev"], 8 * l + 4)
                    mm = pe.matmul(PS[:, 4 + 2 * (m % 2) + hd % 2, tt * P:(tt + 1) * P], ARH[r:r + 64, 2 * m + tt, 0, :],
                                   BTIL[r:r + 64, m, tok], start=True, stop=True)
                    if c % 4 == 3:
                        mm.then_inc(sem["rw_mat"], 1)
                pe.wait_ge(sem["rw_trev"], 8 * l + 4)
                pe.wait_ge(sem["rw_matev"], 20 * (l + 1))
                m1 = MM[:, :, 0, :]
                steps = ((m1, NA), (NA, m1), (NB, WW), (NC_, NB), (NB, NC_), (NA, WW), (NC_, NA), (NB, WW))
                after = (None, None, 0, 1, 2, 3, 4, 6)
                for st, (lhs, rhs) in enumerate(steps):
                    for b in range(4):
                        if after[st] is not None:
                            pe.wait_ge(sem["rw_neuev"], 36 * l + 4 + 4 * after[st] + b + 1)
                        for j in range(4):
                            c = 4 * b + j
                            mm = pe.matmul(PS[:, (4 * st + b) % 8, j * P:(j + 1) * P], lhs[:, c, :], rhs[:, c, :], start=True, stop=True)
                        mm.then_inc(sem["rw_neu"], 1)
                pe.wait_ge(sem["rw_neuev"], 36 * (l + 1))
                for b in range(2):
                    for j in range(8):
                        c = 8 * b + j
                        hd, tt = c // 2, c % 2
                        mm = pe.matmul(PS[:, b, j * 64:(j + 1) * 64], MM[:, c, 2, :], VTK[:, tt, hd * 64:(hd + 1) * 64],
                                       start=True, stop=True)
                mm.then_inc(sem["rw_x"], 1)
                pe.wait_ge(sem["rw_xev"], l + 1)
                for c in range(16):
                    mm = pe.matmul(PS[:, 4 + c // 4, (c % 4) * P:(c % 4 + 1) * P], WW[:, c, :], XB[:, c, :], start=True, stop=True)
                mm.then_inc(sem["rw_pq"], 1)
                pe.wait_ge(sem["rw_pqev"], l + 1)
                for hd in range(RH):
                    m, r = hd // 2, 64 * (hd % 2)
                    for tt in range(TT):
                        c = 2 * hd + tt
                        at = (m % 2) * T + tt * P
                        oz, oy = PS[r:r + 64, m // 2, at:at + P], PS[r:r + 64, 2 + m // 2, at:at + P]
                        pe.matmul(oz, PQ[:, c, 0:64], MM[:, c, 1, :], start=True, stop=True)
                        pe.matmul(oy, PQ[:, c, 64:128], MM[:, c, 1, :], start=True, stop=False)
                        mm = pe.matmul(oy, VTK[:, tt, hd * 64:(hd + 1) * 64], MM[:, c, 3, :], start=False, stop=True)
                mm.then_inc(sem["rw_zy"], 1)
                for tt in range(TT):
                    turned(4 + tt, lambda m: BHAT[:, m, tt * P:(tt + 1) * P])
                for tt in range(TT):
                    turned(6 + tt, lambda m: KHAT[:, m, tt * P:(tt + 1) * P])
                pe.wait_ge(sem["rw_trev"], 8 * (l + 1))
                for m in range(4):
                    if m:
                        pe.wait_ge(sem["rw_ghev"], 4 * l + m)
                    for a in range(2):
                        hd, r = 2 * m + a, 64 * a
                        for tt in range(TT):
                            for q in range(4):
                                rows = slice(32 * q, 32 * q + 32)
                                pq = PQ[rows, 2 * hd + tt, :]
                                o = PS[r:r + 64, 4 + q, :]
                                pe.matmul(o[:, tt * P:(tt + 1) * P], pq[:, 0:64], BEO[rows, tt, hd, :], start=True, stop=True,
                                          tile_position=(32 * q, r))
                                for par in range(2):
                                    at = 256 + tt * P + par * 64
                                    pe.matmul(o[:, at:at + 64], BEO[rows, tt, hd, par * 64:(par + 1) * 64], pq[:, 64:128],
                                              start=True, stop=False, tile_position=(32 * q, r))
                                    mm = pe.matmul(o[:, at:at + 64], KEO[rows, tt, hd, par * 64:(par + 1) * 64],
                                                   VTK[rows, tt, hd * 64:(hd + 1) * 64], start=False, stop=True,
                                                   tile_position=(32 * q, r))
                    mm.then_inc(sem["rw_gh"], 1)
                pe.wait_ge(sem["rw_ghev"], 4 * (l + 1))
                for c in range(NCH - 1):
                    pe.wait_ge(sem["rw_state"], NCH * l + c + 1)
                    for m in range(4):
                        mm = pe.matmul(PS[:, 4 + c % 2, m * 64:(m + 1) * 64], GT[:, m, c, :], ST[:, c, m, :],
                                       start=True, stop=True)
                    mm.then_inc(sem["rw_step"], 1)
                pe.wait_ge(sem["rw_state"], NCH * (l + 1))
                pe.wait_ge(sem["rw_zyev"], l + 1)
                for hd in range(RH):
                    m, r = hd // 2, 64 * (hd % 2)
                    for c in range(NCH):
                        at = (m % 2) * T + c * CH
                        mm = pe.matmul(PS[r:r + 64, (6 if r else 0) + m // 2, at:at + CH], ST[r:r + 64, c, m, :],
                                       ZT_[r:r + 64, m, c * CH:(c + 1) * CH], start=True, stop=True)
                mm.then_inc(sem["rw_y"], 1)
                pe.wait_ge(sem["rw_yall"], l + 1)
                for c in range(2):
                    mm = pe.matmul(PS[:, 2 + c, :], half, flat(YR[:, 2 * c:2 * c + 2, :]), start=True, stop=True)
                mm.then_inc(sem["rw_mean"], 1)
                for c in range(2):
                    mm = pe.matmul(PS[:, 4 + c, :], half, flat(BON[:, 2 * c:2 * c + 2, :]), start=True, stop=True)
                mm.then_inc(sem["rw_bonus"], 1)
                pe.wait_ge(sem["rw_pool"], l + 1)
                for m in range(4):
                    mm = pe.matmul(PS[:, 6 + m // 2, (m % 2) * T:(m % 2 + 1) * T], POOLW[:, m * P:(m + 1) * P], PL[:, m, :],
                                   start=True, stop=True)
                mm.then_inc(sem["rw_pl"], 1)
                pe.wait_ge(sem["rw_cent"], l + 1)
                for c in range(2):
                    mm = pe.matmul(PS[:, c, :], half, flat(S0[:, 2 * c:2 * c + 2, :]), start=True, stop=True)
                mm.then_inc(sem["rw_var"], 1)
                pe.wait_ge(sem["rw_mix"], l + 1)
                out_project(BASE["mix_out", l], lambda k: YR[:, k, :] if k < 4 else PL[:, k - 4, :])

            def peer(l):
                h_in(7 + 2 * l)
                project(BASE["peer_q", l], 16, EV["peer_q", l])
                pe.wait_ge(sem["proj_evac"], EV["peer_q", l] + 16 + PRIME)
                pe.wait_ge(sem["pe_keys"], 16 * (l + 1))
                for tt in range(TT):
                    for b in range(4):
                        n = tt * 4 + b
                        if n >= 4:
                            pe.wait_ge(sem["pe_scev"], 8 * l + n - 3)
                        for j in range(4):
                            hp = 4 * b + j
                            mm = pe.matmul(PS[:, 4 + n % 4, j * P:(j + 1) * P], QP[:, hp, tt * P:(tt + 1) * P], KEYS[:, hp, :],
                                           start=True, stop=True)
                        mm.then_inc(sem["pe_sc"], 1)
                pe.wait_ge(sem["pe_sm"], l + 1)
                for k in range(3):
                    for tt in range(TT):
                        o = PS[:, k // 2, (k % 2) * T + tt * P:(k % 2) * T + (tt + 1) * P]
                        mm = pe.transpose(o, IJT[:, k, tt, :], ident)
                mm.then_inc(sem["pe_tr"], 1)
                pe.wait_ge(sem["pe_ijg"], l + 1)
                with pe.Fori(0, T // 8) as i:
                    for k in range(2):
                        pe.wait_ge(sem["pe_oh"], i * 2 + (64 * l + k + 1))
                        pe.wait_ge(sem["pe_wev"], i * 2 + (64 * l + k - 1 + PRIME))
                        for j in range(4):
                            mm = pe.matmul(PS[:, k, j * P:(j + 1) * P], OHI[:, k, j, :], OHJ[:, k, j, :],
                                           start=True, stop=True)
                        mm.then_inc(sem["pe_w"], 1)
                pe.wait_ge(sem["pe_wev"], 64 * (l + 1) + PRIME)
                open_acc()

                section = "uv", l
                pe.wait_ge(sem["h_lo"], 32 + l + 1)

                def down(n, j, i):
                    w, wl = parts(section, n, i)
                    pe.wait_ge(sem["pe_gelu"], i * 4 + (NK * l + j - 1 + PRIME))
                    columns_in_parts(PS[:, j % 2, 0:T], w, wl)

                def up(n, j, i):
                    w, wl = parts(section, n, i)
                    pe.wait_ge(sem["gate_lo"], i * 4 + (SPLIT[section][1] + j + 1))
                    rows_in_parts(w, wl, gat_hi[:, j % 2, :], gat_lo[:, j % 4, :])

                down(0, 0, 0)
                whole = (NK - 1) // 4
                with pe.Fori(0, whole) as i:
                    for k in range(4):
                        down(1 + 2 * k, k + 1, i)
                        up(2 + 2 * k, k, i)
                for j in range(4 * whole, NK - 1):
                    down(1 + 2 * j, j + 1, 0)
                    up(2 + 2 * j, j, 0)
                up(2 * NK - 1, NK - 1, 0)

            def begin(s):
                group = (0,) if s == 0 else MOD_GROUPS.get(s - 1, ())
                if group:
                    mod_columns(group[0], 0)
                norm_sum(s)
                for j in range(1, len(group)):
                    mod_columns(group[j], j)
                if len(group) > 1:
                    pe.wait_ge(sem["mod_cols"], group[-1] + 1)

            pe.wait_ge(sem["inits"], 4)
            pe.wait_ge(sem["loads"], 48)
            for i in range(2):
                for s, stage in ((3 * i, lambda: ffn(3 * i, 2 * i)), (3 * i + 1, ssd if i == 0 else mla),
                                 (3 * i + 2, lambda: ffn(3 * i + 2, 2 * i + 1))):
                    begin(s)
                    stage()
            for l in range(2):
                for s, stage in ((6 + 2 * l, rwkv), (7 + 2 * l, peer)):
                    begin(s)
                    stage(l)
            norm_sum(NSUB)


        @block.scalar
        def _(act):
            chain = [0]

            def link(ins):
                chain[0] += 1
                ins.then_inc(sem["act_chain"], 1)
                act.wait_ge(sem["act_chain"], chain[0])

            def ready(n, i=0):
                act.wait_ge(sem["block_used"], i * STEP + (n + 1))

            def norm_squares(s):
                for d in range(DT):
                    if s:
                        act.wait_ge(sem["x_upd"], 8 * (s - 1) + d + 1)
                    act.activation(SQ[:, d, :], x[:, d, :], ACT.Square).then_inc(sem["norm_sq"], 1)
                act.wait_ge(sem["norm_var"], s + 1)
                act.activation(rs[:, :], rv[:, :], ACT.Sqrt).then_inc(sem["norm_sqrt"], 1)

            def shift(s):
                for d in range(DT):
                    act.wait_ge(sem["norm_scaled"], 8 * s + d + 1)
                    if s in (0, 2, 3, 5):
                        act.activation(h_hi[:, d, :], h[:, d, :], ACT.Identity, bias=modc[:, s, d:d + 1], scale=1.0)
                    act.activation(h[:, d, :], h[:, d, :], ACT.Identity, bias=modc[:, s, d:d + 1], scale=1.0)\
                       .then_inc(sem["h_ready"], 1)

            def split_hi(section, n, i):
                block = BASE[section] + n
                act.wait_ge(slot_full[block % RING], i * (STEP // RING * 16) + (block // RING + 1) * 16)
                ready(block - WS, i)
                act.activation(whi[:, n % WS, :], ring[:, block % RING, :], ACT.Copy).then_inc(sem["block_hi"], 1)

            def ffn(f):
                section = "ffn", f
                base = BASE[section]

                def turn(k, i):
                    split_hi(section, 2 * k + 4, i)
                    act.wait_ge(sem["block_used"], i * 8 + (base + 2 * k + 2))
                    act.activation(sil[:, k % 4, :], PS[:, k % 2, 0:T], ACT.Silu).then_inc(sem["ffn_silu"], 1)
                    split_hi(section, 2 * k + 5, i)

                for n in range(4):
                    split_hi(section, n, 0)
                with act.Fori(0, FT // 4) as i:
                    for k in range(4):
                        turn(k, i)
                for k in range(FT // 4 * 4, FT):
                    turn(k, 0)

                def gate_hi(j, i):
                    act.wait_ge(sem["ffn_a"], i * 8 + (FT * f + j + 1 + PRIME - 2))
                    act.activation(gat_hi[:, j % 2, :], ATF[:, i * 8 + j, :], ACT.Copy).then_inc(sem["gate_hi"], 1)

                def row(j, i):
                    ready(base + 2 * FT + j, i)
                    gate_hi(j + 2, i)
                    if j + 4 + 2 * FT < 3 * FT:
                        split_hi(section, 2 * FT + j + 4, i)

                gate_hi(0, 0)
                gate_hi(1, 0)
                with act.Fori(0, FT // 8) as i:
                    for j in range(8):
                        row(j, i)
                for j in range(FT // 8 * 8, FT - 2):
                    row(j, 0)

            def ssd():
                b0 = BASE["ssd_in"]
                with act.Fori(0, ZT // 8) as i:
                    for k in range(8):
                        ready(b0 + k, i)
                        act.activation(Z[:, i * 8 + k, :], PS[:, k % 2, 0:T], ACT.Silu)\
                           .then_inc(sem["proj_evac"], 1)
                with act.Fori(0, XBCT // 8) as i:
                    for k in range(8):
                        ready(b0 + ZT + k, i)
                        act.activation(PADS[:, k % 4, 2:2 + T], PS[:, k % 2, 0:T], ACT.Copy)\
                           .then_inc(sem["proj_evac"], 1)
                        act.wait_ge(sem["conv_step"], i * 40 + 5 * (k + 1))
                        act.activation(AR[:, i * 8 + (16 + k), :], CVA[:, k % 4, :], ACT.Silu,
                                       bias=cols[:, bass.ds(i * 8 + (COLS["conv_b"] + k), 1)], scale=1.0)\
                           .then_inc(sem["conv_silu"], 1)
                ready(b0 + ZT + XBCT)
                act.activation(AUX, PS[0:64, 0, 0:T], ACT.Abs, bias=col("dt_bias")[0:64, :], scale=1.0)
                act.activation(DTF, PS[0:64, 0, 0:T], ACT.Relu, bias=col("dt_bias")[0:64, :], scale=1.0)\
                   .then_inc(sem["proj_evac"], 1)
                act.wait_ge(sem["proj_evac"], EV["ssd_dt"] + 1 + PRIME)
                link(act.activation(eps[0:64, 2:3], col("a_log")[0:64, :], ACT.Exp))
                act.activation(AUX, AUX, ACT.Exp, scale=-1.0).then_inc(sem["ssd_abs"], 1)
                act.wait_ge(sem["ssd_w"], 1)
                act.activation(AF, SF, ACT.Ln).then_inc(sem["ssd_ln"], 1)
                for n in range(8):
                    act.wait_ge(sem["ssd_tr"], n + 1)
                    act.activation(XTOK[:, n // 4, (n % 4) * 512:(n % 4 + 1) * 512], PS[:, 4 + n % 2, :], ACT.Copy)\
                       .then_inc(sem["ssd_xtok"], 1)
                act.wait_ge(sem["ssd_tr"], 9)
                act.activation(flat(NST), PS[:, 0, 0:P], ACT.Copy, scale=-1.0)
                act.activation(flat(DTT), PS[:, 0, P:2 * P], ACT.Copy).then_inc(sem["ssd_xtok"], 1)
                for g in range(SSD_GROUPS):
                    act.wait_ge(sem["ssd_cb"], g + 1)
                    act.activation(flat(CBS[:, g, :, :]), PS[:, 6 + g % 2, :], ACT.Copy).then_inc(sem["ssd_cb_sb"], 1)
                act.wait_ge(sem["ssd_xtok"], 9)
                for n in range(2 * SSD_HEADS):
                    hd, u = n // 2, n % 2
                    main, other = (hd, 32 + hd) if u == 0 else (32 + hd, hd)
                    act.wait_ge(sem["ssd_seg"], n + 1)
                    if n >= 2:
                        act.wait_ge(sem["ssd_m"], n - 1)
                    act.activation(EXB[:, n % 2, 0:T], PS[:, n % 2, 0:T], ACT.Exp, bias=NST[:, u, main:main + 1], scale=1.0)
                    act.activation(EXB[:, n % 2, T:T + P], PS[:, n % 2, T:T + P], ACT.Exp, bias=NST[:, u, other:other + 1],
                                   scale=1.0).then_inc(sem["ssd_exp"], 1)
                act.wait_ge(sem["ssd_yz"], 1)
                act.activation(flat(XS), flat(Y), ACT.Square).then_inc(sem["ssd_ysq"], 1)
                act.wait_ge(sem["ssd_var"], 1)
                act.activation(flat(BM), flat(CM), ACT.Sqrt).then_inc(sem["ssd_ysqrt"], 1)

            def mla():
                b0 = BASE["mla_in"]
                for k in range(5):
                    ready(b0 + k)
                    act.activation(AR[:, 24 + k, :], PS[:, k % 2, 0:T], ACT.Copy)\
                       .then_inc(sem["proj_evac"], 1)
                ready(b0 + 5)
                act.activation(KPE[64:96, :], PS[64:96, 1, 0:T], ACT.Copy).then_inc(sem["proj_evac"], 1)
                act.wait_ge(sem["proj_evac"], EV["mla_in"] + 6 + PRIME)
                act.activation(flat(SQM[:, 0:5, :]), flat(AR[:, 24:29, :]), ACT.Square).then_inc(sem["mla_latsq"], 1)
                act.wait_ge(sem["mla_latvar"], 1)
                act.activation(flat(RSM[:, 0:2, :]), flat(AR[:, 20:22, :]), ACT.Sqrt)\
                   .then_inc(sem["mla_latsqrt"], 1)

                def evac(n):
                    act.wait_ge(sem["mla_proj"], n + 1)
                    if n < 16:
                        rows = QK if n < 8 else NOPE
                        o = AR[0:rows, 66 + 2 * n:68 + 2 * n, :]
                        act.activation(flat(o), PS[0:rows, 4 + n % 4, :], ACT.Copy).then_inc(sem["mla_pev"], 1)
                    else:
                        c = n - 16
                        act.activation(VTOK[:, c // 2, (c % 2) * 512:(c % 2 + 1) * 512], PS[:, 4 + c, :], ACT.Copy)\
                           .then_inc(sem["mla_pev"], 1)

                for n in range(8):
                    evac(n)
                act.wait_ge(sem["mla_pev"], 8)
                act.activation(flat(SQM[0:QK, :, :]), flat(QH), ACT.Square).then_inc(sem["mla_sq"], 1)
                for n in range(8, 20):
                    evac(n)
                for n in range(16):
                    if n == 8:
                        act.wait_ge(sem["mla_sum"], 8)
                        act.wait_ge(sem["mla_kpe"], 1)
                        act.wait_ge(sem["mla_pev"], 16)
                        act.activation(flat(SQM[0:QK, :, :]), flat(KH), ACT.Square).then_inc(sem["mla_sq"], 1)
                    act.wait_ge(sem["mla_var"], n + 1)
                    act.activation(flat(RSM[0:QK, 2 * (n % 2):2 * (n % 2) + 2, :]),
                                   flat(AR[0:QK, 20 + 2 * (n % 2):22 + 2 * (n % 2), :]), ACT.Sqrt).then_inc(sem["mla_sqrt"], 1)
                act.wait_ge(sem["mla_angr"], 1)
                act.activation(SIN, ANG[:, 1, :], ACT.Sin)
                act.activation(COS, ANG[:, 2, :], ACT.Sin).then_inc(sem["mla_ang"], 1)
                for n in range(MH + 1):
                    if n < MH:
                        act.wait_ge(sem["mla_max"], n + 1)
                        if n >= 2:
                            act.wait_ge(sem["mla_pt"], n - 1)
                        for q in range(TT):
                            e = act.activation(PROB[:, n % 2, q, :], PS[:, n % 2, q * T:(q + 1) * T], ACT.Exp,
                                               bias=STAT[:, 8 * n + 2 + q:8 * n + 3 + q], scale=QK ** -0.5,
                                               accum_out=STAT[:, 8 * n + 4 + q:8 * n + 5 + q])
                        e.then_inc(sem["mla_exp"], 1)
                    if n >= 1:
                        act.wait_ge(sem["mla_pt"], n)
                        if n >= 3:
                            act.wait_ge(sem["mla_o"], n - 2)
                        act.activation(flat(PT[:, (n - 1) % 2, :, :]), PS[:, 2 + (n - 1) % 2, :], ACT.Copy)\
                           .then_inc(sem["mla_pts"], 1)

            def rwkv(l):
                first, shifted = BASE["mix_in", l], 14 * l
                act.wait_ge(sem["rw_zpad"], l + 1)
                for n in range(18 + l):
                    ready(first + n)
                    bank = PS[:, n % 2, 0:T]
                    if n < 14:
                        if n >= 4:
                            act.wait_ge(sem["rw_shift"], shifted + n - 3)
                        act.activation(ZPAD[:, n % 4, 1:1 + T], bank, ACT.Copy).then_inc(sem["proj_evac"], 1)
                    elif n < 18:
                        act.activation(PL[:, n - 14, :], bank, ACT.Copy).then_inc(sem["proj_evac"], 1)
                    else:
                        act.wait_ge(sem["rw_shift"], shifted + 14)
                        act.activation(ZPAD[0:32, 2, 1:1 + T], PS[0:32, 0, 0:T], ACT.Copy).then_inc(sem["proj_evac"], 1)
                act.wait_ge(sem["rw_shift"], shifted + 14 + l)
                act.activation(LO[0:64, :], LO[0:64, :], ACT.Tanh)
                act.activation(GD, GD, ACT.Sigmoid).then_inc(sem["rw_lo"], 1)
                act.wait_ge(sem["rw_lora"], l + 1)
                for m in range(4):
                    e = act.activation(LD[:, m, :], PS[:, m // 2, (m % 2) * T:(m % 2 + 1) * T], ACT.Sigmoid,
                                       bias=col("w0", 4 * l + m), scale=1.0)
                e.then_inc(sem["rw_gates"], 1)
                for m in range(4):
                    e = act.activation(AA[:, m, :], acc[:, m, :], ACT.Sigmoid, bias=col("a0", 4 * l + m), scale=1.0)
                e.then_inc(sem["rw_gates"], 1)
                act.activation(flat(GG), flat(acc[:, 4:8, :]), ACT.Copy).then_inc(sem["rw_gates"], 1)
                if l == 1:
                    act.wait_ge(sem["rw_vres"], 1)
                    for m in range(4):
                        e = act.activation(S0[:, m, :], PS[:, m // 2, (m % 2) * T:(m % 2 + 1) * T], ACT.Sigmoid,
                                           bias=col("vres_v0", m), scale=1.0)
                    e.then_inc(sem["rw_vresa"], 1)
                act.wait_ge(sem["rw_kkvar"], l + 1)
                act.activation(flat(S0), flat(KTIL), ACT.Sqrt).then_inc(sem["rw_kksqrt"], 1)
                act.wait_ge(sem["rw_ld"], l + 1)
                act.activation(flat(EL), flat(LL), ACT.Exp)
                act.activation(flat(EM), flat(LL), ACT.Exp, scale=-1.0)
                act.activation(flat(LD), flat(LD), ACT.Exp).then_inc(sem["rw_exps"], 1)
                act.wait_ge(sem["rw_gnvar"], l + 1)
                act.activation(flat(S0), flat(GNV), ACT.Sqrt).then_inc(sem["rw_sd"], 1)

            def peer(l):
                act.wait_ge(sem["h_ready"], 8 * (8 + 2 * l))
                act.activation(flat(h_hi[:, :, :]), flat(h[:, :, :]), ACT.Copy).then_inc(sem["uv_h_hi"], 1)
                for n in range(16):
                    ready(BASE["peer_q", l] + n)
                    act.activation(QP[:, n, :], PS[:, n % 2, 0:T], ACT.Copy)\
                       .then_inc(sem["proj_evac"], 1)
                for n in range(8):
                    act.wait_ge(sem["pe_sc"], 8 * l + n + 1)
                    o = SC[:, n // 4, 4 * (n % 4):4 * (n % 4) + 4, :]
                    act.activation(flat(o), PS[:, 4 + n % 4, :], ACT.Copy).then_inc(sem["pe_scev"], 1)
                act.wait_ge(sem["pe_top"], l + 1)
                act.activation(SMX, SMX, ACT.Exp).then_inc(sem["pe_exp"], 1)
                act.wait_ge(sem["pe_tr"], l + 1)
                act.activation(flat(ijg[:, :, :]), PS[:, 0:2, :].rearrange("p a b -> p (a b)")[:, 0:3 * T], ACT.Copy)\
                   .then_inc(sem["pe_ijg"], 1)
                with act.Fori(0, T // 8) as i:
                    for k in range(2):
                        act.wait_ge(sem["pe_w"], i * 2 + (64 * l + k + 1 + 2))
                        act.activation(WALL[:, bass.ds(i * 8 + 4 * k, 4), :].rearrange("p a b -> p (a b)"), PS[:, k, :], ACT.Copy)\
                           .then_inc(sem["pe_wev"], 1)
                base = BASE["uv", l]

                def gelu(j, i):
                    act.wait_ge(sem["block_used"], i * 8 + (base + max(1, 2 * j)))
                    act.activation(sil[:, j % 4, :], PS[:, j % 2, 0:T], ACT.Gelu).then_inc(sem["pe_gelu"], 1)

                section = "uv", l

                def turn(j, i):
                    gelu(j, i)
                    split_hi(section, 2 * j + 2, i)
                    split_hi(section, 2 * j + 3, i)

                split_hi(section, 0, 0)
                split_hi(section, 1, 0)
                for j in range(4):
                    turn(j, 0)
                with act.Fori(0, NK // 4 - 2) as i:
                    for k in range(4):
                        turn(4 + k, i)
                for j in range(NK - 4, NK - 1):
                    turn(j, 0)
                gelu(NK - 1, 0)

            act.sem_inc(sem["proj_evac"], PRIME)
            act.sem_inc(sem["conv_silu"], PRIME)
            act.sem_inc(sem["pe_wev"], PRIME)
            act.sem_inc(sem["pe_gelu"], PRIME)
            act.sem_inc(sem["pe_gated"], PRIME)
            act.sem_inc(sem["ffn_a"], PRIME - 2)
            act.sem_inc(sem["pe_w"], 2)
            act.wait_ge(sem["inits"], 4)
            act.wait_ge(sem["loads"], 48)
            act.activation(cond[:, :], cols[:, 0:16], ACT.Silu).then_inc(sem["cond_ready"], 1)
            for s in range(NSUB):
                norm_squares(s)
                shift(s)
                if s in (0, 2, 3, 5):
                    ffn((0, 2, 3, 5).index(s))
                elif s == 1:
                    ssd()
                elif s == 4:
                    mla()
                elif s % 2 == 0:
                    rwkv((s - 6) // 2)
                else:
                    peer((s - 7) // 2)
            norm_squares(NSUB)

        @block.vector
        def _(dve):
            chain = [0]

            def link(ins):
                chain[0] += 1
                ins.then_inc(sem["dve_chain"], 1)
                dve.wait_ge(sem["dve_chain"], chain[0])

            def ready(n):
                dve.wait_ge(sem["block_used"], n + 1)

            def inverse_root(r, v, t):
                link(dve.reciprocal(r, r))
                link(dve.scalar_tensor_tensor(t, r, -0.5, v, ALU.mult, ALU.mult))
                link(dve.tensor_tensor(t, t, r, ALU.mult))
                link(dve.scalar_tensor_tensor(r, t, 1.5, r, ALU.add, ALU.mult))

            def first_products():
                dve.wait_ge(sem["cond_ready"], 1)
                for n in range(24):
                    t, d = divmod(n, 8)
                    dve.wait_ge(slot_full[n % RING], (n // RING + 1) * 16)
                    w, out = ring[:, n % RING, :], MODSUM[:, t, :]
                    if d == 0:
                        ins = dve.tensor_scalar(out, w, cond[:, 0:1], None, ALU.mult)
                    else:
                        dve.wait_ge(sem["block_used"], n)
                        ins = dve.scalar_tensor_tensor(out, w, cond[:, d:d + 1], out, ALU.mult, ALU.add)
                    ins.then_inc(sem["block_used"], 1)

            def mod_products(f, d, t):
                first = 24 * (MOD_GROUPS[f][0] - 1)
                c, slot, out = cond[:, (0 if f < 3 else 8) + d:][:, 0:1], MODRING[d % MOD_RING], MODSUM[:, t, :]
                dve.wait_ge(mod_full[d % MOD_RING], t * 32 + (first // MOD_RING + d // MOD_RING + 1) * 16)
                if d == 0:
                    ins = dve.tensor_scalar(out, slot, c, None, ALU.mult)
                else:
                    dve.wait_ge(sem["mod_acc"], t * 8 + (first + d))
                    ins = dve.scalar_tensor_tensor(out, slot, c, out, ALU.mult, ALU.add)
                ins.then_inc(sem["mod_acc"], 1)

            def mod_columns(s, j):
                dve.wait_ge(sem["mod_sum"], s + 1)
                bias = col("b_mod", 24 * s, 24) if s < 6 else col("ada_b", 24 * (s - 6), 24)
                g = col("norm_g", 8 * s, 8) if s < 6 else col("ln1" if s % 2 == 0 else "ln2", 8 * ((s - 6) // 2), 8)
                m = modc[:, s, :]
                dve.tensor_tensor(m, PS[:, 3, 24 * j:24 * j + 24], bias, ALU.add).then_inc(sem["mod_cols"], 1)
                dve.wait_ge(sem["mod_cols"], s + 1)
                link(dve.scalar_tensor_tensor(m[:, 8:16], m[:, 8:16], 1.0, g, ALU.add, ALU.mult))
                if s in (0, 2, 3, 5):
                    link(dve.tensor_scalar(m[:, 16:24], m[:, 16:24], 0.5, None, ALU.mult))

            def normed(s):
                dve.wait_ge(sem["norm_sum"], s + 1)
                dve.tensor_scalar(rv[:, :], PS[:, 2, 0:T], 1.0 / D, EPS, ALU.mult, ALU.add).then_inc(sem["norm_var"], 1)
                dve.wait_ge(sem["norm_sqrt"], s + 1)
                inverse_root(rs[:, :], rv[:, :], SQ[:, 0, :])
                for d in range(DT):
                    g = modc[:, s, 8 + d:9 + d] if s < NSUB else col("lnf", d)
                    dve.scalar_tensor_tensor(h[:, d, :], x[:, d, :], g, rs[:, :], ALU.mult, ALU.mult)\
                       .then_inc(sem["norm_scaled" if s < NSUB else "out_ready"], 1)

            def residual(s, last):
                for d in range(DT):
                    ready(last(d | 1))
                    dve.scalar_tensor_tensor(x[:, d, :], acc[:, d, :], modc[:, s, 16 + d:17 + d], x[:, d, :], ALU.mult, ALU.add)\
                       .then_inc(sem["x_upd"], 1)

            def split_lo(section, n, i):
                slot = (BASE[section] + n) % RING
                dve.wait_ge(sem["block_hi"], i * 8 + (SPLIT[section][0] + n + 1))
                dve.tensor_tensor(ring_lo[:, slot, :], ring[:, slot, :], whi[:, n % WS, :].bitcast(F32), ALU.subtract)\
                   .then_inc(sem["block_lo"], 1)

            def ffn(f):
                section = "ffn", f
                base = BASE[section]
                s = (0, 2, 3, 5)[f]
                for d in range(DT):
                    dve.wait_ge(sem["h_ready"], 8 * s + d + 1)
                    dve.tensor_tensor(h_lo[:, d, :], h[:, d, :], h_hi[:, d, :].bitcast(F32), ALU.subtract).then_inc(sem["h_lo"], 1)

                def turn(k, i):
                    split_lo(section, 2 * k + 4, i)
                    if k < FT // 4 * 4:
                        mod_products(s, 2 * k % 8, i)
                    dve.wait_ge(sem["ffn_silu"], i * 4 + (FT * f + k + 1))
                    dve.wait_ge(sem["block_used"], i * 8 + (base + 2 * k + 2))
                    dve.tensor_tensor(ATF[:, i * 4 + k, :], sil[:, k % 4, :], PS[:, k % 2, T:2 * T], ALU.mult)\
                       .then_inc(sem["ffn_a"], 1)
                    split_lo(section, 2 * k + 5, i)
                    if k < FT // 4 * 4:
                        mod_products(s, 2 * k % 8 + 1, i)

                for n in range(4):
                    split_lo(section, n, 0)
                with dve.Fori(0, FT // 4) as i:
                    for k in range(4):
                        turn(k, i)
                for k in range(FT // 4 * 4, FT):
                    turn(k, 0)

                def gate_lo(j, i):
                    dve.wait_ge(sem["gate_hi"], i * 8 + (SPLIT[section][1] + j + 1))
                    dve.tensor_tensor(gat_lo[:, j % 4, :], ATF[:, i * 8 + j, :], gat_hi[:, j % 2, :].bitcast(F32), ALU.subtract)\
                       .then_inc(sem["gate_lo"], 1)

                def row(j, i):
                    gate_lo(j + 2, i)
                    if j + 4 + 2 * FT < 3 * FT:
                        split_lo(section, 2 * FT + j + 4, i)

                gate_lo(0, 0)
                gate_lo(1, 0)
                t0, thirds = FT // 4, 3 * len(MOD_GROUPS[s])
                if thirds - t0 == 4:
                    with dve.Fori(0, FT // 8) as i:
                        for j in range(8):
                            row(j, i)
                            for d in range(2):
                                mod_products(s, (2 * j + d) % 8, i * 2 + (t0 + j // 4))
                    for j in range(FT // 8 * 8, FT - 2):
                        row(j, 0)
                else:
                    for j in range(FT - 2):
                        row(j, 0)
                        if 4 <= j < 12:
                            mod_products(s, j - 4, t0)
                residual(s, lambda d: base + 3 * FT - 1)

            def ssd():
                cw = COLS["conv_w"]
                with dve.Fori(0, XBCT // 8) as i:
                    for k in range(8):
                        o = CVA[:, k % 4, :]
                        dve.wait_ge(sem["proj_evac"], i * 8 + (EV["ssd_xbc"] + k + 1 + PRIME))
                        dve.wait_ge(sem["conv_silu"], i * 8 + (k - 3 + PRIME))
                        for j in range(CONV):
                            w = cols[:, bass.ds(i * 40 + (cw + 5 * k + j), 1)]
                            src = PADS[:, k % 4, j:j + T]
                            if j == 0:
                                ins = dve.tensor_scalar(o, src, w, None, ALU.mult)
                            else:
                                dve.wait_ge(sem["conv_step"], i * 40 + (5 * k + j))
                                ins = dve.scalar_tensor_tensor(o, src, w, o, ALU.mult, ALU.add)
                            ins.then_inc(sem["conv_step"], 1)
                dve.wait_ge(sem["ssd_abs"], 1)
                dve.tensor_scalar(SF, AUX, 1.0, None, ALU.add).then_inc(sem["ssd_w"], 1)
                dve.wait_ge(sem["ssd_ln"], 1)
                t0, t1 = AR[0:64, 117, :], AR[0:64, 110, :]
                link(dve.tensor_tensor(AF, AF, AUX, ALU.mult))
                link(dve.tensor_scalar(SF, SF, -1.0, None, ALU.add))
                link(dve.tensor_scalar(t0, SF, 1e-30, None, ALU.max))
                link(dve.reciprocal(t0, t0))
                link(dve.tensor_tensor(AF, AF, t0, ALU.mult))
                link(dve.scalar_tensor_tensor(t1, SF, 0.0, AUX, ALU.is_equal, ALU.mult))
                link(dve.tensor_tensor(AF, AF, t1, ALU.add))
                link(dve.tensor_tensor(DTF, DTF, AF, ALU.add))
                link(dve.tensor_scalar(AF, DTF, eps[0:64, 2:3], -1.0, ALU.mult, ALU.mult))
                link(dve.memset(AUX, 1.0))
                link(dve.tensor_tensor_scan(SF, AUX, AF, 0.0, ALU.mult, ALU.add))
                dve.tensor_tensor(SF[32:64, :], AF[32:64, :], SF[32:64, :], ALU.subtract).then_inc(sem["ssd_dt"], 1)
                dve.wait_ge(sem["ssd_cb_sb"], SSD_GROUPS)
                dve.wait_ge(sem["ssd_xtok"], 9)

                def out_pair(p):
                    dve.wait_ge(sem["ssd_y"], 2 * p + 2)
                    dve.scalar_tensor_tensor(Y[:, p, :], XS[:, p, :], col("ssd_d", p), PS[:, 4 + p % 2, 0:T], ALU.mult, ALU.add)\
                       .then_inc(sem["ssd_yev"], 1)

                for n in range(2 * SSD_HEADS):
                    hd, u = n // 2, n % 2
                    g = hd // 4
                    main, other = (hd, 32 + hd) if u == 0 else (32 + hd, hd)
                    diag, off = slice(u * P, (u + 1) * P), slice((1 - u) * P, (2 - u) * P)
                    tmp = TMP[:, (n % 2) * P:(n % 2 + 1) * P]
                    dve.wait_ge(sem["ssd_exp"], n + 1)
                    if hd >= 2:
                        dve.wait_ge(sem["ssd_y"], hd - 1)
                    link(dve.tensor_scalar(tmp, EXB[:, n % 2, T:T + P], DTT[:, u, other:other + 1], None, ALU.mult))
                    dve.scalar_tensor_tensor(MB[:, hd % 2, u, off], EXB[:, n % 2, off], DTT[:, u, main:main + 1],
                                             CBS[:, g, u, off], ALU.mult, ALU.mult)
                    link(dve.scalar_tensor_tensor(tmp, EXB[:, n % 2, diag], DTT[:, u, main:main + 1], tmp, ALU.mult, ALU.add))
                    dve.tensor_tensor(MB[:, hd % 2, u, diag], tmp, CBS[:, g, u, diag], ALU.mult).then_inc(sem["ssd_m"], 1)
                    if n >= 6 and (n - 6) % 4 == 0:
                        out_pair((n - 6) // 4)
                out_pair(15)
                dve.wait_ge(sem["ssd_yev"], 16)
                dve.tensor_tensor(flat(Y), flat(Y), flat(Z), ALU.mult).then_inc(sem["ssd_yz"], 1)
                dve.wait_ge(sem["ssd_ysum"], 1)
                dve.tensor_scalar(flat(CM), flat(acc), 1.0 / 256, EPS, ALU.mult, ALU.add).then_inc(sem["ssd_var"], 1)
                dve.wait_ge(sem["ssd_ysqrt"], 1)
                inverse_root(flat(BM), flat(CM), flat(AR[:, 16:24, :]))
                for k in range(ZT):
                    dve.scalar_tensor_tensor(Y[:, k, :], Y[:, k, :], col("ssd_g", k), BM[:, k // 2, :], ALU.mult, ALU.mult)\
                       .then_inc(sem["ssd_yn"], 1)
                residual(1, lambda d: BASE["ssd_out"] + 2 * d + 1)

            def mla():
                dve.wait_ge(sem["mla_w"], 64)
                c1, c2 = 6.28125, 1.93500518798828125e-3
                c3 = 2 * np.pi - c1 - c2
                pi = float(np.float32(np.pi))
                magic = 12582912.0
                link(dve.tensor_copy(ANG[:, 1, :], ANG[:, 0, :].bitcast(I32)))
                link(dve.tensor_scalar(ANG[:, 1, :], ANG[:, 1, :], col("freq")[0:QK, :], None, ALU.mult))
                link(dve.tensor_scalar(ANG[:, 2, :], ANG[:, 1, :], 1.0 / (2 * np.pi), magic, ALU.mult, ALU.add))
                link(dve.tensor_scalar(ANG[:, 2, :], ANG[:, 2, :], -magic, None, ALU.add))
                for c in (c1, c2, c3):
                    link(dve.scalar_tensor_tensor(ANG[:, 1, :], ANG[:, 2, :], -c, ANG[:, 1, :], ALU.mult, ALU.add))
                link(dve.tensor_scalar(ANG[:, 1, :], ANG[:, 1, :], pi, -pi, ALU.min, ALU.max))
                link(dve.tensor_scalar(ANG[:, 2, :], ANG[:, 1, :], np.pi / 2, None, ALU.add))
                link(dve.tensor_scalar(ANG[:, 3, :], ANG[:, 2, :], pi, -2 * np.pi, ALU.is_gt, ALU.mult))
                link(dve.tensor_tensor(ANG[:, 2, :], ANG[:, 2, :], ANG[:, 3, :], ALU.add))
                dve.tensor_scalar(ANG[:, 2, :], ANG[:, 2, :], pi, -pi, ALU.min, ALU.max).then_inc(sem["mla_angr"], 1)
                dve.wait_ge(sem["mla_latsum"], 1)
                dve.tensor_scalar(AR[:, 20, :], PS[:, 1, 0:T], 1.0 / QL, EPS, ALU.mult, ALU.add)
                dve.tensor_scalar(AR[:, 21, :], PS[:, 1, T:2 * T], 1.0 / KVL, EPS, ALU.mult, ALU.add).then_inc(sem["mla_latvar"], 1)
                dve.wait_ge(sem["mla_latsqrt"], 1)
                inverse_root(flat(RSM[:, 0:2, :]), flat(AR[:, 20:22, :]), flat(AR[:, 22:24, :]))
                for k in range(5):
                    e = dve.scalar_tensor_tensor(AR[:, 24 + k, :], AR[:, 24 + k, :], col("q_norm", k) if k < 3 else col("kv_norm", k - 3),
                                                 RSM[:, 0 if k < 3 else 1, :], ALU.mult, ALU.mult)
                e.then_inc(sem["mla_lat"], 1)
                def mean_square(n):
                    dve.wait_ge(sem["mla_sum"], n + 1)
                    dve.tensor_scalar(flat(AR[0:QK, 20 + 2 * (n % 2):22 + 2 * (n % 2), :]), PS[0:QK, n % 2, :], 1.0 / QK, EPS,
                                      ALU.mult, ALU.add).then_inc(sem["mla_var"], 1)

                mean_square(0)
                for n in range(16):
                    q = QH if n < 8 else KH
                    two = flat(q[:, 2 * (n % 8):2 * (n % 8) + 2, :])
                    r, v, t = (flat(AR[0:QK, k + 2 * (n % 2):k + 2 + 2 * (n % 2), :]) for k in (16, 20, 24))
                    if n < 15:
                        mean_square(n + 1)
                    dve.wait_ge(sem["mla_sqrt"], n + 1)
                    inverse_root(r, v, t)
                    dve.scalar_tensor_tensor(two, two, col("q_head" if n < 8 else "k_head")[0:QK, :], r, ALU.mult, ALU.mult)\
                       .then_inc(sem["mla_qkn"], 1)
                dve.wait_ge(sem["mla_ang"], 1)
                dve.wait_ge(sem["mla_qkn"], 16)
                for n in range(16):
                    q = QH if n < 8 else KH
                    two = q[:, 2 * (n % 8):2 * (n % 8) + 2, :]
                    t = SQM[0:QK, 8 + 2 * (n % 2):10 + 2 * (n % 2), :]
                    dve.wait_ge(sem["mla_rot"], n + 1)
                    dve.tensor_tensor(t, PS[0:QK, 6 + n % 2, :].rearrange("p (a b) -> p a b", a=2), rep(SIN, 2), ALU.mult)
                    link(dve.tensor_tensor(two, two, rep(COS, 2), ALU.mult))
                    dve.tensor_tensor(two, two, t, ALU.add).then_inc(sem["mla_rope"], 1)
                for n in range(MH + 3):
                    if n < MH:
                        c = 8 * n
                        dve.wait_ge(sem["mla_logit"], n + 1)
                        link(dve.tensor_reduce(STAT[:, c:c + 2], PS[:, n % 2, :].rearrange("p (a b) -> p a b", a=2), AX.X, ALU.max))
                        dve.tensor_scalar(STAT[:, c + 2:c + 4], STAT[:, c:c + 2], -QK ** -0.5, None, ALU.mult)\
                           .then_inc(sem["mla_max"], 1)
                    if 1 <= n <= MH:
                        c = 8 * (n - 1)
                        dve.wait_ge(sem["mla_exp"], n)
                        link(dve.reciprocal(STAT[:, c + 6:c + 8], STAT[:, c + 4:c + 6]))
                        for q in range(TT):
                            p = PROB[:, (n - 1) % 2, q, :]
                            e = dve.tensor_scalar(p, p, STAT[:, c + 6 + q:c + 7 + q], None, ALU.mult)
                        e.then_inc(sem["mla_prob"], 1)
                    if n >= 3 and n % 2 == 1 and (n - 3) // 2 < 8 and n - 3 < MH:
                        p = (n - 3) // 2
                        dve.wait_ge(sem["mla_o"], 2 * p + 2)
                        dve.tensor_copy(OT[:, p, :], PS[:, 4 + p % 2, 0:T]).then_inc(sem["mla_oev"], 1)
                residual(4, lambda d: BASE["mla_out"] + d)

            def rwkv(l):
                shifted = 14 * l
                V4 = lambda name: col(name, 4 * l, 4)
                for n in list(range(14)) + [18] * l:
                    rows = 32 if n == 18 else P
                    z = ZPAD[0:rows, n % 4, :]
                    dif = ZDIF[0:rows, n % 4, :]
                    o = VD if n == 18 else R_[:, n, :] if n < 4 else K_[:, n - 4, :] if n < 8 else V_[:, n - 8, :] if n < 12 \
                        else (LO, GD)[n - 12]
                    mu = col("vres_mu")[0:32, :] if n == 18 else col("mu", 14 * l + n)
                    dve.wait_ge(sem["proj_evac"], EV["mix_in", l] + n + 1 + PRIME)
                    link(dve.tensor_tensor(dif, z[:, 0:T], z[:, 1:1 + T], ALU.subtract))
                    dve.scalar_tensor_tensor(o, dif, mu, z[:, 1:1 + T], ALU.mult, ALU.add).then_inc(sem["rw_shift"], 1)
                dve.wait_ge(sem["rw_shift"], shifted + 14 + l)
                dve.wait_ge(sem["rw_w"], 64 + 80 * l)
                if l == 0:
                    link(dve.tensor_copy(flat(vfirst[:, :, :]), flat(V_)))
                else:
                    dve.wait_ge(sem["rw_vresa"], 1)
                    link(dve.tensor_tensor(flat(S1), flat(vfirst[:, :, :]), flat(V_), ALU.subtract))
                    link(dve.tensor_tensor(flat(S1), flat(S1), flat(S0), ALU.mult))
                    link(dve.tensor_tensor(flat(V_), flat(V_), flat(S1), ALU.add))
                link(dve.tensor_tensor(KK, K_, bc(V4("k_k"), T), ALU.mult))
                dve.tensor_tensor(flat(S0), flat(KK), flat(KK), ALU.mult).then_inc(sem["rw_kksq"], 1)
                dve.wait_ge(sem["rw_gates"], 3 * l + 1)
                link(dve.tensor_scalar(flat(LD), flat(LD), -float(np.exp(-0.5)), None, ALU.mult))
                for m in range(4):
                    e = dve.tensor_tensor_scan(LL[:, m, :], RESTART, LD[:, m, :], 0.0, ALU.mult, ALU.add)
                link(e)
                dve.tensor_tensor(flat(LD), flat(LL), flat(LD), ALU.subtract).then_inc(sem["rw_ld"], 1)
                dve.wait_ge(sem["rw_gates"], 3 * l + 2)
                link(dve.tensor_scalar(flat(S1), flat(AA), -1.0, None, ALU.add))
                link(dve.tensor_tensor(S1, S1, bc(V4("k_a"), T), ALU.mult))
                link(dve.scalar_tensor_tensor(flat(K_), flat(S1), 1.0, flat(K_), ALU.add, ALU.mult))
                link(dve.tensor_tensor(flat(BON), flat(R_), flat(K_), ALU.mult))
                link(dve.tensor_tensor(BON, BON, bc(V4("r_k"), T), ALU.mult))
                dve.wait_ge(sem["rw_kksum"], l + 1)
                dve.tensor_scalar(flat(KTIL), PS[:, 4:6, :].rearrange("p a b -> p (a b)"), 1e-24, None, ALU.max)\
                   .then_inc(sem["rw_kkvar"], 1)
                dve.wait_ge(sem["rw_kksqrt"], l + 1)
                inverse_root(flat(S0), flat(KTIL), flat(BTIL))
                link(dve.tensor_tensor(flat(KK), flat(KK), flat(S0), ALU.mult))
                link(dve.tensor_tensor(flat(AA), flat(KK), flat(AA), ALU.mult))
                dve.wait_ge(sem["rw_exps"], l + 1)

                def m8(v):
                    return v.rearrange("p m (t c) -> p (m t) c", t=TT)

                dve.scalar_tensor_tensor(ARH[:, :, 0, :], m8(KK), -1.0, m8(LD), ALU.mult, ALU.mult)
                dve.tensor_tensor(ARH[:, :, 1, :], m8(R_), m8(EL), ALU.mult)
                dve.tensor_tensor(flat(ZT_), flat(R_), flat(EL), ALU.mult)
                dve.tensor_tensor(flat(BTIL), flat(AA), flat(EM), ALU.mult)
                dve.tensor_tensor(flat(KTIL), flat(K_), flat(EM), ALU.mult)
                link(dve.tensor_copy(LC, flat(EL).rearrange("p (c j) -> p c j", j=CH)[:, :, CH - 1]))

                def chunks(v):
                    return flat(v).rearrange("p (c j) -> p c j", j=CH)

                dve.tensor_tensor(chunks(BHAT), chunks(BTIL), bc(LC, CH), ALU.mult)
                dve.tensor_tensor(chunks(KHAT), chunks(KTIL), bc(LC, CH), ALU.mult).then_inc(sem["rw_feat"], 1)
                for n in range(4):
                    dve.wait_ge(sem["rw_tr"], 8 * l + n + 1)
                    dve.tensor_copy((ATK if n < 2 else VTK)[:, n % 2, :], PS[:, 6 + n % 2, :]).then_inc(sem["rw_trev"], 1)
                for c in range(16):
                    dve.wait_ge(sem["rw_mat"], 20 * l + 5 * (c // 4) + c % 4 + 1)
                    dve.tensor_tensor(MM[:, c, :, :].rearrange("p a b -> p (a b)"), PS[:, c % 4, :], MASK4, ALU.mult)\
                       .then_inc(sem["rw_matev"], 1)
                    if c % 4 == 3:
                        b = c // 4
                        dve.wait_ge(sem["rw_mat"], 20 * l + 5 * b + 5)
                        dve.tensor_tensor(NA[:, 4 * b:4 * b + 4, :].rearrange("p (a t) n -> p a (t n)", t=2), PS[:, 4 + 2 * (b % 2):6 + 2 * (b % 2), 0:T],
                                          rep(MASKN, 2), ALU.mult).then_inc(sem["rw_matev"], 1)
                dve.wait_ge(sem["rw_matev"], 20 * (l + 1))
                for b in range(4):
                    dve.tensor_tensor(WW[:, 4 * b:4 * b + 4, :], MM[:, 4 * b:4 * b + 4, 0, :], rep(ident, 4), ALU.add)\
                       .then_inc(sem["rw_neuev"], 1)
                dve.wait_ge(sem["rw_neuev"], 36 * l + 4)
                for st, o in enumerate((NB, NC_, WW, NA, NC_, WW, NB, WW)):
                    for b in range(4):
                        dve.wait_ge(sem["rw_neu"], 32 * l + 4 * st + b + 1)
                        src = PS[:, (4 * st + b) % 8, :].rearrange("p (a b) -> p a b", a=4)
                        to = o[:, 4 * b:4 * b + 4, :]
                        if o is WW:
                            dve.wait_ge(sem["rw_neuev"], 36 * l + 4 + 4 * (st - 1) + b + 1)
                            e = dve.tensor_tensor(to, src, to, ALU.add)
                        else:
                            e = dve.tensor_copy(to, src)
                        e.then_inc(sem["rw_neuev"], 1)
                dve.wait_ge(sem["rw_x"], l + 1)
                for tt in range(TT):
                    v = XB.rearrange("p (h t) n -> p h t n", t=TT)[:, :, tt, :]
                    dve.tensor_copy(v[:, :, 0:64], ATK[:, tt, :].rearrange("p (h k) -> p h k", h=RH))
                for b in range(2):
                    e = dve.tensor_copy(XB[:, 8 * b:8 * b + 8, 64:128], PS[:, b, :].rearrange("p (a b) -> p a b", a=8))
                e.then_inc(sem["rw_xev"], 1)
                dve.wait_ge(sem["rw_pq"], l + 1)
                for b in range(4):
                    e = dve.tensor_copy(PQ[:, 4 * b:4 * b + 4, :].rearrange("p a b -> p (a b)"), PS[:, 4 + b, :])
                e.then_inc(sem["rw_pqev"], 1)
                dve.wait_ge(sem["rw_zy"], l + 1)
                dve.tensor_tensor(flat(ZT_), flat(ZT_), PS[:, 0:2, :].rearrange("p a b -> p (a b)"), ALU.add)
                dve.tensor_copy(flat(YR), PS[:, 2:4, :].rearrange("p a b -> p (a b)")).then_inc(sem["rw_zyev"], 1)
                dve.wait_ge(sem["rw_zeroed"], l + 1)
                for a in range(2):
                    r = slice(64 * a, 64 * a + 64)
                    e = dve.tensor_tensor(GT[r, :, :, 64 * a:64 * a + 64].rearrange("p m c n -> p (m c) n"), bc(LC[r, :], 64),
                                          rep(ident[r, 64 * a:64 * a + 64], 64), ALU.mult)
                link(e)
                for n in range(4, 8):
                    dve.wait_ge(sem["rw_tr"], 8 * l + n + 1)
                    src = PS[:, 6 + n % 2, :].rearrange("p (h k) -> p h k", h=RH)
                    to = (BEO if n < 6 else KEO)[:, n % 2, :, :]
                    dve.tensor_scalar(to[:, :, 0:64], src, col("even"), None, ALU.mult)
                    dve.tensor_scalar(to[:, :, 64:128], src, col("odd"), None, ALU.mult).then_inc(sem["rw_trev"], 1)
                for m in range(4):
                    dve.wait_ge(sem["rw_gh"], 4 * l + m + 1)
                    for tt in range(TT):
                        for a in range(2):
                            r = slice(64 * a, 64 * a + 64)
                            to = GT[r, m, 8 * tt:8 * tt + 8, 64 * a:64 * a + 64].rearrange("p (q e) n -> p q e n", e=2)
                            dve.tensor_tensor(to, PS[r, 4:8, tt * P:(tt + 1) * P].rearrange("p q (e n) -> p q e n", e=2), to, ALU.add)
                        e = dve.tensor_copy(ST[:, 1 + 8 * tt:9 + 8 * tt, m, :].rearrange("p (q e) n -> p q e n", e=2),
                                            PS[:, 4:8, 256 + tt * P:256 + (tt + 1) * P].rearrange("p q (e n) -> p q e n", e=2))
                    e.then_inc(sem["rw_ghev"], 1)
                dve.wait_ge(sem["rw_ghev"], 4 * (l + 1))
                dve.memset(ST[:, 0, :, :].rearrange("p a b -> p (a b)"), 0.0).then_inc(sem["rw_state"], 1)
                for c in range(NCH - 1):
                    dve.wait_ge(sem["rw_step"], (NCH - 1) * l + c + 1)
                    s = ST[:, c + 1, :, :].rearrange("p a b -> p (a b)")
                    dve.tensor_tensor(s, PS[:, 4 + c % 2, 0:256], s, ALU.add).then_inc(sem["rw_state"], 1)
                dve.wait_ge(sem["rw_y"], l + 1)
                for a in range(2):
                    r = slice(64 * a, 64 * a + 64)
                    e = dve.tensor_tensor(flat(YR[r, :, :]), flat(YR[r, :, :]),
                                          PS[r, 6 * a:6 * a + 2, :].rearrange("p a b -> p (a b)"), ALU.add)
                e.then_inc(sem["rw_yall"], 1)
                dve.wait_ge(sem["rw_mean"], l + 1)
                link(dve.scalar_tensor_tensor(flat(YR), PS[:, 2:4, :].rearrange("p a b -> p (a b)"), -1.0 / HS, flat(YR),
                                              ALU.mult, ALU.add))
                dve.tensor_tensor(flat(S0), flat(YR), flat(YR), ALU.mult).then_inc(sem["rw_cent"], 1)
                dve.wait_ge(sem["rw_bonus"], l + 1)
                dve.tensor_tensor(flat(S1), PS[:, 4:6, :].rearrange("p a b -> p (a b)"), flat(V_), ALU.mult)
                dve.wait_ge(sem["rw_var"], l + 1)
                dve.tensor_scalar(flat(GNV), PS[:, 0:2, :].rearrange("p a b -> p (a b)"), 1.0 / HS, GN_EPS, ALU.mult, ALU.add)\
                   .then_inc(sem["rw_gnvar"], 1)
                dve.wait_ge(sem["rw_sd"], l + 1)
                inverse_root(flat(S0), flat(GNV), flat(GNT))
                link(dve.tensor_tensor(flat(YR), flat(YR), flat(S0), ALU.mult))
                link(dve.tensor_tensor(YR, YR, bc(V4("lnx_g"), T), ALU.mult))
                link(dve.tensor_tensor(YR, YR, bc(V4("lnx_b"), T), ALU.add))
                link(dve.tensor_tensor(flat(YR), flat(YR), flat(S1), ALU.add))
                dve.wait_ge(sem["rw_pl"], l + 1)
                dve.tensor_tensor(PL, PS[:, 6:8, :].rearrange("p a (b t) -> p (a b) t", b=2), bc(V4("pool_scale"), T), ALU.mult)
                dve.tensor_tensor(flat(YR), flat(YR), flat(GG), ALU.mult).then_inc(sem["rw_mix"], 1)
                residual(6 + 2 * l, lambda d: BASE["mix_out", l] + d)

            def top16(groups):
                for v, s, o, ix in groups:
                    e = dve.max(o[:, 0:8], v)
                link(e)
                for v, s, o, ix in groups:
                    dve.max_index(ix[:, 0:8], o[:, 0:8], v)
                    e = dve.match_replace(s, o[:, 0:8], v, -3.0e38)
                link(e)
                for v, s, o, ix in groups:
                    e = dve.max(o[:, 8:16], s)
                link(e)
                for v, s, o, ix in groups:
                    e = dve.max_index(ix[:, 8:16], o[:, 8:16], s)
                link(e)

            def peer(l):
                ready(BASE["peer_q", l] + 15)
                dve.wait_ge(sem["uv_h_hi"], l + 1)
                dve.tensor_tensor(flat(h_lo[:, :, :]), flat(h[:, :, :]), flat(h_hi[:, :, :]).bitcast(F32), ALU.subtract)\
                   .then_inc(sem["h_lo"], 1)
                dve.wait_ge(sem["pe_scev"], 8 * (l + 1))
                IU, SU = IDX.bitcast(U32), SEL.bitcast(U32)
                top16([(SC[:, t, n, :], SC2[:, t, n, :], VAL[:, t, n, :], IU[:, t, n, :]) for t in range(TT) for n in range(16)])
                link(dve.tensor_copy(IDXF.rearrange("p t n k -> p (t n k)"), IU.rearrange("p t n k -> p (t n k)")))
                vp = VAL.rearrange("p t (n h) k -> p t n h k", h=2)
                for t in range(TT):
                    e = dve.tensor_tensor(CAND[:, t, :, :].rearrange("p n (a b) -> p n a b", a=16),
                                          vp[:, t, :, 0, :].rearrange("p n (k o) -> p n k o", o=1).to_broadcast([P, PH, 16, 16]),
                                          vp[:, t, :, 1:2, :].to_broadcast([P, PH, 16, 16]), ALU.add)
                link(e)
                top16([(CAND[:, t, n, :], CAND2[:, t, n, :], TOP[:, t, n, :], SU[:, t, n, :]) for t in range(TT) for n in range(PH)])

                def f1(v):
                    return v.rearrange("p t n k -> p (t n k)")

                sel = SELI.bitcast(U32)
                link(dve.tensor_scalar(sel, f1(SU), 4, None, ALU.logical_shift_right))
                link(dve.tensor_copy(f1(HI), sel))
                link(dve.tensor_scalar(sel, f1(SU), 15, None, ALU.bitwise_and))
                link(dve.tensor_copy(f1(LOW), sel))
                fp = IDXF.rearrange("p t (n h) k -> p t n h k", h=2)
                for k, which in enumerate((HI, LOW)):
                    for t in range(TT):
                        e3 = EQ.rearrange("p (n a) -> p n a", a=16)
                        link(dve.tensor_tensor(e3, bc(which[:, t, :, :].rearrange("p n k -> p (n k)"), 16), rep(iota[:, 0:16], P),
                                               ALU.is_equal))
                        e4 = EQ.rearrange("p (n k a) -> p n k a", n=PH, a=16)
                        link(dve.tensor_tensor(e4, e4, fp[:, t, :, k:k + 1, :].to_broadcast([P, PH, 16, 16]), ALU.mult))
                        link(dve.tensor_reduce(IJT[:, k, t, :], e3, AX.X, ALU.add))
                tf = TOP.rearrange("p t n k -> p (t n) k")
                sm = SMX.rearrange("p (n k) -> p n k", k=16)
                dve.tensor_tensor(sm, tf, tf[:, :, 0:1].to_broadcast([P, 16, 16]), ALU.subtract).then_inc(sem["pe_top"], 1)
                dve.wait_ge(sem["pe_exp"], l + 1)
                tot = SELI[:, 0:16]
                link(dve.tensor_reduce(tot, sm, AX.X, ALU.add))
                link(dve.reciprocal(tot, tot))
                dve.tensor_tensor(IJT[:, 2, :, :].rearrange("p t (n k) -> p (t n) k", k=16), sm, bc(tot, 16), ALU.mult)\
                   .then_inc(sem["pe_sm"], 1)
                dve.wait_ge(sem["pe_ijg"], l + 1)
                with dve.Fori(0, T // 8) as i:
                    for k in range(2):
                        dve.wait_ge(sem["pe_w"], i * 2 + (64 * l + k - 1 + 2))
                        for j in range(4):
                            t = bass.ds(i * 8 + (4 * k + j), 1)
                            dve.tensor_scalar(OHI[:, k, j, :], iota, ijg[:, 0, t], ijg[:, 2, t], ALU.is_equal, ALU.mult)
                        dve.tensor_tensor(OHJ[:, k, :, :], rep(iota, 4), bc(ijg[:, 1, bass.ds(i * 8 + 4 * k, 4)], P), ALU.is_equal)\
                           .then_inc(sem["pe_oh"], 1)
                section = "uv", l

                def gate(j, i):
                    dve.wait_ge(sem["pe_gelu"], i * 4 + (NK * l + j + 1 + PRIME))
                    g, hi, lo = gat[:, j % 4, :], gat_hi[:, j % 2, :], gat_lo[:, j % 4, :]
                    dve.tensor_tensor(g, sil[:, j % 4, :], WALL[:, :, i * 4 + j], ALU.mult).then_inc(sem["pe_gated"], 1)
                    dve.wait_ge(sem["pe_gated"], i * 4 + (NK * l + j + 1 + PRIME))
                    dve.tensor_copy(hi, g).then_inc(sem["gate_hi"], 1)
                    dve.wait_ge(sem["gate_hi"], i * 4 + (SPLIT[section][1] + j + 1))
                    dve.tensor_tensor(lo, g, hi.bitcast(F32), ALU.subtract).then_inc(sem["gate_lo"], 1)

                def turn(j, i):
                    gate(j, i)
                    split_lo(section, 2 * j + 2, i)
                    split_lo(section, 2 * j + 3, i)

                split_lo(section, 0, 0)
                split_lo(section, 1, 0)
                with dve.Fori(0, NK // 4 - 1) as i:
                    for j in range(4):
                        turn(j, i)
                for j in range(NK - 4, NK - 1):
                    turn(j, 0)
                gate(NK - 1, 0)
                residual(7 + 2 * l, lambda d: BASE["uv", l] + 2 * NK - 1)

            dve.wait_ge(sem["inits"], 4)
            dve.wait_ge(sem["loads"], 48)
            first_products()
            for s in range(NSUB):
                group = (0,) if s == 0 else MOD_GROUPS.get(s - 1, ())
                if group:
                    mod_columns(group[0], 0)
                normed(s)
                for j in range(1, len(group)):
                    mod_columns(group[j], j)
                if s in (0, 2, 3, 5):
                    ffn((0, 2, 3, 5).index(s))
                elif s == 1:
                    ssd()
                elif s == 4:
                    mla()
                elif s % 2 == 0:
                    rwkv((s - 6) // 2)
                else:
                    peer((s - 7) // 2)
            normed(NSUB)

        @block.gpsimd
        def _(pool):
            chain = [0]

            def link(ins):
                chain[0] += 1
                ins.then_inc(sem["pool_chain"], 1)
                pool.wait_ge(sem["pool_chain"], chain[0])

            def mod_loads(f):
                if f == 0:
                    pool.wait_ge(sem["inits"], 4)
                else:
                    pool.wait_ge(sem["x_upd"], 8 * f)
                first, blocks = 24 * (MOD_GROUPS[f][0] - 1), 24 * len(MOD_GROUPS[f])
                for slot in range(MOD_RING):
                    pool.dma_start(MODRING[slot], mods[first + slot]).then_inc(mod_full[slot], 16)
                with pool.Fori(0, blocks // MOD_RING - 1) as i:
                    for slot in range(MOD_RING):
                        pool.wait_ge(sem["mod_acc"], i * MOD_RING + (first + slot + 1))
                        pool.dma_start(MODRING[slot], mods[i * MOD_RING + (first + slot + MOD_RING)]).then_inc(mod_full[slot], 16)

            pool.memset(zeros[:, :], 0.0).then_inc(sem["inits"], 1)
            pool.memset(AR[:, 101:106, :].rearrange("p a b -> p (a b)"), 0.0).then_inc(sem["inits"], 1)
            pool.dma_start(CMASK, const("causal")).then_inc(sem["aux_loads"], 16)
            pool.wait_ge(sem["aux_loads"], 16)
            pool.tensor_copy(CMB, CMASK).then_inc(sem["inits"], 1)
            pool.wait_ge(sem["loads"], 48)
            pool.tensor_copy(IDB[:, :], ident).then_inc(sem["inits"], 1)
            mod_loads(0)
            pool.wait_ge(sem["x_upd"], 16)
            pool.dma_start(WUQ, wuq_d).then_inc(sem["mla_w"], 16)
            pool.dma_start(WUKV, wukv_d).then_inc(sem["mla_w"], 16)
            pool.dma_start(RPM, const("rope")[0:QK, :]).then_inc(sem["mla_w"], 16)
            pool.dma_start(ANG[:, 0, :].bitcast(I32), pos_d[0:1, :].to_broadcast([QK, T])).then_inc(sem["mla_w"], 16)
            mod_loads(2)
            mod_loads(3)
            pool.wait_ge(sem["proj_evac"], EV["mla_in"] + 6 + PRIME)
            pool.tensor_copy(KH[64:96, :, :], rep(KPE[64:96, :], MH)).then_inc(sem["mla_kpe"], 1)
            mod_loads(5)
            for l in range(2):
                pool.wait_ge(sem["x_upd"], 8 * (6 + 2 * l))
                pool.dma_start(RC, consts_d[:, CONSTS["mask4"][0]:CONSTS["mask4"][0] + RCN]).then_inc(sem["rw_w"], 16)
                pool.dma_start(WUP, lora_d[l]).then_inc(sem["rw_w"], 16)
                pool.dma_start(GUP, gup_d[l]).then_inc(sem["rw_w"], 16)
                pool.dma_start(POOLW, pool_d[l]).then_inc(sem["rw_w"], 16)
                if l == 1:
                    pool.dma_start(VUP[0:32, :], vup_d).then_inc(sem["rw_w"], 16)
                pool.memset(ZPAD[:, :, 0:1], 0.0).then_inc(sem["rw_zpad"], 1)
                pool.wait_ge(sem["rw_w"], 64 + 80 * l)
                pool.wait_ge(sem["proj_evac"], EV["mix_in", l] + 18 + PRIME)
                for j in range(4):
                    cur = PL[:, j, :]
                    for k in range(j + 1):
                        w, nxt = 1 << k, ijg[:, k % 2, :]
                        pool.tensor_copy(nxt[:, 0:w], cur[:, 0:w])
                        link(pool.tensor_tensor(nxt[:, w:T], cur[:, w:T], cur[:, 0:T - w], ALU.add))
                        cur = nxt
                    link(pool.tensor_tensor(cur, cur, RECIP[:, j * T:(j + 1) * T], ALU.mult))
                    link(pool.tensor_tensor(PL[:, j, :], cur, PL[:, j, :], ALU.subtract))
                pool.sem_inc(sem["rw_pool"], 1)
                pool.wait_ge(sem["rw_zy"], l + 1)
                link(pool.memset(GT[0:64, :, :, 64:128].rearrange("p m c n -> p (m c) n"), 0.0))
                pool.memset(GT[64:128, :, :, 0:64].rearrange("p m c n -> p (m c) n"), 0.0).then_inc(sem["rw_zeroed"], 1)
                pool.wait_ge(sem["x_upd"], 8 * (7 + 2 * l))
                pool.dma_start(KEYS, keys_d[l]).then_inc(sem["pe_keys"], 16)


def _columns(v, n):
    return np.ascontiguousarray(v.reshape(n, P).T)


def _square(v):
    out = np.zeros((P, 1), np.float32)
    out[:v.size, 0] = v.reshape(-1)
    return out


def _blocks(w):
    k, n = w.shape
    m = -(-n // P)
    if m * P != n:
        w = np.concatenate([w, np.zeros((k, m * P - n), w.dtype)], axis=1)
    return w.reshape(k // 1024, 8, P, m, P).transpose(3, 0, 2, 1, 4).reshape(-1, P, 1024)


def _constants():
    c = np.zeros((P, NCONST), np.float32)
    i = np.arange(P)

    def put(name, v):
        s, n = CONSTS[name]
        c[:v.shape[0], s:s + n] = v

    put("ident", np.eye(P, dtype=np.float32))
    put("ones", np.ones((P, P), np.float32))
    put("iota", np.broadcast_to(i.astype(np.float32), (P, P)))
    put("half", (i[:, None] // HS == i[None, :] // HS).astype(np.float32))
    same = i[:, None] // CH == i[None, :] // CH
    strict = (same & (i[:, None] < i[None, :])).astype(np.float32)
    incl = (same & (i[:, None] <= i[None, :])).astype(np.float32)
    put("mask4", np.concatenate([strict, incl, strict, incl], axis=1))
    put("maskn", np.concatenate([strict.T, strict.T], axis=1))
    put("restart", np.broadcast_to((np.arange(T) % CH != 0).astype(np.float32), (P, T)))
    rope = np.zeros((QK, QK), np.float32)
    for j in range(ROPE // 2):
        rope[NOPE + ROPE // 2 + j, NOPE + j] = -1.0
        rope[NOPE + j, NOPE + ROPE // 2 + j] = 1.0
    put("rope", rope)
    put("causal", np.concatenate([np.where(i[:, None] <= i[None, :], 0, NEG), np.where(i[:, None] >= i[None, :], 0, NEG)],
                                 axis=1).astype(np.float32))
    pos = np.arange(1, T + 1, dtype=np.float32)
    put("recip", np.broadcast_to(np.concatenate([1.0 / np.minimum(pos, w) for w in (2, 4, 8, 16)]).astype(np.float32), (P, 4 * T)))
    return c


def kernel(**inputs):
    import concourse.bacc as bacc
    from concourse.bass_utils import run_bass_kernel_spmd as run

    a = {k: np.asarray(v) for k, v in inputs.items()}
    stream = np.empty((NBLOCKS, P, 1024), np.float32)

    mods = np.concatenate([a[n][i].reshape(DT, P, -1, D).transpose(2, 0, 1, 3).reshape(-1, P, D)
                           for n in ("w_mod", "ada_w_2") for i in range(2)])

    def put(name, blocks):
        stream[BASE[name]:BASE[name] + len(blocks)] = blocks

    for i in range(2):
        for s in range(2):
            b = BASE["ffn", 2 * i + s]
            stream[b:b + 2 * FT:2] = _blocks(a["ffn_w_gate"][i, s])
            stream[b + 1:b + 2 * FT:2] = _blocks(a["ffn_w_up"][i, s])
            stream[b + 2 * FT:b + 3 * FT] = a["ffn_w_down"][i, s].reshape(FT, P, 1024)
    put("mod0", mods[:24])
    put("ssd_in", _blocks(a["ssd_w_in"][0]))
    put("ssd_out", _blocks(a["ssd_w_out"][0]))
    put("mla_in", _blocks(a["mla_w_in"][0]))
    put("mla_out", _blocks(a["mla_w_out"][0]))
    for l in range(2):
        w = a["w_in_2"][l]
        put(("mix_in", l), _blocks(w if l == 0 else np.concatenate([w, a["vres_down_2"][0]], axis=1)))
        put(("mix_out", l), _blocks(a["w_out_2"][l]))
        put(("peer_q", l), _blocks(a["peer_q_2"][l]))
        b = BASE["uv", l]
        u = a["peer_u_2"][l].reshape(NK, NK, 8, P).transpose(1, 3, 2, 0).reshape(NK, P, 1024)
        v = a["peer_v_2"][l].reshape(NK, NK, D).transpose(1, 0, 2)
        stream[b] = u[0]
        stream[b + 1:b + 2 * NK - 1:2] = u[1:]
        stream[b + 2:b + 2 * NK - 1:2] = v[:-1]
        stream[b + 2 * NK - 1] = v[-1]

    freq = np.zeros(QK, np.float32)
    inv = (10000.0 ** (-np.arange(0, ROPE, 2, dtype=np.float32) / ROPE)).astype(np.float32)
    freq[NOPE:] = np.concatenate([inv, inv])
    parity = ((np.arange(P) // CH) % 2).astype(np.float32)
    parts = {
        "c": _columns(a["c"], 8), "c_2": _columns(a["c_2"], 8), "norm_g": _columns(a["norm_g"], 48),
        "b_mod": _columns(a["b_mod"], 144), "ada_b": _columns(a["ada_b_2"], 96), "ln1": _columns(a["ln1_g_2"], 16),
        "ln2": _columns(a["ln2_g_2"], 16), "lnf": _columns(a["lnf_g_2"], 8), "dt_bias": _square(a["ssd_dt_bias"]),
        "a_log": _square(a["ssd_a_log"]),
        "conv_w": a["ssd_conv_w"][0].reshape(CONV, XBCT, P).transpose(2, 1, 0).reshape(P, XBCT * CONV),
        "conv_b": _columns(a["ssd_conv_b"], XBCT), "ssd_d": _columns(np.repeat(a["ssd_d"][0], 64), ZT),
        "ssd_g": _columns(a["ssd_norm_g"], ZT), "q_norm": _columns(a["mla_q_norm_g"], 3),
        "kv_norm": _columns(a["mla_kv_norm_g"], 2), "q_head": _square(a["mla_q_head_g"]), "k_head": _square(a["mla_k_head_g"]),
        "mu": _columns(a["mu_shift_2"], 28), "w0": _columns(a["w0_2"], 8), "a0": _columns(a["a0_2"], 8),
        "k_k": _columns(a["k_k_2"], 8), "k_a": _columns(a["k_a_2"], 8), "r_k": _columns(a["r_k_2"], 8),
        "lnx_g": _columns(a["lnx_g_2"], 8), "lnx_b": _columns(a["lnx_b_2"], 8), "pool_scale": _columns(a["pool_scale_2"], 8),
        "vres_mu": _square(a["vres_mu_2"]), "vres_v0": _columns(a["vres_v0_2"], 4), "freq": _square(freq),
        "even": 1.0 - parity[:, None], "odd": parity[:, None],
    }
    cols = np.concatenate([parts[n] for n in COLS], axis=1).astype(np.float32)
    ukv = a["mla_w_ukv"][0].reshape(2, P, MH, 2, 64).transpose(1, 0, 3, 2, 4).reshape(P, 2, 2048)
    arrays = {
        "stream": stream, "mod_weights": mods[24:], "columns": cols, "constants": _constants(),
        "x_in": a["x"][0].reshape(T, DT, P).transpose(2, 1, 0),
        "positions": a["positions"],
        "w_uq": a["mla_w_uq"][0].reshape(3, P, MH * QK).transpose(1, 0, 2),
        "w_ukv": ukv,
        "keys": a["peer_keys_2"].reshape(2, 16, NK, P).transpose(0, 3, 1, 2),
        "pool_w": a["pool_w_2"].transpose(0, 2, 1, 3).reshape(2, P, 512),
        "lora_up": np.concatenate([a["w_up_2"], a["a_up_2"]], axis=1),
        "gate_up": a["g_up_2"], "vres_up": a["vres_up_2"][0],
    }
    arrays = {k: np.ascontiguousarray(v) for k, v in arrays.items()}
    nc = bacc.Bacc("TRN2", target_bir_lowering=False, num_devices=1)
    aps = [nc.dram_tensor(k, v.shape, mybir.dt.from_np(v.dtype), kind="ExternalInput").ap() for k, v in arrays.items()]
    out = nc.dram_tensor("out", (P, DT, T), F32, kind="ExternalOutput").ap()
    build(nc, *aps, out)
    r = run(nc, [arrays], core_ids=[0])
    return np.ascontiguousarray(r.results[0]["out"].transpose(2, 1, 0).reshape(1, T, D))
```
